# Optimizing a Trainium2 kernel written in Bass

```python
import jax, jax.numpy as jnp
from jax import lax
import numpy as np

D_MODEL = 1024
BATCH = 1
SEQ = 1024
DEPTH = 1

ML_HEADS = 4
ML_HEAD_DIM = 64
ML_WIDTH = ML_HEADS * ML_HEAD_DIM
ML_CHUNK = 64
LRU_WIDTH = 256
LRU_BLOCKS = 4
LRU_BLOCK_DIM = LRU_WIDTH // LRU_BLOCKS
CONV_WIDTH = 4
LRU_C = 8.0
MLA_HEADS = 8
MLA_NOPE = 64
MLA_ROPE = 32
MLA_V = 64
MLA_WIDTH = MLA_HEADS * MLA_V
Q_LORA = 256
KV_LORA = 128
ROPE_THETA = 10000.0
Q_BLOCK = 128
MIX_WIDTH = ML_WIDTH + LRU_WIDTH + MLA_WIDTH
N_GROUPS = 4
EXPERTS_PER_GROUP = 8
N_EXPERTS = N_GROUPS * EXPERTS_PER_GROUP
TOP_K = 2
D_EXPERT = 256
EPS = 1e-6

SPLIT_SIZES = (ML_WIDTH, ML_WIDTH, ML_WIDTH, ML_WIDTH, ML_HEADS, ML_HEADS,
               LRU_WIDTH, LRU_WIDTH,
               Q_LORA, KV_LORA, MLA_ROPE)
N_IN = int(sum(SPLIT_SIZES))
SPLIT_POINTS = [int(v) for v in np.cumsum(SPLIT_SIZES)[:-1]]

kernel_name = "hybrid_mlstm_rglru_mla_hmoe"

def rmsnorm(x, g):
    xf = x.astype(jnp.float32)
    y = xf * lax.rsqrt(jnp.mean(xf * xf, axis=-1, keepdims=True) + EPS)
    return (y * g.astype(jnp.float32)).astype(x.dtype)

def mlstm(q, k, v, i_pre, f_pre, o_pre, norm_g):
    B, S, _ = q.shape
    H, dh, L = ML_HEADS, ML_HEAD_DIM, ML_CHUNK
    nc = S // L
    f32 = jnp.float32

    def heads(t):
        return t.astype(f32).reshape(B, nc, L, H, dh).transpose(1, 0, 3, 2, 4)

    def gates(t):
        return t.astype(f32).reshape(B, nc, L, H).transpose(1, 0, 3, 2)

    qh, kh, vh = heads(q), heads(k) * (dh ** -0.5), heads(v)
    log_i = gates(i_pre)
    log_f = jax.nn.log_sigmoid(gates(f_pre))
    causal = jnp.tril(jnp.ones((L, L), dtype=bool))

    def step(carry, inp):
        C, n, m = carry
        qc, kc, vc, li, lf = inp
        b = jnp.cumsum(lf, axis=-1)
        D = b[..., :, None] - b[..., None, :] + li[..., None, :]
        D = jnp.where(causal, D, -jnp.inf)
        inter = b + m[..., None]
        m_row = jnp.maximum(jnp.max(D, axis=-1), inter)
        w_intra = jnp.exp(D - m_row[..., None])
        w_inter = jnp.exp(inter - m_row)
        s = jnp.einsum('bhjd,bhsd->bhjs', qc, kc) * w_intra
        num = jnp.einsum('bhjs,bhsd->bhjd', s, vc) + w_inter[..., None] * jnp.einsum('bhvk,bhjk->bhjv', C, qc)
        den = jnp.sum(s, axis=-1) + w_inter * jnp.einsum('bhk,bhjk->bhj', n, qc)
        h = num / jnp.maximum(jnp.abs(den), jnp.exp(-m_row))[..., None]
        bL = b[..., -1]
        g = bL[..., None] - b + li
        m_new = jnp.maximum(bL + m, jnp.max(g, axis=-1))
        ws = jnp.exp(g - m_new[..., None])
        decay = jnp.exp(bL + m - m_new)
        C_new = decay[..., None, None] * C + jnp.einsum('bhs,bhsv,bhsk->bhvk', ws, vc, kc)
        n_new = decay[..., None] * n + jnp.einsum('bhs,bhsk->bhk', ws, kc)
        return (C_new, n_new, m_new), h

    init = (jnp.zeros((B, H, dh, dh), f32), jnp.zeros((B, H, dh), f32), jnp.zeros((B, H), f32))
    _, h = lax.scan(step, init, (qh, kh, vh, log_i, log_f))
    h = h.transpose(1, 0, 3, 2, 4).reshape(B, S, H, dh)
    o = jax.nn.sigmoid(o_pre.astype(f32)).reshape(B, S, H, dh)
    y = rmsnorm(o * h, norm_g.reshape(H, dh))
    return y.reshape(B, S, ML_WIDTH).astype(q.dtype)

def rglru(xb, gate, conv_w, conv_b, w_r, b_r, w_i, b_i, lam):
    B, S, W = xb.shape
    f32 = jnp.float32
    xc = lax.conv_general_dilated(xb, conv_w[:, None, :], window_strides=(1,),
                                  padding=[(CONV_WIDTH - 1, 0)],
                                  dimension_numbers=('NWC', 'WIO', 'NWC'),
                                  feature_group_count=W) + conv_b
    xc = xc.astype(f32)
    xblk = xc.reshape(B, S, LRU_BLOCKS, LRU_BLOCK_DIM)
    r = jax.nn.sigmoid(jnp.einsum('bsnd,nde->bsne', xblk, w_r.astype(f32)).reshape(B, S, W) + b_r.astype(f32))
    i = jax.nn.sigmoid(jnp.einsum('bsnd,nde->bsne', xblk, w_i.astype(f32)).reshape(B, S, W) + b_i.astype(f32))
    log_a = -LRU_C * r * jax.nn.softplus(-lam.astype(f32))
    a = jnp.exp(log_a)
    u = jnp.sqrt(-jnp.expm1(2.0 * log_a)) * (i * xc)

    def combine(lhs, rhs):
        a1, b1 = lhs
        a2, b2 = rhs
        return a1 * a2, a2 * b1 + b2

    _, h = lax.associative_scan(combine, (a, u), axis=1)
    return (h * jax.nn.gelu(gate.astype(f32))).astype(xb.dtype)

def rope_tables(S):
    inv = 1.0 / (ROPE_THETA ** (jnp.arange(0, MLA_ROPE, 2, dtype=jnp.float32) / MLA_ROPE))
    ang = jnp.arange(S, dtype=jnp.float32)[:, None] * inv[None, :]
    return jnp.cos(ang), jnp.sin(ang)

def apply_rope(t, cos, sin):
    t1, t2 = jnp.split(t.astype(jnp.float32), 2, axis=-1)
    return jnp.concatenate([t1 * cos - t2 * sin, t1 * sin + t2 * cos], axis=-1).astype(t.dtype)

def mla(cq, ckv, kr, q_g, w_uq, kv_g, w_ukv, cos, sin):
    B, S, _ = cq.shape
    H = MLA_HEADS
    q = (rmsnorm(cq, q_g) @ w_uq).reshape(B, S, H, MLA_NOPE + MLA_ROPE)
    q_nope = q[..., :MLA_NOPE]
    q_rope = apply_rope(q[..., MLA_NOPE:], cos[:, None, :], sin[:, None, :])
    kv = (rmsnorm(ckv, kv_g) @ w_ukv).reshape(B, S, H, MLA_NOPE + MLA_V)
    k_nope, v = kv[..., :MLA_NOPE], kv[..., MLA_NOPE:]
    k_rope = apply_rope(kr, cos, sin)
    scale = (MLA_NOPE + MLA_ROPE) ** -0.5
    nb = S // Q_BLOCK
    qn_b = q_nope.reshape(B, nb, Q_BLOCK, H, MLA_NOPE).transpose(1, 0, 2, 3, 4)
    qr_b = q_rope.reshape(B, nb, Q_BLOCK, H, MLA_ROPE).transpose(1, 0, 2, 3, 4)
    key_pos = jnp.arange(S)

    def block(args):
        qn, qr, idx = args
        s = (jnp.einsum('bqhd,bkhd->bhqk', qn, k_nope) +
             jnp.einsum('bqhr,bkr->bhqk', qr, k_rope)).astype(jnp.float32) * scale
        q_pos = idx * Q_BLOCK + jnp.arange(Q_BLOCK)
        s = jnp.where(key_pos[None, :] <= q_pos[:, None], s, -jnp.inf)
        p = jax.nn.softmax(s, axis=-1).astype(v.dtype)
        return jnp.einsum('bhqk,bkhd->bqhd', p, v)

    o = lax.map(block, (qn_b, qr_b, jnp.arange(nb)))
    return o.transpose(1, 0, 2, 3, 4).reshape(B, S, MLA_WIDTH)

def hier_moe(x, w_grp, b_grp, w_exp, b_exp, w_gate, w_up, w_down):
    B, S, D = x.shape
    T = B * S
    t = x.reshape(T, D)
    grp_p = jax.nn.softmax((t @ w_grp + b_grp).astype(jnp.float32), axis=-1)
    g_val, g_idx = lax.top_k(grp_p, 1)
    exp_logits = (t @ w_exp + b_exp).astype(jnp.float32).reshape(T, N_GROUPS, EXPERTS_PER_GROUP)
    sel = jnp.take_along_axis(exp_logits, g_idx[:, :, None], axis=1)[:, 0]
    e_val, e_idx = lax.top_k(jax.nn.softmax(sel, axis=-1), TOP_K)
    e_w = e_val / jnp.sum(e_val, axis=-1, keepdims=True) * g_val
    expert_id = g_idx * EXPERTS_PER_GROUP + e_idx
    combine = jnp.sum(jax.nn.one_hot(expert_id, N_EXPERTS, dtype=jnp.float32) * e_w[..., None], axis=1)

    def expert_step(acc, ew):
        wg, wu, wd, c = ew
        h = jax.nn.silu(t @ wg) * (t @ wu)
        return acc + c[:, None].astype(t.dtype) * (h @ wd), None

    y, _ = lax.scan(expert_step, jnp.zeros_like(t), (w_gate, w_up, w_down, combine.T))
    return y.reshape(B, S, D)

def setup_inputs(seed: int = 0) -> dict:
    key = jax.random.key(seed)
    ks = iter(jax.random.split(key, 40))
    f32 = jnp.float32
    L = DEPTH

    def nrm(shape, scale):
        return scale * jax.random.normal(next(ks), shape, f32)

    def gain(shape):
        return 1.0 + 0.02 * jax.random.normal(next(ks), shape, f32)

    x = jax.random.normal(next(ks), (BATCH, SEQ, D_MODEL), f32)
    norm1_g = gain((L, D_MODEL))
    w_in = nrm((L, D_MODEL, N_IN), D_MODEL ** -0.5)
    ml_i_bias = nrm((L, ML_HEADS), 0.1)
    ml_f_bias = jnp.linspace(3.0, 6.0, ML_HEADS, dtype=f32)[None, :] + nrm((L, ML_HEADS), 0.1)
    ml_norm_g = gain((L, ML_WIDTH))
    conv_w = nrm((L, CONV_WIDTH, LRU_WIDTH), CONV_WIDTH ** -0.5)
    conv_b = nrm((L, LRU_WIDTH), 0.02)
    lru_w_r = nrm((L, LRU_BLOCKS, LRU_BLOCK_DIM, LRU_BLOCK_DIM), LRU_BLOCK_DIM ** -0.5)
    lru_b_r = nrm((L, LRU_WIDTH), 0.02)
    lru_w_i = nrm((L, LRU_BLOCKS, LRU_BLOCK_DIM, LRU_BLOCK_DIM), LRU_BLOCK_DIM ** -0.5)
    lru_b_i = nrm((L, LRU_WIDTH), 0.02)
    a_c = jax.random.uniform(next(ks), (L, LRU_WIDTH), f32, 0.9, 0.999)
    a_base = a_c ** (1.0 / LRU_C)
    lru_lambda = jnp.log(a_base) - jnp.log1p(-a_base)
    lru_norm_g = gain((L, LRU_WIDTH))
    q_norm_g = gain((L, Q_LORA))
    w_uq = nrm((L, Q_LORA, MLA_HEADS * (MLA_NOPE + MLA_ROPE)), Q_LORA ** -0.5)
    kv_norm_g = gain((L, KV_LORA))
    w_ukv = nrm((L, KV_LORA, MLA_HEADS * (MLA_NOPE + MLA_V)), KV_LORA ** -0.5)
    mla_norm_g = gain((L, MLA_WIDTH))
    w_out = nrm((L, MIX_WIDTH, D_MODEL), MIX_WIDTH ** -0.5)
    norm2_g = gain((L, D_MODEL))
    w_group = nrm((L, D_MODEL, N_GROUPS), D_MODEL ** -0.5)
    b_group = nrm((L, N_GROUPS), 0.01)
    w_expert = nrm((L, D_MODEL, N_EXPERTS), D_MODEL ** -0.5)
    b_expert = nrm((L, N_EXPERTS), 0.01)
    w_gate = nrm((L, N_EXPERTS, D_MODEL, D_EXPERT), D_MODEL ** -0.5)
    w_up = nrm((L, N_EXPERTS, D_MODEL, D_EXPERT), D_MODEL ** -0.5)
    w_down = nrm((L, N_EXPERTS, D_EXPERT, D_MODEL), D_EXPERT ** -0.5)
    final_norm_g = gain((D_MODEL,))
    return {"x": x, "norm1_g": norm1_g, "w_in": w_in, "ml_i_bias": ml_i_bias, "ml_f_bias": ml_f_bias,
            "ml_norm_g": ml_norm_g, "conv_w": conv_w, "conv_b": conv_b, "lru_w_r": lru_w_r,
            "lru_b_r": lru_b_r, "lru_w_i": lru_w_i, "lru_b_i": lru_b_i, "lru_lambda": lru_lambda,
            "lru_norm_g": lru_norm_g, "q_norm_g": q_norm_g, "w_uq": w_uq, "kv_norm_g": kv_norm_g,
            "w_ukv": w_ukv, "mla_norm_g": mla_norm_g, "w_out": w_out, "norm2_g": norm2_g,
            "w_group": w_group, "b_group": b_group, "w_expert": w_expert, "b_expert": b_expert,
            "w_gate": w_gate, "w_up": w_up, "w_down": w_down, "final_norm_g": final_norm_g}

def reference(x, norm1_g, w_in, ml_i_bias, ml_f_bias, ml_norm_g, conv_w, conv_b, lru_w_r, lru_b_r,
              lru_w_i, lru_b_i, lru_lambda, lru_norm_g, q_norm_g, w_uq, kv_norm_g, w_ukv, mla_norm_g,
              w_out, norm2_g, w_group, b_group, w_expert, b_expert, w_gate, w_up, w_down, final_norm_g):
    S = x.shape[1]
    cos, sin = rope_tables(S)
    for l in range(DEPTH):
        hn = rmsnorm(x, norm1_g[l])
        proj = hn @ w_in[l]
        mq, mk, mv, mo, mi, mf, rx, rg, cq, ckv, kr = jnp.split(proj, SPLIT_POINTS, axis=-1)
        y_m = mlstm(mq, mk, mv, mi + ml_i_bias[l], mf + ml_f_bias[l], mo, ml_norm_g[l])
        y_r = rmsnorm(rglru(rx, rg, conv_w[l], conv_b[l], lru_w_r[l], lru_b_r[l],
                            lru_w_i[l], lru_b_i[l], lru_lambda[l]), lru_norm_g[l])
        y_a = rmsnorm(mla(cq, ckv, kr, q_norm_g[l], w_uq[l], kv_norm_g[l], w_ukv[l], cos, sin),
                      mla_norm_g[l])
        x = x + jnp.concatenate([y_m, y_r, y_a], axis=-1) @ w_out[l]
        x = x + hier_moe(rmsnorm(x, norm2_g[l]), w_group[l], b_group[l], w_expert[l], b_expert[l],
                         w_gate[l], w_up[l], w_down[l])
    return rmsnorm(x, final_norm_g)


_drawn_inputs = setup_inputs


def setup_inputs(seed=0):
    import zlib

    import numpy as np

    out = dict(_drawn_inputs(seed))
    spreads = {}
    factors = {'ml_i_bias': 172.178,
     'ml_norm_g': 18.196,
     'lru_b_r': 8.0,
     'lru_b_i': 7.616,
     'lru_norm_g': 17.741,
     'q_norm_g': 3.081,
     'mla_norm_g': 13.793,
     'b_group': 23.01,
     'b_expert': 23.862,
     'final_norm_g': 20.425,
     'norm2_g': 6.601}
    for name, (base, spread) in spreads.items():
        noise = np.random.default_rng([zlib.crc32(name.encode()), seed]).standard_normal(out[name].shape)
        drawn = base * np.exp(spread * noise) if base else spread * noise
        out[name] = __import__('jax').numpy.asarray(drawn.astype(out[name].dtype))
    for name, factor in factors.items():
        out[name] = (out[name] * factor).astype(out[name].dtype)
    return out
```

```python
from contextlib import ExitStack

import numpy as np
import concourse.bass as bass
from concourse import mybir

F32 = mybir.dt.float32
BF16 = mybir.dt.bfloat16
I32 = mybir.dt.int32
ALU = mybir.AluOpType
ACT = mybir.ActivationFunctionType
AX = mybir.AxisListType

P = 128
D = 1024
S = 1024
NT = S // P
KD = D // P
MLH, MLD = 4, 64
MLW = MLH * MLD
VA = MLD + 1
LRU = 256
CONV = 4
H, NOPE, ROPE, VD = 8, 64, 32, 64
QK = NOPE + ROPE
QL, KVL = 256, 128
NG, EPG = 4, 8
NE = NG * EPG
DE = 256
EPS = 1e-6
BIG = 1.0e30
SCALE = float(QK) ** -0.5
LRU_C = 8.0

C_MQ, C_MK, C_MV, C_MO, C_MI = 0, 256, 512, 768, 1024
C_RX, C_RG, C_CQ = 1032, 1288, 1544
N_IN = 1960
N_LAT = QL + KVL + ROPE

CAP = P
NMAIN = NE
NOVER = 2 * S // P - 1
NBLK = NMAIN + NOVER
NW = 4

GELU_S = 1.5957691216057308
GELU_A = 0.044715


def build(nc, t):
    ctx = ExitStack()
    with ctx:
        def sb(name, cols, dt=F32, parts=P):
            return ctx.enter_context(nc.sbuf_tensor(name, [parts, cols], dt))

        def sem(name):
            return ctx.enter_context(nc.semaphore(name))

        mem = sb("mem", 45696)

        def at(a, n, parts=P, p0=0):
            return mem[p0:p0 + parts, a:a + n]

        W_IN = at(0, KD * N_IN).rearrange("p (k n) -> p k n", k=KD)
        HNT = at(15680, 8192).rearrange("p (k n) -> p k n", k=KD)
        R2 = 24576
        KTOK = at(R2, 2048).rearrange("p (i n) -> p i n", i=NT)
        VAUG = at(R2 + 2048, 2080).rearrange("p (i h n) -> p i h n", i=NT, h=MLH)
        OTOK = at(R2 + 4128, 2048).rearrange("p (i n) -> p i n", i=NT)
        MQT = at(R2 + 6176, 2048).rearrange("p (m n) -> p m n", m=2)
        R3 = R2 + 8224
        CQT = at(R3, 2048).rearrange("p (m n) -> p m n", m=2)
        CKVT = at(R3 + 2048, 1024)
        KPT = at(R3 + 3072, 1024)
        R4 = R3 + 4096
        RXP = at(R4, 2 * (S + 3)).rearrange("p (m n) -> p m n", m=2)
        RG = at(R4 + 2054, 2048).rearrange("p (m n) -> p m n", m=2)
        R5 = R4 + 4102
        XB = [at(R5 + 1024 * j, 1024) for j in range(3)]
        CQR = [at(R5 + 3072 + N_LAT * j, N_LAT) for j in range(2)]
        KRP = [at(R5 + 3072 + 2 * N_LAT + QK * j, QK) for j in range(2)]
        ZERO = at(R5 + 4186, 512)
        ROW_F, ROW_I, ROW_LF, ROW_B, ROW_M, ROW_T, ROW_RS = (at(1024 * j, 1024, MLH) for j in range(7))
        LT = [[at(7168 + 5120 * f + 1024 * j, 1024) for j in range(5)] for f in range(2)]
        ROWS4 = at(17408, 1024)
        ROW_A = at(18432, 1024, MLH)
        ROW_T2 = at(19456, 1024, MLH)
        KTM = at(20480, 2048).rearrange("p (m n) -> p m n", m=2)
        DSB, WSB, PWB = (at(512 * j, MLH * P) for j in range(3))
        KSB, SQB = at(1536, MLW), at(1792, MLW)
        INT, NUM = at(2048, MLH * VA), at(2308, MLH * VA)
        KT = at(0, 8192).rearrange("p (h n) -> p h n", h=H)
        QT = at(8192, 8192).rearrange("p (h n) -> p h n", h=H)
        V = at(16384, 4096).rearrange("p (i h n) -> p i h n", i=NT, h=H)
        YA = at(20480, 4096).rearrange("p (i n) -> p i n", i=NT)
        W_UQ = at(R5, 1536).rearrange("p (k n) -> p k n", k=2)
        W_UKV = at(R5 + 1536, 1024).rearrange("p (h n) -> p h n", h=H)
        YM = at(R5 + 2560, 2048).rearrange("p (m n) -> p m n", m=2)
        QTOK = [at(R4 + 2054 + 768 * j, 768).rearrange("p (h n) -> p h n", h=H) for j in range(2)]
        PB = [at(R3 + 1024 * j, 1024) for j in range(2)]
        PTB = [at(R3 + 2048 + 512 * j, 512) for j in range(4)]
        W_OUT = at(R2, 8192).rearrange("p (k n) -> p k n", k=KD)
        X2 = at(8192, 8192).rearrange("p (i n) -> p i n", i=NT)
        XR = [at(1024 * j, 1024) for j in range(2)]
        X2N = [at(2048 + 1024 * j, 1024) for j in range(2)]
        X2NT = [at(4096 + 1024 * j, 1024).rearrange("p (k n) -> p k n", k=KD) for j in range(2)]
        YAT = [at(6144 + 512 * j, 512) for j in range(2)]
        G2B = at(R3, 1024)
        WOFF = (0, 16384, R2, R3)
        WGU = [at(o, 4096).rearrange("p (g k n) -> p g k n", g=2, k=KD) for o in WOFF]
        WDN = [at(o + 4096, 2048).rearrange("p (k n) -> p k n", k=2) for o in WOFF]
        E5 = R3 + 6144
        XG = [at(E5 + 1024 * j, 1024) for j in range(2)]
        XGT = [at(E5 + 2048 + 1024 * j, 1024).rearrange("p (k n) -> p k n", k=KD) for j in range(2)]
        SG = at(6144, 256)
        HT = [at(6400 + 256 * j, 256).rearrange("p (k n) -> p k n", k=2) for j in range(2)]
        YB = [at(6912 + 512 * j, 512) for j in range(2)]
        RA = at(E5 + 4096, 6 * NT * NE)
        YG = [[at((0, 16384)[j] + 1024 * q, 1024) for q in range(2)] for j in range(2)]
        OUT = [at(R2 + 1024 * j, 1024) for j in range(2)]
        GFB = at(R3, 1024)

        IDENT = sb("ident", P)
        ONES = sb("ones", P)
        CMASK = sb("cmask", P)
        TMASK = sb("tmask", P)
        TRI = sb("tri", P)
        SEL = sb("sel", MLH * P, parts=MLH)
        GB = sb("gb", D)
        COS = sb("cos", NT * 16)
        SIN = sb("sin", NT * 16)
        GQ = sb("gq", QL + KVL)
        GML = sb("gml", MLW)
        GMLA = sb("gmla", H * VD)
        GLRU = sb("glru", 2)
        CW = sb("cw", 2 * CONV)
        CB = sb("cb", 2)
        BR = sb("br", 2)
        BI = sb("bi", 2)
        LAM = sb("lam", 2)
        BGI = sb("bgi", 1, parts=MLH)
        BGF = sb("bgf", 1, parts=MLH)
        BD = sb("bd", 4 * P)
        WR = sb("wr", KD * 36)
        BRT = sb("brt", 36)
        EPSC = sb("epsc", 1)
        ONEC = sb("onec", 1)
        JUNK = sb("junk", D, BF16)
        ST1 = sb("st1", 2 * NT)
        ST2 = sb("st2", 4 * NT)
        GATES = sb("gates", NT * 8)
        RTMP = sb("rtmp", 4 * H * 16)
        SPT = sb("spt", 16)
        COL = sb("col", NT * 16)
        DEC = sb("dec", 8, parts=MLH)
        MPV = sb("mpv", 8, parts=MLH)
        DECB = sb("decb", MLH * NT)
        CST = sb("cst", 2 * VA)
        DEN = sb("den", 16)
        NMX = sb("nmx", 64)
        RSM = sb("rsm", 64)
        RIN = sb("rin", 64)
        LG = sb("lg", NT * 36)
        RB = sb("rb", 24 * NT)
        CNT = sb("cnt", 8 * NE)
        IOT = sb("iot", 4 * NE)
        SLOTF = sb("slotf", 2 * NT)
        SLOT = sb("slot", 2 * NT, I32)
        TOK = sb("tok", NT)
        WTS = sb("wts", 2 * NT)
        IDR = sb("idr", P, parts=NBLK)
        IDX = sb("idx", NBLK, I32)
        IDXC = [sb(f"idxc{j}", 1, I32) for j in range(2)]
        OVE = sb("ove", 32, I32, parts=1)

        ps = [ctx.enter_context(nc.psum_tensor(f"ps{b}", [P, 512], F32)) for b in range(8)]

        x2n_d = nc.dram_tensor("x2n_rows", [S, D], F32, kind="Internal").ap()
        ids_d = nc.dram_tensor("slot_ids", [NBLK * CAP, 1], F32, kind="Internal").ap()
        y_d = nc.dram_tensor("expert_rows", [NBLK * CAP, D], F32, kind="Internal").ap()

        x_d = t["x"].rearrange("b (i p) d -> (b i) p d", p=P)
        out_d = t["out"].rearrange("b (i p) d -> (b i) p d", p=P)

        act_chain, dve_chain, pool_chain = sem("act_chain"), sem("dve_chain"), sem("pool_chain")
        const_in, masks_set = sem("const_in"), sem("masks_set")
        x_in = [sem(f"x_in{j}") for j in range(3)]
        win_in = [sem(f"win_in{k}") for k in range(KD)]
        x_sq, x_rstd, hn_ready = sem("x_sq"), sem("x_rstd"), sem("hn_ready")
        hnt_ps, hnt_act, hnt_dve = sem("hnt_ps"), sem("hnt_act"), sem("hnt_dve")
        proj_ps, proj_act = sem("proj_ps"), sem("proj_act")
        lat_rstd, lat_ready, krp_ready = sem("lat_rstd"), sem("lat_ready"), sem("krp_ready")
        latt_ps, latt_sb = sem("latt_ps"), sem("latt_sb")
        gate_ps, gate_rows, lf_t, rows_pre, rows_done = (sem(n) for n in
                                                         ("gate_ps", "gate_rows", "lf_t", "rows_pre", "rows_done"))
        rs_set = sem("rs_set")
        cols_ps, cols_sb = sem("cols_ps"), sem("cols_sb")
        ktm_ps, ktm_sb = sem("ktm_ps"), sem("ktm_sb")
        lam_s, lam_done = sem("lam_s"), sem("lam_done")
        conv_done, lgate_ps, lgate_sb = sem("conv_done"), sem("lgate_ps"), sem("lgate_sb")
        gelu_arg, gelu_sig, gelu_done = sem("gelu_arg"), sem("gelu_sig"), sem("gelu_done")
        lru_a, lru_ratio, lru_root = sem("lru_a"), sem("lru_ratio"), sem("lru_root")
        yr_sq, yr_ps, yr_rstd, yr_done = sem("yr_sq"), sem("yr_ps"), sem("yr_rstd"), sem("yr_done")
        db_ps, d_ready, w_ready = sem("db_ps"), sem("d_ready"), sem("w_ready")
        st_ps, pw_ready, ks_ready = sem("st_ps"), sem("pw_ready"), sem("ks_ready")
        inter_ps, inter_sb, upd_ps, state_ready = sem("inter_ps"), sem("inter_sb"), sem("upd_ps"), sem("state_ready")
        intra_ps, num_ready, mh_ss, mh_rstd, ymt_ready = (sem(n) for n in ("intra_ps", "num_ready", "mh_ss", "mh_rstd", "ymt_ready"))
        ym_ps, ym_sb = sem("ym_ps"), sem("ym_sb")
        wu_in, kv_ps, kv_sb, kr_sb = sem("wu_in"), sem("kv_ps"), sem("kv_sb"), sem("kr_sb")
        q_ps, q_sb, q_rope, qt_ps, qt_act, qt_dve = (sem(n) for n in ("q_ps", "q_sb", "q_rope", "qt_ps", "qt_act", "qt_dve"))
        s_ps, s_max, p_ready = sem("s_ps"), sem("s_max"), sem("p_ready")
        pt_ps, pt_act, pt_dve, pv_ps, pv_sb = sem("pt_ps"), sem("pt_act"), sem("pt_dve"), sem("pv_ps"), sem("pv_sb")
        wout_in, g2_in = sem("wout_in"), sem("g2_in")
        xr_in = [sem(f"xr_in{j}") for j in range(2)]
        ya_sq, ya_rstd, ya_ready, yat_ps, yat_sb = (sem(n) for n in ("ya_sq", "ya_rstd", "ya_ready", "yat_ps", "yat_sb"))
        o_ps, x2_ready, x2_rstd, x2n_ready = sem("o_ps"), sem("x2_ready"), sem("x2_rstd"), sem("x2n_ready")
        x2n_out = [sem(f"x2n_out{j}") for j in range(2)]
        x2nt_ps, x2nt_act, x2nt_dve, r_ps, r_sb = (sem(n) for n in ("x2nt_ps", "x2nt_act", "x2nt_dve", "r_ps", "r_sb"))
        rt_a, rt_b, mask_ready, pos_ps, slot_ready = (sem(n) for n in ("rt_a", "rt_b", "mask_ready", "pos_ps", "slot_ready"))
        iota_set, ids_init, ids_out, ids_in, ids_ps, idx_ready = (sem(n) for n in
                                                                  ("iota_set", "ids_init", "ids_out", "ids_in", "ids_ps", "idx_ready"))
        w_in_ = [sem(f"wexp_in{j}") for j in range(NW)]
        pool_waits, zero_set, zero_out = sem("pool_waits"), sem("zero_set"), sem("zero_out")
        list_ready = sem("list_ready")
        xg_set = sem("xg_set")
        xg_in = [sem(f"xg_in{j}") for j in range(2)]
        xgt_ps, xgt_act, xgt_dve = sem("xgt_ps"), sem("xgt_act"), sem("xgt_dve")
        gu_ps, sg_ready, h_ready = sem("gu_ps"), sem("sg_ready"), sem("h_ready")
        y_ps, y_act, y_dve = sem("y_ps"), sem("y_act"), sem("y_dve")
        y_out = [sem(f"y_out{j}") for j in range(2)]
        yg_in = [sem(f"yg_in{j}") for j in range(2)]
        gf_in = sem("gf_in")
        f_sum, f_rstd, f_ready = sem("f_sum"), sem("f_rstd"), sem("f_ready")
        out_done = [sem(f"out_done{j}") for j in range(2)]

        PROJ = []
        for s in range(2):
            for i in range(4 * s, 4 * s + 4):
                PROJ += [("T", i, b) for b in range(3)]
            PROJ += [("F", s, m) for m in range(6)]
        NPROJ = len(PROJ)
        T_COLS = ((C_MK, 512), (C_MO, MLW + 8), (C_CQ, N_LAT))
        F_COLS = (C_MQ, C_MQ + P, C_RX, C_RX + P, C_RG, C_RG + P)

        def job(kind, a, b):
            return PROJ.index((kind, a, b))

        NC_ = 28

        def chained(eng, chain):
            count = [0]

            def link(ins):
                count[0] += 1
                ins.then_inc(chain, 1)
                eng.wait_ge(chain, count[0])
            return link

        ATT = [(i, h) for i in range(NT) for h in range(H)]
        GROUPS = [(n, g) for n, (i, h) in enumerate(ATT) for g in range((i + 4) // 4)]
        G0 = [sum(1 for (m, _) in GROUPS if m < n) for n in range(len(ATT) + 1)]

        block = ctx.enter_context(nc.Block())

        @block.sync
        def _(sp):
            def load_x(i):
                if i >= 3:
                    sp.wait_ge(hnt_ps, 2 * (i - 2))
                sp.dma_start(XB[i % 3], x_d[i]).then_inc(x_in[i % 3], 16)

            load_x(0)
            sp.dma_start(GB[:, :], t["norm1_g"].rearrange("l d -> (l d)").partition_broadcast(P)).then_inc(const_in, 16)
            load_x(1)
            load_x(2)
            for k in range(KD):
                sp.dma_start(W_IN[:, k, :], t["w_in"][0, k * P:(k + 1) * P, :]).then_inc(win_in[k], 16)
            for i in range(3, NT):
                load_x(i)
            sp.wait_ge(hnt_ps, 2 * NT)
            sp.dma_start(W_UQ, t["w_uq"][0].rearrange("(k p) n -> p k n", p=P)).then_inc(wu_in, 16)
            sp.dma_start(W_UKV, t["w_ukv"][0].rearrange("p (h n) -> p h n", h=H)).then_inc(wu_in, 16)
            sp.wait_ge(ym_sb, NT)
            sp.wait_ge(upd_ps, NT)
            sp.dma_start(W_OUT, t["w_out"][0].rearrange("(k p) n -> p k n", p=P)).then_inc(wout_in, 16)
            sp.wait_ge(pv_ps, len(ATT))
            sp.dma_start(G2B, t["norm2_g"].rearrange("l d -> (l d)").partition_broadcast(P)).then_inc(g2_in, 16)

            def load_xr(i):
                if i >= 2:
                    sp.wait_ge(x2_ready, i - 1)
                sp.dma_start(XR[i % 2], x_d[i]).then_inc(xr_in[i % 2], 16)

            load_xr(0)
            load_xr(1)
            for i in range(NT):
                sp.wait_ge(x2n_ready, i + 1)
                sp.dma_start(x2n_d[i * P:(i + 1) * P, :], X2N[i % 2]).then_inc(x2n_out[i % 2], 16)
                if i + 2 < NT:
                    load_xr(i + 2)

            def load_expert(j, e):
                sp.dma_start(WGU[j][:, 0], t["w_gate"][0, e].rearrange("(k p) n -> p k n", p=P)).then_inc(w_in_[j], 16)
                sp.dma_start(WGU[j][:, 1], t["w_up"][0, e].rearrange("(k p) n -> p k n", p=P)).then_inc(w_in_[j], 16)
                sp.dma_start(WDN[j], t["w_down"][0, e].rearrange("(k p) n -> p k n", p=P)).then_inc(w_in_[j], 16)

            sp.wait_ge(r_ps, NT)
            sp.wait_ge(x2n_out[0], 16 * (NT // 2))
            sp.wait_ge(x2n_out[1], 16 * (NT // 2))
            sp.wait_ge(x2nt_dve, NT)
            for j in range(NW):
                load_expert(j, j)

            def store(row, done):
                rows = y_d.rearrange("(b p) d -> b p d", p=CAP)[row]
                sp.wait_ge(y_act, done)
                sp.dma_start(rows[:, 0:512], YB[0]).then_inc(y_out[0], 16)
                sp.wait_ge(y_dve, done)
                sp.dma_start(rows[:, 512:1024], YB[1]).then_inc(y_out[1], 16)

            sp.sem_inc(y_out[0], 16)
            sp.sem_inc(y_out[1], 16)
            with sp.Fori(0, NMAIN // NW - 1) as it:
                for j in range(NW):
                    store(it * NW + j, it * NW + (j + 2))
                    sp.wait_ge(y_ps, it * NW + (j + 1))
                    load_expert(j, it * NW + (NW + j))
            for n in range(NMAIN - NW, NMAIN):
                store(n, n + 2)
            sp.wait_ge(idx_ready, 1)
            nover = sp.value_load(OVE[0:1, NOVER:NOVER + 1], min_val=0, max_val=NOVER)
            with sp.Fori(0, NOVER) as b:
                eid = sp.value_load(OVE[0:1, bass.ds(b, 1)], min_val=0, max_val=NE - 1)
                with sp.If(b < nover):
                    sp.wait_ge(y_ps, NMAIN + b)
                    load_expert(0, eid)
                    store(b + NMAIN, b + (NMAIN + 2))
                with sp.Else():
                    sp.nop()
            sp.wait_ge(f_sum, 1)
            sp.dma_start(GFB, t["final_norm_g"].partition_broadcast(P)).then_inc(gf_in, 16)
            for i in range(NT):
                sp.wait_ge(f_ready, i + 1)
                sp.dma_start(out_d[i], OUT[i % 2]).then_inc(out_done[i % 2], 16)
            sp.wait_ge(out_done[0], 16 * (NT // 2))
            sp.wait_ge(out_done[1], 16 * (NT // 2))

        @block.tensor
        def _(pe):
            def turn(out, in_, n=P):
                return pe.transpose(out, in_, IDENT[0:n, 0:n])

            pe.wait_ge(masks_set, 7)

            def norm1_turn(i):
                pe.wait_ge(hn_ready, i + 1)
                for h in range(2):
                    if i >= 1:
                        pe.wait_ge(hnt_act if h == 0 else hnt_dve, i)
                    for q in range(4):
                        k = 4 * h + q
                        ins = turn(ps[h][:, q * P:(q + 1) * P], XB[i % 3][:, k * P:(k + 1) * P])
                    ins.then_inc(hnt_ps, 1)

            def proj(n):
                kind, a, b = PROJ[n]
                bank = ps[4 + n % 4]
                if n >= 4:
                    pe.wait_ge(proj_act, n - 3)
                need = a + 1 if kind == "T" else 4 * a + 4
                pe.wait_ge(hnt_act, need)
                pe.wait_ge(hnt_dve, need)
                for k in range(KD):
                    if n < 3:
                        pe.wait_ge(win_in[k], 16)
                    if kind == "T":
                        c0, w = T_COLS[b]
                        ins = pe.matmul(bank[:, 0:w], HNT[:, k, a * P:(a + 1) * P], W_IN[:, k, c0:c0 + w],
                                        start=(k == 0), stop=(k == KD - 1))
                    else:
                        ins = pe.matmul(bank[:, :], W_IN[:, k, F_COLS[b]:F_COLS[b] + P],
                                        HNT[:, k, a * 512:(a + 1) * 512], start=(k == 0), stop=(k == KD - 1))
                ins.then_inc(proj_ps, 1)

            def latent_turn(i):
                pe.wait_ge(lat_ready, i + 1)
                pe.wait_ge(krp_ready, i + 1)
                if i >= 1:
                    pe.wait_ge(latt_sb, i)
                c = CQR[i % 2]
                for q in range(3):
                    turn(ps[2][:, q * P:(q + 1) * P], c[:, q * P:(q + 1) * P])
                turn(ps[2][0:QK, 3 * P:4 * P], KRP[i % 2]).then_inc(latt_ps, 1)

            norm1_turn(0)
            n = 0
            for s in range(2):
                for i in range(4 * s, 4 * s + 4):
                    if i + 1 < NT:
                        norm1_turn(i + 1)
                    for b in range(3):
                        proj(n)
                        n += 1
                    if i >= 1:
                        latent_turn(i - 1)
                for m in range(6):
                    proj(n)
                    n += 1
            latent_turn(NT - 1)

            pe.wait_ge(hnt_act, NT)
            pe.wait_ge(hnt_dve, NT)
            pe.wait_ge(latt_sb, NT)
            pe.wait_ge(proj_act, NPROJ)
            for kind in range(2):
                for half in range(2):
                    for q in range(4):
                        i = 4 * half + q
                        ins = turn(ps[2 * kind + half][0:MLH, q * P:(q + 1) * P],
                                   GATES[:, i * 8 + 4 * kind:i * 8 + 4 * kind + 4])
                    ins.then_inc(gate_ps, 1)
            for m in range(2):
                for half in range(2):
                    for q in range(4):
                        i = 4 * half + q
                        ins = turn(ps[4 + 2 * m + half][:, q * P:(q + 1) * P], KTOK[:, i, m * P:(m + 1) * P])
                    ins.then_inc(ktm_ps, 1)
            j = 0
            for f in range(2):
                pe.wait_ge(conv_done, f + 1)
                for g in range(2):
                    for half in range(2):
                        if j < 4:
                            pe.wait_ge(ktm_sb, j + 1)
                        else:
                            pe.wait_ge(lgate_sb, j - 3)
                        pe.matmul(ps[4 + j % 4][:, :], BD[:, (2 * g + f) * P:(2 * g + f + 1) * P],
                                  LT[f][0][:, half * 512:(half + 1) * 512], start=True, stop=True).then_inc(lgate_ps, 1)
                        j += 1
            pe.wait_ge(rows_done, 5)
            for half in range(2):
                for q in range(4):
                    i = 4 * half + q
                    ins = turn(ps[half][:, q * P:(q + 1) * P], ROWS4[:, i * P:(i + 1) * P])
                ins.then_inc(cols_ps, 1)
            for h in range(MLH):
                ins = pe.matmul(ps[2][:, h * NT:(h + 1) * NT], SEL[:, h * P:(h + 1) * P], DEC[:, :], start=True, stop=True)
            ins.then_inc(cols_ps, 1)
            pe.wait_ge(cols_sb, 3)
            pe.wait_ge(lgate_sb, 8)

            def chunk_front(c):
                if c >= 1:
                    pe.wait_ge(d_ready, c)
                    pe.wait_ge(pw_ready, c)
                for h in range(MLH):
                    ins = pe.matmul(ps[0][:, h * P:(h + 1) * P], SEL[:, h * P:(h + 1) * P],
                                    ROW_A[:, c * P:(c + 1) * P], start=True, stop=True)
                ins.then_inc(db_ps, 1)
                for par in range(2):
                    for m in range(2):
                        r = slice(64 * par, 64 * par + 64)
                        ins = pe.matmul(ps[1 + par][:, m * P:(m + 1) * P], KTM[r, m, c * P:(c + 1) * P],
                                        MQT[r, m, c * P:(c + 1) * P], start=True, stop=True)
                ins.then_inc(st_ps, 1)

            def chunk_back(c):
                pe.wait_ge(state_ready, c + 1)
                if c >= 1:
                    pe.wait_ge(inter_sb, c)
                for par in range(2):
                    for m in range(2):
                        r = slice(64 * par, 64 * par + 64)
                        ins = pe.matmul(ps[4 + par][:, m * VA:(m + 1) * VA], MQT[r, m, c * P:(c + 1) * P],
                                        CST[r, m * VA:(m + 1) * VA], start=True, stop=True)
                ins.then_inc(inter_ps, 1)
                pe.wait_ge(ks_ready, c + 1)
                for m in range(2):
                    ins = pe.matmul(ps[6][:, m * 2 * VA:(m + 1) * 2 * VA], KSB[:, m * P:(m + 1) * P],
                                    VAUG[:, c, 2 * m:2 * m + 2, :], start=True, stop=True)
                ins.then_inc(upd_ps, 1)
                pe.wait_ge(pw_ready, c + 1)
                if c >= 1:
                    pe.wait_ge(num_ready, c)
                for h in range(MLH):
                    ins = pe.matmul(ps[3][:, h * VA:(h + 1) * VA], PWB[:, h * P:(h + 1) * P], VAUG[:, c, h, :],
                                    start=True, stop=True)
                ins.then_inc(intra_ps, 1)

            def chunk_turn(c):
                pe.wait_ge(ymt_ready, c + 1)
                if c >= 1:
                    pe.wait_ge(ym_sb, c)
                for m in range(2):
                    ins = turn(ps[7][:, m * P:(m + 1) * P], NUM[:, m * P:(m + 1) * P])
                ins.then_inc(ym_ps, 1)

            pe.wait_ge(ktm_sb, 4)
            for c in range(NT):
                chunk_front(c)
                chunk_back(c)
                chunk_turn(c)
            pe.wait_ge(yr_sq, 2)
            for half in range(2):
                for f in range(2):
                    ins = pe.matmul(ps[half][:, :], ONES[:, :], LT[f][3][:, half * 512:(half + 1) * 512],
                                    start=(f == 0), stop=(f == 1))
                ins.then_inc(yr_ps, 1)

            pe.wait_ge(wu_in, 32)
            pe.wait_ge(yr_rstd, 2)
            pe.wait_ge(ym_sb, NT)
            j = 0
            for h in range(H):
                for half in range(2):
                    if j >= 4:
                        pe.wait_ge(kv_sb, j - 3)
                    pe.matmul(ps[j % 4][0:NOPE, :], W_UKV[:, h, 0:NOPE], CKVT[:, half * 512:(half + 1) * 512],
                              start=True, stop=True).then_inc(kv_ps, 1)
                    j += 1
            for i in range(NT):
                pe.wait_ge(kv_sb, j - 3)
                pe.matmul(ps[j % 4][:, :], CKVT[:, i * P:(i + 1) * P], W_UKV[:, :, NOPE:],
                          start=True, stop=True).then_inc(kv_ps, 1)
                j += 1

            def q_proj(i):
                if i >= 1:
                    pe.wait_ge(q_sb, i)
                for b in range(2):
                    for k in range(2):
                        ins = pe.matmul(ps[4 + b][:, 0:384], CQT[:, k, i * P:(i + 1) * P],
                                        W_UQ[:, k, b * 384:(b + 1) * 384], start=(k == 0), stop=(k == 1))
                ins.then_inc(q_ps, 1)

            def q_turn(i):
                pe.wait_ge(q_rope, i + 1)
                for b in range(2):
                    if i >= 1:
                        pe.wait_ge(qt_act if b == 0 else qt_dve, i)
                    for q in range(4):
                        ins = turn(ps[6 + b][0:QK, q * P:(q + 1) * P], QTOK[i % 2][:, 4 * b + q, :])
                    ins.then_inc(qt_ps, 1)

            q_proj(0)
            for i in range(NT):
                if i + 1 < NT:
                    q_proj(i + 1)
                q_turn(i)

            def scores(n):
                i, h = ATT[n]
                if n >= 2:
                    pe.wait_ge(p_ready, n - 1)
                L = (i + 1) * P
                for b in range((L + 511) // 512):
                    w = min(512, L - 512 * b)
                    ins = pe.matmul(ps[2 * (n % 2) + b][:, 0:w], QT[0:QK, h, i * P:(i + 1) * P],
                                    KT[0:QK, h, 512 * b:512 * b + w], start=True, stop=True)
                ins.then_inc(s_ps, 1)

            def probs_turn(n):
                i, h = ATT[n]
                pe.wait_ge(p_ready, n + 1)
                for g in range(G0[n + 1] - G0[n]):
                    gg = G0[n] + g
                    if gg >= 2:
                        pe.wait_ge(pt_act if gg % 2 == 0 else pt_dve, gg // 2)
                    for q in range(min(4, i + 1 - 4 * g)):
                        ins = turn(ps[4 + gg % 2][:, q * P:(q + 1) * P], PB[n % 2][:, (4 * g + q) * P:(4 * g + q + 1) * P])
                    ins.then_inc(pt_ps, 1)

            def values(n):
                i, h = ATT[n]
                if n >= 2:
                    pe.wait_ge(pv_sb, n - 1)
                for kb in range(i + 1):
                    gg = G0[n] + kb // 4
                    if kb % 4 == 0:
                        pe.wait_ge(pt_act if gg % 2 == 0 else pt_dve, gg // 2 + 1)
                    q = kb % 4
                    ins = pe.matmul(ps[6 + n % 2][:, 0:VD], PTB[gg % 4][:, q * P:(q + 1) * P], V[:, kb, h, :],
                                    start=(kb == 0), stop=(kb == i))
                ins.then_inc(pv_ps, 1)

            pe.wait_ge(kv_sb, 24)
            pe.wait_ge(kr_sb, 1)
            pe.wait_ge(qt_act, NT)
            pe.wait_ge(qt_dve, NT)
            N = len(ATT)
            scores(0)
            for n in range(N):
                if n + 1 < N:
                    scores(n + 1)
                probs_turn(n)
                if n >= 1:
                    values(n - 1)
            values(N - 1)

            pe.wait_ge(pv_sb, N)
            pe.wait_ge(wout_in, 16)
            pe.wait_ge(yr_done, 1)

            def ya_turn(i):
                pe.wait_ge(ya_ready, i + 1)
                if i >= 1:
                    pe.wait_ge(yat_sb, i)
                for q in range(4):
                    ins = turn(ps[4][:, q * P:(q + 1) * P], YA[:, i, q * P:(q + 1) * P])
                ins.then_inc(yat_ps, 1)

            def out_proj(i):
                pe.wait_ge(yat_sb, i + 1)
                if i >= 2:
                    pe.wait_ge(x2_ready, i - 1)
                cols = slice(i * P, (i + 1) * P)
                lhs = [YM[:, 0, cols], YM[:, 1, cols], RXP[:, 0, 3 + i * P:3 + (i + 1) * P],
                       RXP[:, 1, 3 + i * P:3 + (i + 1) * P]] + [YAT[i % 2][:, q * P:(q + 1) * P] for q in range(4)]
                for b in range(2):
                    for k in range(KD):
                        ins = pe.matmul(ps[2 * (i % 2) + b][:, :], lhs[k], W_OUT[:, k, b * 512:(b + 1) * 512],
                                        start=(k == 0), stop=(k == KD - 1))
                ins.then_inc(o_ps, 1)

            def router(i):
                pe.wait_ge(x2n_ready, i + 1)
                for h in range(2):
                    if i >= 1:
                        pe.wait_ge(x2nt_act if h == 0 else x2nt_dve, i)
                    for q in range(4):
                        k = 4 * h + q
                        ins = turn(ps[5 + h][:, q * P:(q + 1) * P], X2N[i % 2][:, k * P:(k + 1) * P])
                    ins.then_inc(x2nt_ps, 1)
                pe.wait_ge(x2nt_act, i + 1)
                pe.wait_ge(x2nt_dve, i + 1)
                if i >= 1:
                    pe.wait_ge(r_sb, i)
                for k in range(KD):
                    ins = pe.matmul(ps[7][:, 0:36], X2NT[i % 2][:, k, :], WR[:, k * 36:(k + 1) * 36],
                                    start=(k == 0), stop=(k == KD - 1))
                ins.then_inc(r_ps, 1)

            ya_turn(0)
            for i in range(NT):
                if i + 1 < NT:
                    ya_turn(i + 1)
                out_proj(i)
                if i >= 1:
                    router(i - 1)
            router(NT - 1)

            pe.wait_ge(mask_ready, 1)
            mask = RA[:, 0:NT * NE].rearrange("p (i e) -> p i e", i=NT)
            for i in range(NT):
                pe.matmul(ps[0][:, i * NE:(i + 1) * NE], TRI[:, :], mask[:, i, :], start=True, stop=(i == 0))
                for i2 in range(i):
                    pe.matmul(ps[0][:, i * NE:(i + 1) * NE], ONES[:, :], mask[:, i2, :], start=False, stop=(i2 == i - 1))
            for i in range(NT):
                ins = pe.matmul(ps[1][:, 0:NE], ONES[:, :], mask[:, i, :], start=(i == 0), stop=(i == NT - 1))
            ins.then_inc(pos_ps, 1)
            pe.wait_ge(ids_in, 16)
            turn(ps[2][:, 0:NBLK], IDR[:, :], NBLK).then_inc(ids_ps, 1)
            pe.wait_ge(idx_ready, 1)

            def rows_turn(u, done):
                pe.wait_ge(xgt_act, done)
                pe.wait_ge(xgt_dve, done)
                for h in range(2):
                    for q in range(4):
                        k = 4 * h + q
                        ins = turn(ps[h][:, q * P:(q + 1) * P], XG[u][:, k * P:(k + 1) * P])
                    ins.then_inc(xgt_ps, 1)

            def gate_up(u, w, done):
                pe.wait_ge(xgt_act, done + 1)
                pe.wait_ge(xgt_dve, done + 1)
                for g in range(2):
                    for m in range(2):
                        for k in range(KD):
                            ins = pe.matmul(ps[2 + 2 * u + g][:, m * P:(m + 1) * P],
                                            WGU[w][:, g, k, m * P:(m + 1) * P], XGT[u][:, k, :],
                                            start=(k == 0), stop=(k == KD - 1))
                    ins.then_inc(gu_ps, 1)

            def down(u, w, done):
                pe.wait_ge(h_ready, done + 1)
                pe.wait_ge(y_act, done)
                pe.wait_ge(y_dve, done)
                for b in range(2):
                    for k in range(2):
                        ins = pe.matmul(ps[6 + b][:, :], HT[u][:, k, :], WDN[w][:, k, b * 512:(b + 1) * 512],
                                        start=(k == 0), stop=(k == 1))
                ins.then_inc(y_ps, 1)

            pe.wait_ge(xg_in[0], 16)
            rows_turn(0, 1)
            with pe.Fori(0, NMAIN // NW) as it:
                for j in range(NW):
                    u = j % 2
                    pe.wait_ge(w_in_[j], it * 48 + 48)
                    gate_up(u, j, it * NW + (j + 1))
                    pe.wait_ge(xg_in[1 - u], it * (NW // 2 * 16) + 16 * ((j + 1) // 2 + 1))
                    rows_turn(1 - u, it * NW + (j + 2))
                    down(u, j, it * NW + (j + 1))
            nover = pe.value_load(OVE[0:1, NOVER:NOVER + 1], min_val=0, max_val=NOVER)
            with pe.Fori(0, NOVER) as b:
                with pe.If(b < nover):
                    pe.wait_ge(xg_in[0], (NMAIN // 2 + 2) * 16 + b * 16)
                    pe.wait_ge(w_in_[0], (NMAIN // NW) * 48 + 48 + b * 48)
                    rows_turn(0, NMAIN + 2 + b)
                    gate_up(0, 0, NMAIN + 2 + b)
                    down(0, 0, NMAIN + 1 + b)
                with pe.Else():
                    pe.nop()

        @block.scalar
        def _(act):
            link = chained(act, act_chain)

            def col_load(dst, src, n):
                act.dma_start(dst, src).then_inc(const_in, 16)

            row = lambda a: a.rearrange("l n -> (l n)").partition_broadcast(P)
            colw = lambda a: a[0].rearrange("(f p) -> p f", p=P)
            with nc.allow_non_contiguous_dma(reason="small columns"):
                act.dma_start(GQ[:, 0:QL], row(t["q_norm_g"])).then_inc(const_in, 16)
                act.dma_start(GQ[:, QL:], row(t["kv_norm_g"])).then_inc(const_in, 16)
                act.dma_start(COS[:, :].rearrange("p (i n) -> p i n", i=NT), t["rope_cos"].rearrange("(i p) n -> p i n", p=P)).then_inc(const_in, 16)
                act.dma_start(SIN[:, :].rearrange("p (i n) -> p i n", i=NT), t["rope_sin"].rearrange("(i p) n -> p i n", p=P)).then_inc(const_in, 16)
                act.dma_start(BGI[:, :], t["ml_i_bias"].rearrange("l h -> h l")).then_inc(const_in, 16)
                act.dma_start(BGF[:, :], t["ml_f_bias"].rearrange("l h -> h l")).then_inc(const_in, 16)
                for f in range(2):
                    act.dma_start(CW[:, f * CONV:(f + 1) * CONV], t["conv_w"][0, :, f * P:(f + 1) * P].rearrange("j p -> p j")).then_inc(const_in, 16)
                act.dma_start(CB[:, :], colw(t["conv_b"])).then_inc(const_in, 16)
                act.dma_start(BR[:, :], colw(t["lru_b_r"])).then_inc(const_in, 16)
                act.dma_start(BI[:, :], colw(t["lru_b_i"])).then_inc(const_in, 16)
                act.dma_start(LAM[:, :], colw(t["lru_lambda"])).then_inc(const_in, 16)
                act.dma_start(GLRU[:, :], colw(t["lru_norm_g"])).then_inc(const_in, 16)
                act.dma_start(GML[:, :], row(t["ml_norm_g"])).then_inc(const_in, 16)
                act.dma_start(GMLA[:, :], row(t["mla_norm_g"])).then_inc(const_in, 16)
                act.wait_ge(masks_set, 7)
                for g, w in enumerate(("lru_w_r", "lru_w_i")):
                    for f in range(2):
                        for q in range(2):
                            r = slice(64 * q, 64 * q + 64)
                            c0 = (2 * g + f) * P + 64 * q
                            act.dma_start(BD[r, c0:c0 + 64], t[w][0, 2 * f + q]).then_inc(const_in, 16)
                wr = WR[:, :].rearrange("p (k n) -> p k n", k=KD)
                act.dma_start(wr[:, :, 0:NG], t["w_group"][0].rearrange("(k p) n -> p k n", p=P)).then_inc(const_in, 16)
                act.dma_start(wr[:, :, NG:], t["w_expert"][0].rearrange("(k p) n -> p k n", p=P)).then_inc(const_in, 16)
                act.dma_start(BRT[:, 0:NG], row(t["b_group"])).then_inc(const_in, 16)
                act.dma_start(BRT[:, NG:], row(t["b_expert"])).then_inc(const_in, 16)

            def norm1_stats(i):
                act.wait_ge(x_in[i % 3], 16 * (i // 3 + 1))
                link(act.activation(JUNK[:, :], XB[i % 3], ACT.Square, accum_out=ST1[:, i:i + 1]))
                link(act.activation(ST1[:, NT + i:NT + i + 1], ST1[:, i:i + 1], ACT.Ln, bias=EPSC[:, :], scale=1.0 / D))
                act.activation(ST1[:, NT + i:NT + i + 1], ST1[:, NT + i:NT + i + 1], ACT.Exp, scale=-0.5).then_inc(x_rstd, 1)

            def norm1_evac(i):
                act.wait_ge(hnt_ps, 2 * i + 1)
                act.activation(HNT[:, 0:4, i * P:(i + 1) * P], ps[0][:, :].rearrange("p (k n) -> p k n", k=4),
                               ACT.Copy).then_inc(hnt_act, 1)

            def proj_evac(n):
                kind, a, b = PROJ[n]
                bank = ps[4 + n % 4]
                act.wait_ge(proj_ps, n + 1)
                if kind == "F":
                    s = slice(a * 512, (a + 1) * 512)
                    dst = [MQT[:, 0, s], MQT[:, 1, s], RXP[:, 0, 3 + a * 512:3 + (a + 1) * 512],
                           RXP[:, 1, 3 + a * 512:3 + (a + 1) * 512], RG[:, 0, s], RG[:, 1, s]][b]
                    act.activation(dst, bank[:, :], ACT.Copy).then_inc(proj_act, 1)
                elif b == 0:
                    act.activation(KTOK[:, a, :], bank[:, 0:MLW], ACT.Copy, scale=MLD ** -0.5)
                    act.activation(VAUG[:, a, :, 0:MLD], bank[:, MLW:512].rearrange("p (h n) -> p h n", h=MLH), ACT.Copy).then_inc(proj_act, 1)
                elif b == 1:
                    act.activation(GATES[:, a * 8:a * 8 + 8], bank[:, MLW:MLW + 8], ACT.Copy)
                    act.activation(OTOK[:, a, :], bank[:, 0:MLW], ACT.Exp, scale=-1.0).then_inc(proj_act, 1)
                else:
                    if a >= 2:
                        act.wait_ge(latt_ps, a - 1)
                    act.activation(CQR[a % 2], bank[:, 0:N_LAT], ACT.Copy).then_inc(proj_act, 1)
                    act.wait_ge(proj_act, n + 1)
                    c = CQR[a % 2]
                    act.activation(JUNK[:, 0:QL], c[:, 0:QL], ACT.Square, accum_out=ST2[:, 2 * a:2 * a + 1])
                    link(act.activation(JUNK[:, QL:QL + KVL], c[:, QL:QL + KVL], ACT.Square, accum_out=ST2[:, 2 * a + 1:2 * a + 2]))
                    o = 2 * NT + 2 * a
                    act.activation(ST2[:, o:o + 1], ST2[:, 2 * a:2 * a + 1], ACT.Ln, bias=EPSC[:, :], scale=1.0 / QL)
                    link(act.activation(ST2[:, o + 1:o + 2], ST2[:, 2 * a + 1:2 * a + 2], ACT.Ln, bias=EPSC[:, :], scale=1.0 / KVL))
                    act.activation(ST2[:, o:o + 2], ST2[:, o:o + 2], ACT.Exp, scale=-0.5).then_inc(lat_rstd, 1)

            def latent_evac(i):
                act.wait_ge(latt_ps, i + 1)
                s = slice(i * P, (i + 1) * P)
                act.activation(CQT[:, :, s], ps[2][:, 0:2 * P].rearrange("p (m n) -> p m n", m=2), ACT.Copy)
                act.activation(CKVT[:, s], ps[2][:, 2 * P:3 * P], ACT.Copy)
                act.activation(KPT[0:QK, s], ps[2][0:QK, 3 * P:4 * P], ACT.Copy).then_inc(latt_sb, 1)

            norm1_stats(0)
            norm1_stats(1)
            norm1_evac(0)
            n = 0
            for s in range(2):
                for i in range(4 * s, 4 * s + 4):
                    if i + 2 < NT:
                        norm1_stats(i + 2)
                    if i + 1 < NT:
                        norm1_evac(i + 1)
                    for b in range(3):
                        proj_evac(n)
                        n += 1
                    if i >= 1:
                        latent_evac(i - 1)
                for m in range(6):
                    proj_evac(n)
                    n += 1
            latent_evac(NT - 1)

            act.wait_ge(const_in, 16 * NC_)
            for kind, dst, bias in ((0, ROW_I, BGI), (1, ROW_F, BGF)):
                for half in range(2):
                    act.wait_ge(gate_ps, 2 * kind + half + 1)
                    act.activation(dst[:, half * 512:(half + 1) * 512], ps[2 * kind + half][0:MLH, :], ACT.Identity,
                                   bias=bias[:, :]).then_inc(gate_rows, 1)
            act.wait_ge(gate_rows, 4)
            link(act.activation(ROW_T, ROW_F, ACT.Abs))
            link(act.activation(ROW_T, ROW_T, ACT.Exp, scale=-1.0))
            act.activation(ROW_T, ROW_T, ACT.Ln, bias=ONEC[0:MLH, :]).then_inc(lf_t, 1)
            for j in range(4):
                act.wait_ge(ktm_ps, j + 1)
                m, half = j // 2, j % 2
                act.activation(KTM[:, m, half * 512:(half + 1) * 512], ps[4 + j][:, :], ACT.Copy).then_inc(ktm_sb, 1)
            act.wait_ge(lam_s, 1)
            act.activation(SPT[:, 2:4], SPT[:, 0:2], ACT.Exp, scale=-1.0).then_inc(lam_s, 1)
            act.wait_ge(rows_pre, 1)
            act.activation(ROWS4[32:32 + MLH, :], ROW_T, ACT.Exp).then_inc(rows_done, 1)
            act.activation(ROWS4[64:64 + MLH, :], ROW_T2, ACT.Exp).then_inc(rows_done, 1)
            act.activation(ROWS4[96:96 + MLH, :], ROW_M, ACT.Exp, scale=-1.0).then_inc(rows_done, 1)
            act.activation(DEC[:, :], MPV[:, :], ACT.Exp).then_inc(rows_done, 1)
            act.wait_ge(lam_done, 1)
            for f in range(2):
                XC, R, IV, T, D1 = LT[f]
                act.wait_ge(gelu_arg, f + 1)
                act.activation(D1, T, ACT.Sigmoid, scale=GELU_S).then_inc(gelu_sig, 1)
                for g in range(2):
                    for half in range(2):
                        j = 4 * f + 2 * g + half
                        act.wait_ge(lgate_ps, j + 1)
                        act.activation((R, IV)[g][:, half * 512:(half + 1) * 512], ps[4 + j % 4][:, :], ACT.Sigmoid,
                                       bias=(BR, BI)[g][:, f:f + 1]).then_inc(lgate_sb, 1)
                act.wait_ge(lgate_sb, 4 * f + 4)
                act.wait_ge(gelu_done, f + 1)
                act.activation(T, R, ACT.Tanh, scale=SPT[:, 8 + f:9 + f]).then_inc(lru_a, 1)
                act.wait_ge(lru_a, 2 * f + 1)
                act.activation(R, R, ACT.Exp, scale=SPT[:, 10 + f:11 + f]).then_inc(lru_a, 1)
            for f in range(2):
                act.wait_ge(lru_ratio, f + 1)
                act.activation(LT[f][3], LT[f][3], ACT.Sqrt).then_inc(lru_root, 1)
            act.wait_ge(cols_sb, 3)
            act.wait_ge(zero_out, 16 * NOVER)
            col = COL[:, :].rearrange("p (i k h) -> p i k h", i=NT, k=4)
            for c in range(NT):
                act.wait_ge(d_ready, c + 1)
                if c >= 1:
                    act.wait_ge(pw_ready, c)
                for h in range(MLH):
                    ins = act.activation(WSB[:, h * P:(h + 1) * P], DSB[:, h * P:(h + 1) * P], ACT.Exp,
                                         bias=col[:, c, 0, h:h + 1])
                ins.then_inc(w_ready, 1)
                act.wait_ge(inter_ps, c + 1)
                if c >= 1:
                    act.wait_ge(num_ready, c)
                for h in range(MLH):
                    ins = act.activation(INT[:, h * VA:(h + 1) * VA], ps[4 + h % 2][:, (h // 2) * VA:(h // 2 + 1) * VA],
                                         ACT.Copy, scale=col[:, c, 1, h:h + 1])
                ins.then_inc(inter_sb, 1)
                act.wait_ge(mh_ss, c + 1)
                link(act.activation(DEN[:, 8:12], DEN[:, 4:8], ACT.Ln, bias=EPSC[:, :], scale=1.0 / MLD))
                act.activation(DEN[:, 12:16], DEN[:, 8:12], ACT.Exp, scale=-0.5).then_inc(mh_rstd, 1)
                act.wait_ge(ym_ps, c + 1)
                act.activation(YM[:, :, c * P:(c + 1) * P], ps[7][:, 0:2 * P].rearrange("p (m n) -> p m n", m=2),
                               ACT.Copy).then_inc(ym_sb, 1)
            R = LT[0][1]
            act.wait_ge(yr_sq, 2)
            for half in range(2):
                s = slice(half * 512, (half + 1) * 512)
                act.wait_ge(yr_ps, half + 1)
                link(act.activation(R[:, s], ps[half][:, :], ACT.Ln, bias=EPSC[:, :], scale=1.0 / LRU))
                act.activation(R[:, s], R[:, s], ACT.Exp, scale=-0.5).then_inc(yr_rstd, 1)

            for j in range(24):
                act.wait_ge(kv_ps, j + 1)
                if j == 0:
                    act.wait_ge(yr_done, 1)
                if j < 16:
                    h, half = j // 2, j % 2
                    act.activation(KT[0:NOPE, h, half * 512:(half + 1) * 512], ps[j % 4][0:NOPE, :], ACT.Copy).then_inc(kv_sb, 1)
                else:
                    act.activation(V[:, j - 16].rearrange("p h n -> p (h n)"), ps[j % 4][:, :], ACT.Copy).then_inc(kv_sb, 1)
            for i in range(NT):
                act.wait_ge(q_ps, i + 1)
                if i >= 2:
                    act.wait_ge(qt_ps, 2 * (i - 1))
                for b in range(2):
                    ins = act.activation(QTOK[i % 2][:, 4 * b:4 * b + 4, :], ps[4 + b][:, 0:384].rearrange("p (h n) -> p h n", h=4), ACT.Copy)
                ins.then_inc(q_sb, 1)
                if i >= 1:
                    act.wait_ge(qt_ps, 2 * i - 1)
                    act.activation(QT[0:QK, 0:4, (i - 1) * P:i * P], ps[6][0:QK, :].rearrange("p (h n) -> p h n", h=4), ACT.Copy).then_inc(qt_act, 1)
            act.wait_ge(qt_ps, 2 * NT - 1)
            act.activation(QT[0:QK, 0:4, (NT - 1) * P:NT * P], ps[6][0:QK, :].rearrange("p (h n) -> p h n", h=4), ACT.Copy).then_inc(qt_act, 1)

            def probs(n):
                i, h = ATT[n]
                L = (i + 1) * P
                act.wait_ge(s_max, n + 1)
                if n >= 2:
                    act.wait_ge(pt_ps, G0[n - 1])
                for b in range((L + 511) // 512):
                    w = min(512, L - 512 * b)
                    ins = act.activation(PB[n % 2][:, 512 * b:512 * b + w], ps[2 * (n % 2) + b][:, 0:w], ACT.Exp,
                                         bias=NMX[:, n:n + 1], scale=SCALE,
                                         accum_out=(RSM if b == 0 else RIN)[:, n:n + 1])
                ins.then_inc(p_ready, 1)

            def probs_evac(n):
                i, h = ATT[n]
                for gg in range(G0[n], G0[n + 1]):
                    if gg % 2 == 0:
                        act.wait_ge(pt_ps, gg + 1)
                        if gg >= 4:
                            act.wait_ge(pv_ps, GROUPS[gg - 4][0] + 1)
                        w = P * min(4, i + 1 - 4 * GROUPS[gg][1])
                        act.activation(PTB[gg % 4][:, 0:w], ps[4][:, 0:w], ACT.Copy).then_inc(pt_act, 1)

            N = len(ATT)
            probs(0)
            for n in range(N):
                if n + 1 < N:
                    probs(n + 1)
                probs_evac(n)

            act.wait_ge(pv_sb, N)
            for i in range(NT):
                act.activation(JUNK[:, 0:H * VD], YA[:, i, :], ACT.Square, accum_out=ST1[:, i:i + 1]).then_inc(ya_sq, 1)
                act.wait_ge(ya_sq, i + 1)
            act.wait_ge(ya_sq, NT)
            link(act.activation(ST1[:, NT:], ST1[:, 0:NT], ACT.Ln, bias=EPSC[:, :], scale=1.0 / (H * VD)))
            act.activation(ST2[:, 0:NT], ST1[:, NT:], ACT.Exp, scale=-0.5).then_inc(ya_rstd, 1)
            act.wait_ge(ya_rstd, 1)
            for i in range(NT):
                act.wait_ge(yat_ps, i + 1)
                if i >= 2:
                    act.wait_ge(o_ps, i - 1)
                act.activation(YAT[i % 2], ps[4][:, :], ACT.Copy).then_inc(yat_sb, 1)

                def after_x2(i):
                    act.wait_ge(x2_ready, i + 1)
                    link(act.activation(JUNK[:, :], X2[:, i, :], ACT.Square, accum_out=ST1[:, i:i + 1]))
                    link(act.activation(ST1[:, NT + i:NT + i + 1], ST1[:, i:i + 1], ACT.Ln, bias=EPSC[:, :], scale=1.0 / D))
                    act.activation(ST2[:, NT + i:NT + i + 1], ST1[:, NT + i:NT + i + 1], ACT.Exp, scale=-0.5).then_inc(x2_rstd, 1)

                def after_turn(i):
                    act.wait_ge(x2nt_ps, 2 * i + 1)
                    if i >= 2:
                        act.wait_ge(r_ps, i - 1)
                    act.activation(X2NT[i % 2][:, 0:4, :], ps[5][:, :].rearrange("p (k n) -> p k n", k=4), ACT.Copy).then_inc(x2nt_act, 1)

                if i >= 1:
                    after_x2(i - 1)
                if i >= 2:
                    after_turn(i - 2)
            after_x2(NT - 1)
            after_turn(NT - 2)
            after_turn(NT - 1)
            act.wait_ge(rt_a, 1)
            act.activation(RB[:, 8 * NT:12 * NT], RB[:, 4 * NT:8 * NT], ACT.Exp).then_inc(rt_b, 1)
            act.wait_ge(rt_a, 2)
            act.activation(RB[:, 13 * NT:14 * NT], RB[:, 12 * NT:13 * NT], ACT.Exp).then_inc(rt_b, 1)
            act.wait_ge(idx_ready, 1)

            def rows_evac(u, done):
                act.wait_ge(xgt_ps, done)
                act.activation(XGT[u][:, 0:4, :], ps[0][:, :].rearrange("p (k n) -> p k n", k=4), ACT.Copy).then_inc(xgt_act, 1)

            def silu(u, gates, prior):
                act.wait_ge(gu_ps, gates)
                act.wait_ge(h_ready, prior)
                act.activation(SG, ps[2 + 2 * u][:, 0:2 * P], ACT.Silu).then_inc(sg_ready, 1)

            def y_evac(done):
                act.wait_ge(y_ps, done)
                act.activation(YB[0], ps[6][:, :], ACT.Copy).then_inc(y_act, 1)

            act.sem_inc(xgt_act, 1)
            act.sem_inc(y_act, 1)
            rows_evac(0, 1)
            with act.Fori(0, NMAIN // NW) as it:
                for j in range(NW):
                    u = j % 2
                    silu(u, it * (2 * NW) + (2 * j + 1), it * NW + (j + 1))
                    rows_evac(1 - u, it * (2 * NW) + (2 * j + 3))
                    act.wait_ge(y_out[0], it * (16 * NW) + 16 * (j + 1))
                    y_evac(it * NW + (j + 1))
            nover = act.value_load(OVE[0:1, NOVER:NOVER + 1], min_val=0, max_val=NOVER)
            with act.Fori(0, NOVER) as b:
                with act.If(b < nover):
                    rows_evac(0, b * 2 + (2 * NMAIN + 3))
                    silu(0, b * 2 + (2 * NMAIN + 1), b + (NMAIN + 1))
                    act.wait_ge(y_out[0], b * 16 + 16 * (NMAIN + 1))
                    y_evac(b + (NMAIN + 1))
                with act.Else():
                    act.nop()
            for i in range(NT):
                act.wait_ge(f_sum, i + 1)
                link(act.activation(JUNK[:, :], X2[:, i, :], ACT.Square, accum_out=ST1[:, i:i + 1]))
                link(act.activation(ST1[:, NT + i:NT + i + 1], ST1[:, i:i + 1], ACT.Ln, bias=EPSC[:, :], scale=1.0 / D))
                act.activation(ST2[:, i:i + 1], ST1[:, NT + i:NT + i + 1], ACT.Exp, scale=-0.5).then_inc(f_rstd, 1)

        @block.vector
        def _(dve):
            link = chained(dve, dve_chain)
            dve.memset(EPSC[:, :], EPS).then_inc(masks_set, 1)
            dve.memset(ONEC[:, :], 1.0).then_inc(masks_set, 1)
            dve.memset(VAUG[:, :, :, MLD:], 1.0)
            dve.memset(RXP[:, :, 0:3], 0.0)
            dve.memset(CST[:, :], 0.0).then_inc(state_ready, 1)

            def norm1_apply(i):
                dve.wait_ge(x_rstd, i + 1)
                dve.wait_ge(x_in[i % 3], 16 * (i // 3 + 1))
                dve.scalar_tensor_tensor(XB[i % 3], XB[i % 3], ST1[:, NT + i:NT + i + 1], GB[:, :], ALU.mult, ALU.mult).then_inc(hn_ready, 1)

            def norm1_evac(i):
                dve.wait_ge(hnt_ps, 2 * i + 2)
                dve.tensor_copy(HNT[:, 4:8, i * P:(i + 1) * P], ps[1][:, :].rearrange("p (k n) -> p k n", k=4)).then_inc(hnt_dve, 1)

            def tile_evac(i):
                dve.wait_ge(lat_rstd, i + 1)
                c = CQR[i % 2]
                o = 2 * NT + 2 * i
                dve.scalar_tensor_tensor(c[:, 0:QL], c[:, 0:QL], ST2[:, o:o + 1], GQ[:, 0:QL], ALU.mult, ALU.mult)
                dve.scalar_tensor_tensor(c[:, QL:QL + KVL], c[:, QL:QL + KVL], ST2[:, o + 1:o + 2], GQ[:, QL:], ALU.mult, ALU.mult).then_inc(lat_ready, 1)

            dve.wait_ge(const_in, 16 * NC_)
            norm1_apply(0)
            norm1_apply(1)
            norm1_evac(0)
            for i in range(NT):
                if i + 2 < NT:
                    norm1_apply(i + 2)
                if i + 1 < NT:
                    norm1_evac(i + 1)
                tile_evac(i)

            link(dve.tensor_scalar(SPT[:, 4:6], LAM[:, :], -1.0, None, ALU.mult))
            dve.tensor_tensor(SPT[:, 0:2], LAM[:, :], SPT[:, 4:6], ALU.max).then_inc(lam_s, 1)
            dve.wait_ge(lam_s, 2)
            z, w, w2, acc = SPT[:, 2:4], SPT[:, 6:8], SPT[:, 12:14], SPT[:, 14:16]
            link(dve.tensor_scalar(w, z, 2.0, None, ALU.add))
            link(dve.reciprocal(w, w))
            link(dve.tensor_tensor(w, z, w, ALU.mult))
            link(dve.tensor_tensor(w2, w, w, ALU.mult))
            link(dve.tensor_scalar(acc, w2, 1.0 / 17, 1.0 / 15, ALU.mult, ALU.add))
            for odd in (13, 11, 9, 7, 5, 3, 1):
                link(dve.tensor_tensor(acc, acc, w2, ALU.mult))
                link(dve.tensor_scalar(acc, acc, 1.0 / odd, None, ALU.add))
            link(dve.tensor_tensor(acc, acc, w, ALU.mult))
            link(dve.tensor_scalar(acc, acc, 2.0, None, ALU.mult))
            link(dve.scalar_tensor_tensor(acc, SPT[:, 4:6], 0.0, acc, ALU.max, ALU.add))
            link(dve.tensor_scalar(SPT[:, 8:10], acc, LRU_C, None, ALU.mult))
            dve.tensor_scalar(SPT[:, 10:12], SPT[:, 8:10], -1.0, None, ALU.mult).then_inc(lam_done, 1)

            dve.wait_ge(gate_rows, 4)
            dve.wait_ge(lf_t, 1)
            dve.wait_ge(rs_set, 3)
            link(dve.scalar_tensor_tensor(ROW_LF, ROW_F, 0.0, ROW_T, ALU.min, ALU.subtract))
            dve.tensor_tensor_scan(ROW_B, ROW_RS, ROW_LF, 0.0, ALU.mult, ALU.add)
            link(dve.tensor_tensor_scan(ROW_M, ROW_LF, ROW_I, 0.0, ALU.add, ALU.max))
            link(dve.tensor_tensor(ROW_A, ROW_B, ROW_M, ALU.subtract))
            dve.tensor_tensor(ROWS4[0:MLH, :], ROW_I, ROW_B, ALU.subtract).then_inc(rows_done, 1)
            chunks = lambda r: r.rearrange("p (c n) -> p c n", c=NT)
            dve.memset(MPV[:, 0:1], 0.0)
            link(dve.tensor_copy(MPV[:, 1:NT].unsqueeze(2), chunks(ROW_M)[:, 0:NT - 1, P - 1:P]))
            dve.wait_ge(rows_done, 1)
            dve.tensor_tensor(chunks(ROW_T), chunks(ROW_A), MPV[:, :].unsqueeze(2).broadcast_to([MLH, NT, P]), ALU.add)
            link(dve.tensor_tensor(chunks(ROW_T2), chunks(ROWS4[0:MLH, :]), chunks(ROW_A)[:, :, P - 1:P].broadcast_to([MLH, NT, P]), ALU.add))
            dve.tensor_tensor(MPV[:, :].unsqueeze(2), MPV[:, :].unsqueeze(2), chunks(ROW_A)[:, :, P - 1:P], ALU.add).then_inc(rows_pre, 1)

            dve.wait_ge(proj_act, NPROJ)
            for f in range(2):
                XC = LT[f][0]
                link(dve.tensor_scalar(XC, RXP[:, f, 3:3 + S], CW[:, f * CONV + 3:f * CONV + 4], CB[:, f:f + 1], ALU.mult, ALU.add))
                for j in range(CONV - 1):
                    ins = dve.scalar_tensor_tensor(XC, RXP[:, f, j:j + S], CW[:, f * CONV + j:f * CONV + j + 1], XC, ALU.mult, ALU.add)
                    if j < CONV - 2:
                        link(ins)
                    else:
                        ins.then_inc(conv_done, 1)
            o = OTOK.rearrange("p i n -> p (i n)")
            link(dve.tensor_scalar(o, o, 1.0, None, ALU.add))
            link(dve.reciprocal(o, o))
            col = COL[:, :].rearrange("p (i k h) -> p i k h", i=NT, k=4)
            for half in range(2):
                dve.wait_ge(cols_ps, half + 1)
                for q in range(4):
                    ins = dve.tensor_copy(col[:, 4 * half + q], ps[half][:, q * P:(q + 1) * P].rearrange("p (k n) -> p k n", k=4)[:, :, 0:MLH])
                ins.then_inc(cols_sb, 1)
            dve.wait_ge(cols_ps, 3)
            dve.tensor_copy(DECB[:, :], ps[2][:, 0:MLH * NT]).then_inc(cols_sb, 1)
            dve.wait_ge(cols_sb, 3)

            def lru(f):
                XC, R, IV, T, D1 = LT[f]
                dve.wait_ge(lru_a, 2 * f + 2)
                link(dve.tensor_scalar(D1, T, 1.0, None, ALU.add))
                link(dve.reciprocal(D1, D1))
                dve.scalar_tensor_tensor(T, T, 2.0, D1, ALU.mult, ALU.mult).then_inc(lru_ratio, 1)
                link(dve.tensor_tensor(IV, IV, XC, ALU.mult))
                dve.wait_ge(lru_root, f + 1)
                link(dve.tensor_tensor(IV, IV, T, ALU.mult))
                link(dve.tensor_tensor_scan(XC, R, IV, 0.0, ALU.mult, ALU.add))
                link(dve.tensor_tensor(RXP[:, f, 3:3 + S], XC, RG[:, f, :], ALU.mult))
                dve.tensor_tensor(T, RXP[:, f, 3:3 + S], RXP[:, f, 3:3 + S], ALU.mult).then_inc(yr_sq, 1)

            lru(0)
            lru(1)

            heads = lambda a, n: a.rearrange("p (h n) -> p h n", n=n)
            for c in range(NT):
                dve.wait_ge(db_ps, c + 1)
                if c >= 1:
                    dve.wait_ge(w_ready, c)
                dve.tensor_tensor(heads(DSB, P), heads(ps[0][:, :], P), TMASK[:, :].unsqueeze(1).broadcast_to([P, MLH, P]), ALU.add).then_inc(d_ready, 1)
                dve.wait_ge(st_ps, c + 1)
                dve.wait_ge(w_ready, c + 1)
                if c >= 1:
                    dve.wait_ge(intra_ps, c)
                for par in range(2):
                    ins = dve.tensor_tensor(heads(PWB, P)[:, par::2, :], heads(ps[1 + par][:, 0:2 * P], P), heads(WSB, P)[:, par::2, :], ALU.mult)
                ins.then_inc(pw_ready, 1)
                dve.wait_ge(upd_ps, c + 1)
                dve.wait_ge(inter_ps, c + 1)
                for h in range(MLH):
                    par, m = h % 2, h // 2
                    r = slice(64 * par, 64 * par + 64)
                    cs = CST[r, m * VA:(m + 1) * VA]
                    ins = dve.scalar_tensor_tensor(cs, cs, DECB[r, h * NT + c:h * NT + c + 1],
                                                   ps[6][r, (2 * m + par) * VA:(2 * m + par + 1) * VA], ALU.mult, ALU.add)
                ins.then_inc(state_ready, 1)
                dve.wait_ge(intra_ps, c + 1)
                dve.wait_ge(inter_sb, c + 1)
                if c >= 1:
                    dve.wait_ge(ym_ps, c)
                dve.tensor_tensor(NUM, ps[3][:, 0:MLH * VA], INT, ALU.add).then_inc(num_ready, 1)
                dve.wait_ge(num_ready, c + 1)
                num = heads(NUM, VA)
                link(dve.scalar_tensor_tensor(DEN[:, 0:4].unsqueeze(2), num[:, :, MLD:VA], -1.0, num[:, :, MLD:VA], ALU.mult, ALU.max))
                link(dve.tensor_tensor(DEN[:, 0:4], DEN[:, 0:4], col[:, c, 3, :], ALU.max))
                link(dve.reciprocal(DEN[:, 0:4], DEN[:, 0:4]))
                link(dve.tensor_tensor(heads(SQB, MLD), num[:, :, 0:MLD], DEN[:, 0:4].unsqueeze(2).broadcast_to([P, MLH, MLD]), ALU.mult))
                link(dve.tensor_tensor(SQB, SQB, OTOK[:, c, :], ALU.mult))
                link(dve.tensor_tensor(NUM[:, 0:MLW], SQB, SQB, ALU.mult))
                dve.tensor_reduce(DEN[:, 4:8], heads(NUM[:, 0:MLW], MLD), AX.X, ALU.add).then_inc(mh_ss, 1)
                dve.wait_ge(mh_rstd, c + 1)
                link(dve.tensor_tensor(heads(SQB, MLD), heads(SQB, MLD), DEN[:, 12:16].unsqueeze(2).broadcast_to([P, MLH, MLD]), ALU.mult))
                dve.tensor_tensor(NUM[:, 0:MLW], SQB, GML[:, :], ALU.mult).then_inc(ymt_ready, 1)
            dve.wait_ge(yr_rstd, 2)
            for f in range(2):
                ins = dve.scalar_tensor_tensor(RXP[:, f, 3:3 + S], RXP[:, f, 3:3 + S], GLRU[:, f:f + 1], LT[0][1], ALU.mult, ALU.mult)
            ins.then_inc(yr_done, 1)

            for i in range(NT):
                dve.wait_ge(qt_ps, 2 * i + 2)
                dve.tensor_copy(QT[0:QK, 4:8, i * P:(i + 1) * P], ps[7][0:QK, :].rearrange("p (h n) -> p h n", h=4)).then_inc(qt_dve, 1)

            def row_max(n):
                i, h = ATT[n]
                L = (i + 1) * P
                dve.wait_ge(s_ps, n + 1)
                b, o = (i * P) // 512, (i * P) % 512
                diag = ps[2 * (n % 2) + b][:, o:o + P]
                link(dve.tensor_tensor(diag, diag, CMASK[:, :], ALU.add))
                nb = (L + 511) // 512
                for b in range(nb):
                    w = min(512, L - 512 * b)
                    dst = (NMX if b == 0 else RIN)[:, n:n + 1]
                    link(dve.tensor_reduce(dst, ps[2 * (n % 2) + b][:, 0:w], AX.X, ALU.max))
                if nb == 2:
                    link(dve.tensor_tensor(NMX[:, n:n + 1], NMX[:, n:n + 1], RIN[:, n:n + 1], ALU.max))
                dve.tensor_scalar(NMX[:, n:n + 1], NMX[:, n:n + 1], -SCALE, None, ALU.mult).then_inc(s_max, 1)

            def probs_evac(n):
                i, h = ATT[n]
                for gg in range(G0[n], G0[n + 1]):
                    if gg % 2 == 1:
                        dve.wait_ge(pt_ps, gg + 1)
                        if gg >= 4:
                            dve.wait_ge(pv_ps, GROUPS[gg - 4][0] + 1)
                        w = P * min(4, i + 1 - 4 * GROUPS[gg][1])
                        dve.tensor_copy(PTB[gg % 4][:, 0:w], ps[5][:, 0:w]).then_inc(pt_dve, 1)

            def normalise(n):
                i, h = ATT[n]
                dve.wait_ge(p_ready, n + 1)
                if i >= 4:
                    link(dve.tensor_tensor(RSM[:, n:n + 1], RSM[:, n:n + 1], RIN[:, n:n + 1], ALU.add))
                link(dve.reciprocal(RIN[:, n:n + 1], RSM[:, n:n + 1]))
                dve.wait_ge(pv_ps, n + 1)
                dve.tensor_scalar(YA[:, i, h * VD:(h + 1) * VD], ps[6 + n % 2][:, 0:VD], RIN[:, n:n + 1], None, ALU.mult).then_inc(pv_sb, 1)

            N = len(ATT)
            row_max(0)
            for n in range(N):
                if n + 1 < N:
                    row_max(n + 1)
                probs_evac(n)
                if n >= 1:
                    normalise(n - 1)
            normalise(N - 1)

            dve.wait_ge(ya_rstd, 1)
            dve.wait_ge(g2_in, 16)

            def ya_norm(i):
                dve.scalar_tensor_tensor(YA[:, i, :], YA[:, i, :], ST2[:, i:i + 1], GMLA[:, :], ALU.mult, ALU.mult).then_inc(ya_ready, 1)

            def residual(i):
                dve.wait_ge(o_ps, i + 1)
                dve.wait_ge(xr_in[i % 2], 16 * (i // 2 + 1))
                for b in range(2):
                    s = slice(b * 512, (b + 1) * 512)
                    ins = dve.tensor_tensor(X2[:, i, s], ps[2 * (i % 2) + b][:, :], XR[i % 2][:, s], ALU.add)
                ins.then_inc(x2_ready, 1)
                dve.wait_ge(x2_ready, i + 1)

            def norm2(i):
                dve.wait_ge(x2_rstd, i + 1)
                if i >= 2:
                    dve.wait_ge(x2n_out[i % 2], 16 * (i // 2))
                    dve.wait_ge(x2nt_ps, 2 * (i - 1))
                dve.scalar_tensor_tensor(X2N[i % 2], X2[:, i, :], ST2[:, NT + i:NT + i + 1], G2B, ALU.mult, ALU.mult).then_inc(x2n_ready, 1)

            def router_evac(i):
                dve.wait_ge(x2nt_ps, 2 * i + 2)
                if i >= 2:
                    dve.wait_ge(r_ps, i - 1)
                dve.tensor_copy(X2NT[i % 2][:, 4:8, :], ps[6][:, :].rearrange("p (k n) -> p k n", k=4)).then_inc(x2nt_dve, 1)
                dve.wait_ge(r_ps, i + 1)
                dve.tensor_tensor(LG[:, i * 36:(i + 1) * 36], ps[7][:, 0:36], BRT[:, :], ALU.add).then_inc(r_sb, 1)

            for i in range(NT):
                ya_norm(i)
            for i in range(NT):
                residual(i)
                norm2(i)
                if i >= 1:
                    router_evac(i - 1)
            router_evac(NT - 1)
            dve.wait_ge(r_sb, NT)

            dve.wait_ge(iota_set, 1)
            lg = LG[:, :].rearrange("p (i n) -> p i n", i=NT)
            gl = lg[:, :, 0:NG]
            el = lg[:, :, NG:].rearrange("p i (g j) -> p i g j", g=NG)

            def rb(a, n):
                return RB[:, a * NT:(a + n) * NT].rearrange("p (i n) -> p i n", i=NT)

            gmax, gd, gex = rb(0, 1), rb(4, 4), rb(8, 4)
            big = [RA[:, q * NT * NE:(q + 1) * NT * NE] for q in range(6)]
            rev4 = IOT[:, 0:NG]
            rev8 = IOT[:, 4:4 + EPG]

            def first_max(dst, vals, n, rev, m, key):
                link(dve.tensor_tensor(key, vals, m.broadcast_to([P, NT, n]), ALU.is_equal))
                link(dve.tensor_tensor(key, key, rev.unsqueeze(1).broadcast_to([P, NT, n]), ALU.mult))
                link(dve.tensor_reduce(rb(15, 1), key, AX.X, ALU.max))
                link(dve.tensor_tensor(dst, key, rb(15, 1).broadcast_to([P, NT, n]), ALU.is_equal))

            link(dve.tensor_reduce(gmax, gl, AX.X, ALU.max))
            link(dve.tensor_tensor(gd, gl, gmax.broadcast_to([P, NT, NG]), ALU.subtract))
            dve.nop().then_inc(rt_a, 1)
            ohg = rb(16, 4)
            first_max(ohg, gl, NG, rev4, gmax, rb(20, 4))
            prod = big[5].rearrange("p (i g j) -> p i g j", i=NT, g=NG)
            sel = big[4][:, 0:NT * EPG].rearrange("p (i j) -> p i j", i=NT)
            for g in range(NG):
                ins = dve.tensor_tensor(prod[:, :, g, :], el[:, :, g, :], ohg[:, :, g:g + 1].broadcast_to([P, NT, EPG]), ALU.mult)
            link(ins)
            link(dve.tensor_tensor(sel, prod[:, :, 0, :], prod[:, :, 1, :], ALU.add))
            link(dve.tensor_tensor(sel, sel, prod[:, :, 2, :], ALU.add))
            link(dve.tensor_tensor(sel, sel, prod[:, :, 3, :], ALU.add))
            e8 = [big[4][:, (1 + q) * NT * EPG:(2 + q) * NT * EPG].rearrange("p (i j) -> p i j", i=NT) for q in range(3)]
            m1, m2 = rb(1, 1), rb(2, 1)
            link(dve.tensor_reduce(m1, sel, AX.X, ALU.max))
            first_max(e8[0], sel, EPG, rev8, m1, e8[2])
            link(dve.scalar_tensor_tensor(sel, e8[0], -BIG, sel, ALU.mult, ALU.add))
            link(dve.tensor_reduce(m2, sel, AX.X, ALU.max))
            first_max(e8[1], sel, EPG, rev8, m2, e8[2])
            link(dve.tensor_tensor(rb(12, 1), m2, m1, ALU.subtract))
            dve.nop().then_inc(rt_a, 1)
            oh = [big[1], big[2]]
            for q in range(2):
                ohq = oh[q].rearrange("p (i g j) -> p i g j", i=NT, g=NG)
                for g in range(NG):
                    ins = dve.tensor_tensor(ohq[:, :, g, :], e8[q], ohg[:, :, g:g + 1].broadcast_to([P, NT, EPG]), ALU.mult)
            link(ins)
            dve.tensor_tensor(big[0], oh[0], oh[1], ALU.add).then_inc(mask_ready, 1)
            dve.wait_ge(rt_b, 2)
            link(dve.tensor_reduce(rb(3, 1), gex, AX.X, ALU.add))
            link(dve.tensor_scalar(rb(14, 1), rb(13, 1), 1.0, None, ALU.add))
            link(dve.tensor_tensor(rb(14, 1), rb(14, 1), rb(3, 1), ALU.mult))
            w0, w1 = WTS[:, 0:NT], WTS[:, NT:2 * NT]
            link(dve.reciprocal(w0, RB[:, 14 * NT:15 * NT]))
            link(dve.tensor_tensor(w1, w0, RB[:, 13 * NT:14 * NT], ALU.mult))
            dve.wait_ge(pos_ps, 1)
            cnt = lambda q: CNT[:, q * NE:(q + 1) * NE]
            link(dve.tensor_copy(cnt(0), ps[1][:, 0:NE]))
            link(dve.tensor_scalar(cnt(1), cnt(0), float(CAP), None, ALU.is_gt))
            for j in range(2, S // CAP):
                link(dve.scalar_tensor_tensor(cnt(1), cnt(0), float(CAP * j), cnt(1), ALU.is_gt, ALU.add))
            link(dve.memset(cnt(4), 1.0))
            link(dve.tensor_tensor_scan(cnt(2), cnt(4), cnt(1), 0.0, ALU.mult, ALU.add))
            link(dve.tensor_tensor(cnt(3), cnt(2), cnt(1), ALU.subtract))
            link(dve.scalar_tensor_tensor(cnt(3), cnt(3), float(NMAIN - 1), IOT[:, NE:2 * NE], ALU.add, ALU.subtract))
            link(dve.tensor_scalar(cnt(3), cnt(3), float(CAP), None, ALU.mult))
            link(dve.tensor_scalar(cnt(5), IOT[:, NE:2 * NE], float(CAP), None, ALU.mult))
            link(dve.tensor_copy(big[3], ps[0][:, 0:NT * NE]))
            b3 = big[3].rearrange("p (i e) -> p i e", i=NT)
            b4 = big[4].rearrange("p (i e) -> p i e", i=NT)
            link(dve.tensor_scalar(big[4], big[3], float(CAP), None, ALU.is_ge))
            link(dve.tensor_tensor(b4, b4, cnt(3).unsqueeze(1).broadcast_to([P, NT, NE]), ALU.mult))
            link(dve.tensor_tensor(big[3], big[3], big[4], ALU.add))
            link(dve.tensor_tensor(b3, b3, cnt(5).unsqueeze(1).broadcast_to([P, NT, NE]), ALU.add))
            for q in range(2):
                link(dve.tensor_tensor(big[5], oh[q], big[3], ALU.mult))
                link(dve.tensor_reduce(SLOTF[:, q * NT:(q + 1) * NT], big[5].rearrange("p (i e) -> p i e", i=NT), AX.X, ALU.add))
            for b in range(NOVER):
                link(dve.tensor_scalar(cnt(6)[0:1, :], cnt(2)[0:1, :], float(b), None, ALU.is_le))
                link(dve.tensor_reduce(cnt(7)[0:1, b:b + 1], cnt(6)[0:1, :], AX.X, ALU.add))
            link(dve.tensor_scalar(cnt(7)[0:1, 0:NOVER], cnt(7)[0:1, 0:NOVER], float(NE - 1), None, ALU.min))
            dve.tensor_copy(OVE[0:1, 0:NOVER], cnt(7)[0:1, 0:NOVER])
            link(dve.tensor_copy(OVE[0:1, NOVER:NOVER + 1], cnt(2)[0:1, NE - 1:NE]))
            dve.tensor_copy(SLOT[:, :], SLOTF[:, :]).then_inc(slot_ready, 1)
            dve.wait_ge(ids_ps, 1)
            dve.tensor_copy(IDX[:, :], ps[2][:, 0:NBLK]).then_inc(idx_ready, 1)

            def rows_evac(u, done):
                dve.wait_ge(xgt_ps, done)
                dve.tensor_copy(XGT[u][:, 4:8, :], ps[1][:, :].rearrange("p (k n) -> p k n", k=4)).then_inc(xgt_dve, 1)

            def swiglu(u, ups, done):
                dve.wait_ge(gu_ps, ups)
                dve.wait_ge(sg_ready, done)
                dve.tensor_tensor(HT[u].rearrange("p k n -> p (k n)"), SG, ps[3 + 2 * u][:, 0:2 * P], ALU.mult).then_inc(h_ready, 1)

            def y_evac(done):
                dve.wait_ge(y_ps, done)
                dve.tensor_copy(YB[1], ps[7][:, :]).then_inc(y_dve, 1)

            dve.sem_inc(xgt_dve, 1)
            dve.sem_inc(y_dve, 1)
            dve.sem_inc(h_ready, 1)
            rows_evac(0, 2)
            with dve.Fori(0, NMAIN // NW) as it:
                for j in range(NW):
                    u = j % 2
                    swiglu(u, it * (2 * NW) + (2 * j + 2), it * NW + (j + 1))
                    rows_evac(1 - u, it * (2 * NW) + (2 * j + 4))
                    dve.wait_ge(y_out[1], it * (16 * NW) + 16 * (j + 1))
                    y_evac(it * NW + (j + 1))
            nover = dve.value_load(OVE[0:1, NOVER:NOVER + 1], min_val=0, max_val=NOVER)
            with dve.Fori(0, NOVER) as b:
                with dve.If(b < nover):
                    rows_evac(0, b * 2 + (2 * NMAIN + 4))
                    swiglu(0, b * 2 + (2 * NMAIN + 2), b + (NMAIN + 1))
                    dve.wait_ge(y_out[1], b * 16 + 16 * (NMAIN + 1))
                    y_evac(b + (NMAIN + 1))
                with dve.Else():
                    dve.nop()

            def combine(i):
                dve.wait_ge(yg_in[i % 2], 32 * (i // 2 + 1))
                link(dve.scalar_tensor_tensor(X2[:, i, :], YG[i % 2][0], WTS[:, i:i + 1], X2[:, i, :], ALU.mult, ALU.add))
                dve.scalar_tensor_tensor(X2[:, i, :], YG[i % 2][1], WTS[:, NT + i:NT + i + 1], X2[:, i, :], ALU.mult, ALU.add).then_inc(f_sum, 1)

            def final_norm(i):
                dve.wait_ge(f_rstd, i + 1)
                if i >= 2:
                    dve.wait_ge(out_done[i % 2], 16 * (i // 2))
                dve.scalar_tensor_tensor(OUT[i % 2], X2[:, i, :], ST2[:, i:i + 1], GFB, ALU.mult, ALU.mult).then_inc(f_ready, 1)

            combine(0)
            dve.wait_ge(gf_in, 16)
            for i in range(NT):
                if i + 1 < NT:
                    combine(i + 1)
                final_norm(i)

        @block.gpsimd
        def _(pool):
            link = chained(pool, pool_chain)
            sel = SEL[:, :].rearrange("p (h n) -> p h n", h=MLH)
            pool.memset(BD[:, :], 0.0)
            pool.memset(ONES[:, :], 1.0)
            pool.memset(KRP[0], 0.0)
            pool.memset(KRP[1], 0.0)
            pool.memset(IDENT[:, :], 0.0)
            pool.memset(CMASK[:, :], 0.0)
            pool.memset(TMASK[:, :], 0.0)
            pool.memset(SEL[:, :], 0.0)
            link(pool.memset(TRI[:, :], 0.0))
            pool.affine_select(out=IDENT[:, :], in_=IDENT[:, :], compare_op=ALU.not_equal, fill=1.0, base=0,
                               pattern=[[-1, P]], channel_multiplier=1).then_inc(masks_set, 1)
            pool.affine_select(out=CMASK[:, :], in_=CMASK[:, :], compare_op=ALU.is_ge, fill=-BIG, base=0,
                               pattern=[[-1, P]], channel_multiplier=1).then_inc(masks_set, 1)
            pool.affine_select(out=TMASK[:, :], in_=TMASK[:, :], compare_op=ALU.is_ge, fill=-BIG, base=0,
                               pattern=[[1, P]], channel_multiplier=-1).then_inc(masks_set, 1)
            pool.affine_select(out=TRI[:, :], in_=TRI[:, :], compare_op=ALU.is_ge, fill=1.0, base=0,
                               pattern=[[-1, P]], channel_multiplier=1).then_inc(masks_set, 1)
            pool.affine_select(out=sel, in_=sel, compare_op=ALU.not_equal, fill=1.0, base=0,
                               pattern=[[-1, MLH], [0, P]], channel_multiplier=1).then_inc(masks_set, 1)
            link(pool.memset(SPT[:, :], 0.0))
            link(pool.iota(IOT[:, 0:4], pattern=[[-1, 4]], base=NG, channel_multiplier=0, allow_small_or_imprecise_dtypes=True))
            link(pool.iota(IOT[:, 4:12], pattern=[[-1, 8]], base=EPG, channel_multiplier=0, allow_small_or_imprecise_dtypes=True))
            link(pool.iota(IOT[:, NE:2 * NE], pattern=[[1, NE]], base=0, channel_multiplier=0, allow_small_or_imprecise_dtypes=True))
            link(pool.iota(TOK[:, :], pattern=[[P, NT]], base=0, channel_multiplier=1, allow_small_or_imprecise_dtypes=True))
            link(pool.memset(IDR[:, :], float(S)))
            pool.nop().then_inc(iota_set, 1)
            pool.dma_start(ids_d.rearrange("(b n) o -> b (n o)", b=NBLK), IDR[:, :]).then_inc(ids_init, 16)
            pool.memset(ZERO, 0.0).then_inc(zero_set, 1)
            pool.wait_ge(zero_set, 1)
            for b in range(NMAIN, NBLK):
                pool.dma_start(y_d[b * CAP:(b + 1) * CAP, :].rearrange("p (q n) -> p q n", q=2),
                               ZERO.unsqueeze(1).broadcast_to([P, 2, 512])).then_inc(zero_out, 16)

            pool.wait_ge(const_in, 16 * NC_)
            for i in range(NT):
                pool.wait_ge(proj_act, job("T", i, 2) + 1)
                if i >= 2:
                    pool.wait_ge(latt_ps, i - 1)
                t1, t2 = CQR[i % 2][:, QL + KVL:QL + KVL + 16], CQR[i % 2][:, QL + KVL + 16:]
                cs, sn = COS[:, i * 16:(i + 1) * 16], SIN[:, i * 16:(i + 1) * 16]
                a, b, c, d = (RTMP[:, q * 16:(q + 1) * 16] for q in range(4))
                pool.tensor_tensor(a, t1, cs, ALU.mult)
                pool.tensor_tensor(b, t2, sn, ALU.mult)
                pool.tensor_tensor(c, t1, sn, ALU.mult)
                link(pool.tensor_tensor(d, t2, cs, ALU.mult))
                pool.tensor_tensor(KRP[i % 2][:, NOPE:NOPE + 16], a, b, ALU.subtract)
                pool.tensor_tensor(KRP[i % 2][:, NOPE + 16:QK], c, d, ALU.add).then_inc(krp_ready, 1)
                pool.wait_ge(krp_ready, i + 1)
            pool.wait_ge(proj_ps, NPROJ)
            pool.memset(ROWS4, 0.0).then_inc(rs_set, 1)
            link(pool.memset(ROW_RS, 1.0))
            pool.memset(ROW_RS.rearrange("p (c n) -> p c n", c=NT)[:, :, 0:1], 0.0).then_inc(rs_set, 2)
            pool.wait_ge(proj_act, NPROJ)
            for f in range(2):
                XC, R, IV, T, D1 = LT[f]
                g = RG[:, f, :]
                link(pool.tensor_tensor(T, g, g, ALU.mult))
                link(pool.tensor_scalar(T, T, GELU_A, 1.0, ALU.mult, ALU.add))
                pool.tensor_tensor(T, T, g, ALU.mult).then_inc(gelu_arg, 1)
            for f in range(2):
                pool.wait_ge(gelu_sig, f + 1)
                pool.tensor_tensor(RG[:, f, :], RG[:, f, :], LT[f][4], ALU.mult).then_inc(gelu_done, 1)
            pool.wait_ge(cols_sb, 3)
            col = COL[:, :].rearrange("p (i k h) -> p i k h", i=NT, k=4)
            for c in range(NT):
                if c >= 1:
                    pool.wait_ge(upd_ps, c)
                pool.tensor_tensor(KSB.rearrange("p (h n) -> p h n", h=MLH),
                                   KTOK[:, c, :].rearrange("p (h n) -> p h n", h=MLH),
                                   col[:, c, 2, :].unsqueeze(2).broadcast_to([P, MLH, MLD]), ALU.mult).then_inc(ks_ready, 1)
            pool.wait_ge(latt_sb, NT)
            pool.wait_ge(yr_done, 1)
            pool.tensor_copy(KT[NOPE:QK, :, :], KPT[NOPE:QK, :].unsqueeze(1).broadcast_to([ROPE, H, S])).then_inc(kr_sb, 1)
            pool.wait_ge(kr_sb, 1)
            for i in range(NT):
                pool.wait_ge(q_sb, i + 1)
                q = QTOK[i % 2]
                t1, t2 = q[:, :, NOPE:NOPE + 16], q[:, :, NOPE + 16:QK]
                cs = COS[:, i * 16:(i + 1) * 16].unsqueeze(1).broadcast_to([P, H, 16])
                sn = SIN[:, i * 16:(i + 1) * 16].unsqueeze(1).broadcast_to([P, H, 16])
                a, b, c, d = (RTMP[:, w * 128:(w + 1) * 128].rearrange("p (h n) -> p h n", h=H) for w in range(4))
                pool.tensor_tensor(a, t1, cs, ALU.mult)
                pool.tensor_tensor(b, t2, sn, ALU.mult)
                pool.tensor_tensor(c, t1, sn, ALU.mult)
                link(pool.tensor_tensor(d, t2, cs, ALU.mult))
                pool.tensor_tensor(t1, a, b, ALU.subtract)
                pool.tensor_tensor(t2, c, d, ALU.add).then_inc(q_rope, 1)
                pool.wait_ge(q_rope, i + 1)
            pool.wait_ge(ids_init, 16)
            pool.wait_ge(slot_ready, 1)
            for q in range(2):
                for i in range(NT):
                    pool.indirect_dma_start(ids_d, bass.IndirectOffsetOnAxis(ap=SLOT[:, q * NT + i:q * NT + i + 1], axis=0),
                                            TOK[:, i:i + 1], None).then_inc(ids_out, 16)
            pool.wait_ge(ids_out, 16 * 2 * NT)
            pool.dma_start(IDR[:, :], ids_d.rearrange("(b n) o -> b (n o)", b=NBLK)).then_inc(ids_in, 16)
            pool.wait_ge(yr_done, 1)
            pool.wait_ge(o_ps, NT)
            pool.memset(XG[0], 0.0).then_inc(xg_set, 1)
            pool.memset(XG[1], 0.0).then_inc(xg_set, 1)
            pool.wait_ge(xg_set, 2)
            pool.wait_ge(idx_ready, 1)
            pool.wait_ge(x2n_out[0], 16 * (NT // 2))
            pool.wait_ge(x2n_out[1], 16 * (NT // 2))

            def stand():
                pool.sem_inc(pool_waits, 1)

            def gather(u, col, done):
                pool.tensor_copy(IDXC[u][:, :], col).then_inc(list_ready, 1)
                pool.wait_ge(list_ready, done)
                stand()
                col = IDXC[u][:, :]
                pool.indirect_dma_start(XG[u], None, x2n_d, bass.IndirectOffsetOnAxis(ap=col, axis=0),
                                        bounds_check=S - 1, oob_is_err=False).then_inc(xg_in[u], 16)

            gather(0, IDX[:, 0:1], 1)
            gather(1, IDX[:, 1:2], 2)
            with pool.Fori(0, NMAIN // NW) as it:
                for j in range(NW):
                    u = j % 2
                    pool.wait_ge(xgt_ps, it * (2 * NW) + (2 * j + 2))
                    stand()
                    gather(u, IDX[:, bass.ds(it * NW + (j + 2), 1)], it * NW + (j + 3))
            nover = pool.value_load(OVE[0:1, NOVER:NOVER + 1], min_val=0, max_val=NOVER)
            with pool.Fori(0, NOVER) as b:
                with pool.If(b < nover):
                    pool.wait_ge(xgt_ps, b * 2 + (2 * NMAIN + 2))
                    stand()
                    gather(0, IDX[:, bass.ds(b + NMAIN, 1)], b + (NMAIN + 3))
                with pool.Else():
                    pool.nop()
            total = pool.snap(nover * 16 + 16 * (NMAIN + 1))
            pool.wait_ge(y_out[0], total)
            pool.wait_ge(y_out[1], total)
            stand()
            for i in range(NT):
                if i >= 2:
                    pool.wait_ge(f_sum, i - 1)
                for q in range(2):
                    pool.indirect_dma_start(YG[i % 2][q], None, y_d, bass.IndirectOffsetOnAxis(ap=SLOT[:, q * NT + i:q * NT + i + 1], axis=0)).then_inc(yg_in[i % 2], 16)


NAMES = ["x", "norm1_g", "w_in", "ml_i_bias", "ml_f_bias", "ml_norm_g", "conv_w", "conv_b", "lru_w_r", "lru_b_r",
         "lru_w_i", "lru_b_i", "lru_lambda", "lru_norm_g", "q_norm_g", "w_uq", "kv_norm_g", "w_ukv", "mla_norm_g",
         "w_out", "norm2_g", "w_group", "b_group", "w_expert", "b_expert", "w_gate", "w_up", "w_down", "final_norm_g"]


def kernel(**inputs):
    import concourse.bacc as bacc
    from concourse.bass_utils import run_bass_kernel_spmd

    nc = bacc.Bacc("TRN2", target_bir_lowering=False, num_devices=1)
    inv = (1.0 / (np.float32(10000.0) ** (np.arange(0, ROPE, 2, dtype=np.float32) / np.float32(ROPE)))).astype(np.float32)
    ang = np.arange(S, dtype=np.float32)[:, None] * inv[None, :]
    arrays = {"rope_cos": np.cos(ang), "rope_sin": np.sin(ang)}
    arrays.update({name: np.ascontiguousarray(inputs[name]) for name in NAMES})
    t = {name: nc.dram_tensor(f"in_{name}", a.shape, mybir.dt.from_np(a.dtype), kind="ExternalInput").ap()
         for name, a in arrays.items()}
    t["out"] = nc.dram_tensor("out_0", (1, S, D), F32, kind="ExternalOutput").ap()
    build(nc, t)
    r = run_bass_kernel_spmd(nc, [{f"in_{name}": a for name, a in arrays.items()}], core_ids=[0])
    return r.results[0]["out_0"]
```

```python
from contextlib import ExitStack

import numpy as np
import concourse.bass as bass
from concourse import mybir

F32 = mybir.dt.float32
BF16 = mybir.dt.bfloat16
I32 = mybir.dt.int32
ALU = mybir.AluOpType
ACT = mybir.ActivationFunctionType
AX = mybir.AxisListType

P = 128
D = 1024
S = 1024
NT = S // P
KD = D // P
MLH, MLD = 4, 64
MLW = MLH * MLD
VA = MLD + 1
LRU = 256
CONV = 4
H, NOPE, ROPE, VD = 8, 64, 32, 64
QK = NOPE + ROPE
QL, KVL = 256, 128
NG, EPG = 4, 8
NE = NG * EPG
DE = 256
EPS = 1e-6
BIG = 1.0e30
SCALE = float(QK) ** -0.5
LRU_C = 8.0

C_MQ, C_MK, C_MV, C_MO, C_MI = 0, 256, 512, 768, 1024
C_RX, C_RG, C_CQ = 1032, 1288, 1544
N_IN = 1960
N_LAT = QL + KVL + ROPE

CAP = P
NMAIN = NE
NOVER = 2 * S // P - 1
NBLK = NMAIN + NOVER
NW = 4

GELU_S = 1.5957691216057308
GELU_A = 0.044715


def build(nc, t):
    ctx = ExitStack()
    with ctx:
        def sb(name, cols, dt=F32, parts=P):
            return ctx.enter_context(nc.sbuf_tensor(name, [parts, cols], dt))

        def sem(name):
            return ctx.enter_context(nc.semaphore(name))

        mem = sb("mem", 45696)

        def at(a, n, parts=P, p0=0):
            return mem[p0:p0 + parts, a:a + n]

        W_IN = at(0, KD * N_IN).rearrange("p (k n) -> p k n", k=KD)
        HNT = at(15680, 8192).rearrange("p (k n) -> p k n", k=KD)
        R2 = 24576
        KTOK = at(R2, 2048).rearrange("p (i n) -> p i n", i=NT)
        VAUG = at(R2 + 2048, 2080).rearrange("p (i h n) -> p i h n", i=NT, h=MLH)
        OTOK = at(R2 + 4128, 2048).rearrange("p (i n) -> p i n", i=NT)
        MQT = at(R2 + 6176, 2048).rearrange("p (m n) -> p m n", m=2)
        R3 = R2 + 8224
        CQT = at(R3, 2048).rearrange("p (m n) -> p m n", m=2)
        CKVT = at(R3 + 2048, 1024)
        KPT = at(R3 + 3072, 1024)
        R4 = R3 + 4096
        RXP = at(R4, 2 * (S + 3)).rearrange("p (m n) -> p m n", m=2)
        RG = at(R4 + 2054, 2048).rearrange("p (m n) -> p m n", m=2)
        R5 = R4 + 4102
        XB = [at(R5 + 1024 * j, 1024) for j in range(3)]
        CQR = [at(R5 + 3072 + N_LAT * j, N_LAT) for j in range(2)]
        KRP = [at(R5 + 3072 + 2 * N_LAT + QK * j, QK) for j in range(2)]
        ZERO = at(R5 + 4186, 512)
        ROW_F, ROW_I, ROW_LF, ROW_B, ROW_M, ROW_T, ROW_RS = (at(1024 * j, 1024, MLH) for j in range(7))
        LT = [[at(R5 + 1024 * f, 1024)] + [at(8192 + 5120 * f + 1024 * j, 1024) for j in range(4)] for f in range(2)]
        ROWS4 = at(17408, 1024)
        ROW_A = at(12288, 1024, MLH)
        ROW_T2 = at(19456, 1024, MLH)
        KTM = at(20480, 2048).rearrange("p (m n) -> p m n", m=2)
        DSB, WSB, PWB = ([at(8192 + 1024 * q + 512 * j, MLH * P) for j in range(2)] for q in range(3))
        KSB = [at(11264 + 256 * j, MLW) for j in range(2)]
        INT, NUM = ([at(13312 + 520 * q + 260 * j, MLH * VA) for j in range(2)] for q in range(2))
        SQ = at(8192, 2048)
        KT = at(0, 8192).rearrange("p (h n) -> p h n", h=H)
        QT = at(8192, 8192).rearrange("p (i h n) -> p i h n", i=NT, h=H)
        V = at(16384, 4096).rearrange("p (i h n) -> p i h n", i=NT, h=H)
        YA = at(20480, 4096).rearrange("p (i n) -> p i n", i=NT)
        W_UQ = at(R5, 1536).rearrange("p (k n) -> p k n", k=2)
        W_UKV = at(22528, 1024).rearrange("p (h n) -> p h n", h=H)
        YM = at(R5 + 2560, 2048).rearrange("p (m n) -> p m n", m=2)
        QTOK = [at(R4 + 2054 + 768 * j, 768).rearrange("p (h n) -> p h n", h=H) for j in range(2)]
        PB = [at(R3 + 1024 * j, 1024) for j in range(2)]
        PTB = [at(R3 + 2048 + 512 * j, 512) for j in range(4)]
        W_OUT = at(R2, 8192).rearrange("p (k n) -> p k n", k=KD)
        X2 = at(8192, 8192).rearrange("p (i n) -> p i n", i=NT)
        XR = [at(R4 + 2054 + 1024 * j, 1024) for j in range(2)]
        YAT = [at(R5 + 512 * j, 512) for j in range(2)]
        G2B = at(R5 + 1024, 1024)
        NX = 4
        X2N = [at(1024 * j, 1024) for j in range(NX)]
        X2NT = [at(4096 + 1024 * j, 1024).rearrange("p (k n) -> p k n", k=KD) for j in range(2)]
        WOFF = (0, 16384, R2, R3)
        WGU = [at(o, 4096).rearrange("p (g k n) -> p g k n", g=2, k=KD) for o in WOFF]
        WDN = [at(o + 4096, 2048).rearrange("p (k n) -> p k n", k=2) for o in WOFF]
        E5 = R3 + 6144
        XG = [at(E5 + 1024 * j, 1024) for j in range(2)]
        XGT = [at(E5 + 2048 + 1024 * j, 1024).rearrange("p (k n) -> p k n", k=KD) for j in range(2)]
        SG = at(6144, 256)
        HT = [at(6400 + 256 * j, 256).rearrange("p (k n) -> p k n", k=2) for j in range(2)]
        YB = [at(6912 + 512 * j, 512) for j in range(2)]
        RA = at(E5 + 4096, 6 * NT * NE)
        NY = 4
        YG = [[at((0, 2048, 16384, 18432)[j] + 1024 * q, 1024) for q in range(2)] for j in range(NY)]
        OUT = [at(R2 + 1024 * j, 1024) for j in range(2)]
        GFB = at(R3, 1024)

        IDENT = sb("ident", P)
        ONES = sb("ones", P)
        CMASK = sb("cmask", P)
        TMASK = sb("tmask", P)
        TRI = sb("tri", P)
        SEL = sb("sel", MLH * P, parts=MLH)
        GB = sb("gb", D)
        COS = sb("cos", NT * 16)
        SIN = sb("sin", NT * 16)
        GQ = sb("gq", QL + KVL)
        GML = sb("gml", MLW)
        GMLA = sb("gmla", H * VD)
        GLRU = sb("glru", 2)
        CW = sb("cw", 2 * CONV)
        CB = sb("cb", 2)
        BR = sb("br", 2)
        BI = sb("bi", 2)
        LAM = sb("lam", 2)
        BGI = sb("bgi", 1, parts=MLH)
        BGF = sb("bgf", 1, parts=MLH)
        BD = sb("bd", 4 * P)
        WR = sb("wr", KD * 36)
        BRT = sb("brt", 36)
        EPSC = sb("epsc", 1)
        ONEC = sb("onec", 1)
        JUNK = sb("junk", D, BF16)
        ST1 = sb("st1", 2 * NT)
        ST2 = sb("st2", 4 * NT)
        GATES = sb("gates", NT * 8)
        RTMP = sb("rtmp", 4 * H * 16)
        SPT = sb("spt", 16)
        COL = sb("col", NT * 16)
        DEC = sb("dec", 8, parts=MLH)
        MPV = sb("mpv", 8, parts=MLH)
        DECB = sb("decb", MLH * NT)
        CST = sb("cst", 2 * VA)
        DEN = sb("den", MLH)
        MSS = sb("mss", 3 * NT * MLH)
        NMX = sb("nmx", 64)
        RSM = sb("rsm", 64)
        RIN = sb("rin", 64)
        LG = sb("lg", NT * 36)
        RB = sb("rb", 24 * NT)
        CNT = sb("cnt", 8 * NE)
        IOT = sb("iot", 4 * NE)
        SLOTF = sb("slotf", 2 * NT)
        SLOT = sb("slot", 2 * NT, I32)
        TOK = sb("tok", NT)
        WTS = sb("wts", 2 * NT)
        IDR = sb("idr", P, parts=NBLK)
        IDX = sb("idx", NBLK, I32)
        IDXC = [sb(f"idxc{j}", 1, I32) for j in range(2)]
        OVE = sb("ove", 32, I32, parts=1)

        ps = [ctx.enter_context(nc.psum_tensor(f"ps{b}", [P, 512], F32)) for b in range(8)]

        x2n_d = nc.dram_tensor("x2n_rows", [S, D], F32, kind="Internal").ap()
        ids_d = nc.dram_tensor("slot_ids", [NBLK * CAP, 1], F32, kind="Internal").ap()
        y_d = nc.dram_tensor("expert_rows", [NBLK * CAP, D], F32, kind="Internal").ap()

        x_d = t["x"].rearrange("b (i p) d -> (b i) p d", p=P)
        out_d = t["out"].rearrange("b (i p) d -> (b i) p d", p=P)

        act_chain, dve_chain, pool_chain = sem("act_chain"), sem("dve_chain"), sem("pool_chain")
        const_in, masks_set = sem("const_in"), sem("masks_set")
        x_in = [sem(f"x_in{j}") for j in range(3)]
        win_in = [sem(f"win_in{k}") for k in range(4)]
        g1_in = sem("g1_in")
        x_sq, x_rstd, hn_ready = sem("x_sq"), sem("x_rstd"), sem("hn_ready")
        hnt_ps, hnt_act, hnt_dve = sem("hnt_ps"), sem("hnt_act"), sem("hnt_dve")
        proj_ps, proj_act = sem("proj_ps"), sem("proj_act")
        lat_rstd, lat_ready, krp_ready = sem("lat_rstd"), sem("lat_ready"), sem("krp_ready")
        latt_ps, latt_sb = sem("latt_ps"), sem("latt_sb")
        gate_ps, gate_rows, lf_t, rows_pre, rows_done = (sem(n) for n in
                                                         ("gate_ps", "gate_rows", "lf_t", "rows_pre", "rows_done"))
        rs_set = sem("rs_set")
        cols_ps, cols_sb = sem("cols_ps"), sem("cols_sb")
        ktm_ps, ktm_sb = sem("ktm_ps"), sem("ktm_sb")
        lam_s, lam_done = sem("lam_s"), sem("lam_done")
        conv_done, lgate_ps, lgate_sb = sem("conv_done"), sem("lgate_ps"), sem("lgate_sb")
        gelu_arg, gelu_sig, gelu_done = sem("gelu_arg"), sem("gelu_sig"), sem("gelu_done")
        lru_a, lru_ratio, lru_root = sem("lru_a"), sem("lru_ratio"), sem("lru_root")
        yr_sq, yr_ps, yr_rstd, yr_done = sem("yr_sq"), sem("yr_ps"), sem("yr_rstd"), sem("yr_done")
        db_ps, d_ready, w_ready = sem("db_ps"), sem("d_ready"), sem("w_ready")
        st_ps, pw_ready, ks_ready = sem("st_ps"), sem("pw_ready"), sem("ks_ready")
        inter_ps, inter_sb, upd_ps, state_ready = sem("inter_ps"), sem("inter_sb"), sem("upd_ps"), sem("state_ready")
        intra_ps, num_ready, mh_sq, mh_ss, mh_rstd, ymt_ready, h_done = (sem(n) for n in (
            "intra_ps", "num_ready", "mh_sq", "mh_ss", "mh_rstd", "ymt_ready", "h_done"))
        ym_ps, ym_sb = sem("ym_ps"), sem("ym_sb")
        wu_in, wuq_in, kv_ps, kv_sb, kr_sb = sem("wu_in"), sem("wuq_in"), sem("kv_ps"), sem("kv_sb"), sem("kr_sb")
        q_ps, q_sb, q_rope, qt_ps, qt_act, qt_dve = (sem(n) for n in ("q_ps", "q_sb", "q_rope", "qt_ps", "qt_act", "qt_dve"))
        s_ps, s_max, p_ready = sem("s_ps"), sem("s_max"), sem("p_ready")
        pt_ps, pt_act, pt_dve, pv_ps, pv_sb = sem("pt_ps"), sem("pt_act"), sem("pt_dve"), sem("pv_ps"), sem("pv_sb")
        wout_in, g2_in = sem("wout_in"), sem("g2_in")
        xr_in = [sem(f"xr_in{j}") for j in range(2)]
        ya_sq, ya_rstd, ya_ready, yat_ps, yat_sb = (sem(n) for n in ("ya_sq", "ya_rstd", "ya_ready", "yat_ps", "yat_sb"))
        o_ps, x2_half, x2_ready, x2_rstd, x2n_ready = sem("o_ps"), sem("x2_half"), sem("x2_ready"), sem("x2_rstd"), sem("x2n_ready")
        x2n_out = [sem(f"x2n_out{j}") for j in range(NX)]
        x2nt_ps, x2nt_act, x2nt_dve, r_ps, r_sb = (sem(n) for n in ("x2nt_ps", "x2nt_act", "x2nt_dve", "r_ps", "r_sb"))
        rt_a, rt_b, mask_ready, pos_ps, slot_ready = (sem(n) for n in ("rt_a", "rt_b", "mask_ready", "pos_ps", "slot_ready"))
        iota_set, ids_init, ids_out, ids_in, ids_ps, idx_ready = (sem(n) for n in
                                                                  ("iota_set", "ids_init", "ids_out", "ids_in", "ids_ps", "idx_ready"))
        w_in_ = [sem(f"wexp_in{j}") for j in range(NW)]
        pool_waits, zero_set, zero_out = sem("pool_waits"), sem("zero_set"), sem("zero_out")
        list_ready = sem("list_ready")
        xg_set = sem("xg_set")
        xg_in = [sem(f"xg_in{j}") for j in range(2)]
        xgt_ps, xgt_act, xgt_dve = sem("xgt_ps"), sem("xgt_act"), sem("xgt_dve")
        gu_ps, sg_ready, h_ready = sem("gu_ps"), sem("sg_ready"), sem("h_ready")
        y_ps, y_act, y_dve = sem("y_ps"), sem("y_act"), sem("y_dve")
        y_out = [sem(f"y_out{j}") for j in range(2)]
        yg_in = [sem(f"yg_in{j}") for j in range(NY)]
        gf_in = sem("gf_in")
        f_sum, f_rstd, f_ready = sem("f_sum"), sem("f_rstd"), sem("f_ready")
        out_done = [sem(f"out_done{j}") for j in range(2)]

        STEPS, PROJ = [], []

        def step(kind, a, b=0):
            STEPS.append((kind, a, b))
            if kind in "TF":
                PROJ.append((kind, a, b))

        step("turn", 0)
        step("turn", 1)
        for i in range(4):
            step("T", i, 0)
            if i < 2:
                step("turn", i + 2)
        for i in range(4):
            step("T", i, 1)
            step("T", i, 2)
            if i >= 1:
                step("latent", i - 1)
        step("turn", 4)
        for m in range(6):
            step("F", 0, m)
            if m == 0:
                step("latent", 3)
        for i in range(4, NT):
            if i + 1 < NT:
                step("turn", i + 1)
            for b in range(3):
                step("T", i, b)
            if i >= 5:
                step("latent", i - 1)
        step("F", 1, 2)
        step("latent", NT - 1)
        for m in (3, 4, 5, 0, 1):
            step("F", 1, m)
        NPROJ = len(PROJ)
        W_PIECES = (((C_MK, 512),), ((C_MO, MLW + 8),), ((C_CQ, N_LAT),), ((C_MQ, 256), (C_RX, 512)))
        T_COLS = ((C_MK, 512), (C_MO, MLW + 8), (C_CQ, N_LAT))
        F_COLS = (C_MQ, C_MQ + P, C_RX, C_RX + P, C_RG, C_RG + P)

        def job(kind, a, b):
            return PROJ.index((kind, a, b))

        NC_ = 27

        def chained(eng, chain):
            count = [0]

            def link(ins):
                count[0] += 1
                ins.then_inc(chain, 1)
                eng.wait_ge(chain, count[0])
            return link

        ORDER = list(reversed(range(NT)))
        ATT = [(i, h) for i in ORDER for h in range(H)]
        GROUPS = [(n, g) for n, (i, h) in enumerate(ATT) for g in range((i + 4) // 4)]
        G0 = [sum(1 for (m, _) in GROUPS if m < n) for n in range(len(ATT) + 1)]
        N = len(ATT)
        DUE = {"sumsq": 1, "scale": 2, "turn": 3, "half0": (4, 5, 6), "add0": 6, "half1": (7, 8, 9), "add1": 9, "sumsq2": 10}
        LAST = N + 11

        def due(n):
            return [(t, n - H * (t + 1)) for t in range(NT) if 0 < n - H * (t + 1) <= 10]

        block = ctx.enter_context(nc.Block())

        @block.sync
        def _(sp):
            def load_x(i):
                if i >= 3:
                    sp.wait_ge(hnt_ps, 2 * (i - 2))
                sp.dma_start(XB[i % 3], x_d[i]).then_inc(x_in[i % 3], 16)

            def load_w(g):
                for c0, w in W_PIECES[g]:
                    sp.dma_start(W_IN[:, :, c0:c0 + w], t["w_in"][0].rearrange("(k p) n -> p k n", p=P)[:, :, c0:c0 + w]).then_inc(win_in[g], 16)

            load_x(0)
            sp.dma_start(GB[:, :], t["norm1_g"].rearrange("l d -> (l d)").partition_broadcast(P)).then_inc(g1_in, 16)
            load_w(0)
            load_x(1)
            load_x(2)
            load_w(1)
            load_x(3)
            load_w(2)
            load_w(3)
            for i in range(4, NT):
                load_x(i)
            sp.wait_ge(zero_set, 1)
            for b in range(NMAIN, NBLK):
                sp.dma_start(y_d[b * CAP:(b + 1) * CAP, :].rearrange("p (q n) -> p q n", q=2),
                             ZERO.unsqueeze(1).broadcast_to([P, 2, 512])).then_inc(zero_out, 16)
            sp.wait_ge(proj_ps, NPROJ)
            sp.dma_start(W_UKV, t["w_ukv"][0].rearrange("p (h n) -> p h n", h=H)).then_inc(wu_in, 16)
            sp.wait_ge(yr_sq, 2)
            sp.dma_start(W_UQ, t["w_uq"][0].rearrange("(k p) n -> p k n", p=P)).then_inc(wuq_in, 16)
            sp.wait_ge(upd_ps, NT)
            sp.wait_ge(ym_ps, 4)
            sp.dma_start(W_OUT, t["w_out"][0].rearrange("(k p) n -> p k n", p=P)).then_inc(wout_in, 16)
            sp.wait_ge(kv_ps, 24)
            sp.wait_ge(qt_ps, 2 * NT)
            sp.dma_start(G2B, t["norm2_g"].rearrange("l d -> (l d)").partition_broadcast(P)).then_inc(g2_in, 16)
            for j, i in enumerate(ORDER):
                if j >= 2:
                    sp.wait_ge(x2_ready, j - 1)
                sp.dma_start(XR[j % 2], x_d[i]).then_inc(xr_in[j % 2], 16)
            for j, i in enumerate(ORDER):
                sp.wait_ge(x2n_ready, j + 1)
                sp.dma_start(x2n_d[i * P:(i + 1) * P, :], X2N[j % NX]).then_inc(x2n_out[j % NX], 16)

            def load_expert(j, e):
                sp.dma_start(WGU[j][:, 0], t["w_gate"][0, e].rearrange("(k p) n -> p k n", p=P)).then_inc(w_in_[j], 16)
                sp.dma_start(WGU[j][:, 1], t["w_up"][0, e].rearrange("(k p) n -> p k n", p=P)).then_inc(w_in_[j], 16)
                sp.dma_start(WDN[j], t["w_down"][0, e].rearrange("(k p) n -> p k n", p=P)).then_inc(w_in_[j], 16)

            for j in (1, 2):
                load_expert(j, j)
            sp.wait_ge(r_ps, NT)
            for j in range(NX):
                sp.wait_ge(x2n_out[j], 16 * (NT // NX))
            load_expert(0, 0)
            load_expert(3, 3)

            def store(row, done):
                rows = y_d.rearrange("(b p) d -> b p d", p=CAP)[row]
                sp.wait_ge(y_act, done)
                sp.dma_start(rows[:, 0:512], YB[0]).then_inc(y_out[0], 16)
                sp.wait_ge(y_dve, done)
                sp.dma_start(rows[:, 512:1024], YB[1]).then_inc(y_out[1], 16)

            sp.sem_inc(y_out[0], 16)
            sp.sem_inc(y_out[1], 16)
            with sp.Fori(0, NMAIN // NW - 1) as it:
                for j in range(NW):
                    store(it * NW + j, it * NW + (j + 2))
                    sp.wait_ge(y_ps, it * NW + (j + 1))
                    load_expert(j, it * NW + (NW + j))
            for n in range(NMAIN - NW, NMAIN):
                store(n, n + 2)
            sp.wait_ge(idx_ready, 1)
            nover = sp.value_load(OVE[0:1, NOVER:NOVER + 1], min_val=0, max_val=NOVER)
            with sp.Fori(0, NOVER) as b:
                eid = sp.value_load(OVE[0:1, bass.ds(b, 1)], min_val=0, max_val=NE - 1)
                with sp.If(b < nover):
                    sp.wait_ge(y_ps, NMAIN + b)
                    load_expert(0, eid)
                    store(b + NMAIN, b + (NMAIN + 2))
                with sp.Else():
                    sp.nop()
            sp.wait_ge(f_sum, 1)
            sp.dma_start(GFB, t["final_norm_g"].partition_broadcast(P)).then_inc(gf_in, 16)
            for i in range(NT):
                sp.wait_ge(f_ready, i + 1)
                sp.dma_start(out_d[i], OUT[i % 2]).then_inc(out_done[i % 2], 16)
            sp.wait_ge(out_done[0], 16 * (NT // 2))
            sp.wait_ge(out_done[1], 16 * (NT // 2))

        @block.tensor
        def _(pe):
            def turn(out, in_, n=P):
                return pe.transpose(out, in_, IDENT[0:n, 0:n])

            pe.wait_ge(masks_set, 7)

            def norm1_turn(i):
                pe.wait_ge(hn_ready, i + 1)
                for h in range(2):
                    if i >= 1:
                        pe.wait_ge(hnt_act if h == 0 else hnt_dve, i)
                    for q in range(4):
                        k = 4 * h + q
                        ins = turn(ps[h][:, q * P:(q + 1) * P], XB[i % 3][:, k * P:(k + 1) * P])
                    ins.then_inc(hnt_ps, 1)

            def proj(n):
                kind, a, b = PROJ[n]
                bank = ps[4 + n % 4]
                if n >= 4:
                    pe.wait_ge(proj_act, n - 3)
                need = a + 1 if kind == "T" else 4 * a + 4
                pe.wait_ge(hnt_act, need)
                pe.wait_ge(hnt_dve, need)
                for k in range(KD):
                    if k == 0:
                        pe.wait_ge(win_in[b if kind == "T" else 3], 16 if kind == "T" else 32)
                    if kind == "T":
                        c0, w = T_COLS[b]
                        ins = pe.matmul(bank[:, 0:w], HNT[:, k, a * P:(a + 1) * P], W_IN[:, k, c0:c0 + w],
                                        start=(k == 0), stop=(k == KD - 1))
                    else:
                        ins = pe.matmul(bank[:, :], W_IN[:, k, F_COLS[b]:F_COLS[b] + P],
                                        HNT[:, k, a * 512:(a + 1) * 512], start=(k == 0), stop=(k == KD - 1))
                ins.then_inc(proj_ps, 1)

            def latent_turn(i):
                pe.wait_ge(lat_ready, i + 1)
                pe.wait_ge(krp_ready, i + 1)
                if i >= 1:
                    pe.wait_ge(latt_sb, i)
                c = CQR[i % 2]
                for q in range(3):
                    turn(ps[2][:, q * P:(q + 1) * P], c[:, q * P:(q + 1) * P])
                turn(ps[2][0:QK, 3 * P:4 * P], KRP[i % 2]).then_inc(latt_ps, 1)

            n = 0
            for kind, a, b in STEPS:
                if kind == "turn":
                    norm1_turn(a)
                elif kind == "latent":
                    latent_turn(a)
                else:
                    proj(n)
                    n += 1

            pe.wait_ge(hnt_act, NT)
            pe.wait_ge(hnt_dve, NT)
            pe.wait_ge(latt_sb, NT)
            pe.wait_ge(proj_act, NPROJ)
            for kind in range(2):
                for half in range(2):
                    for q in range(4):
                        i = 4 * half + q
                        ins = turn(ps[2 * kind + half][0:MLH, q * P:(q + 1) * P],
                                   GATES[:, i * 8 + 4 * kind:i * 8 + 4 * kind + 4])
                    ins.then_inc(gate_ps, 1)
            for m in range(2):
                for half in range(2):
                    for q in range(4):
                        i = 4 * half + q
                        ins = turn(ps[4 + 2 * m + half][:, q * P:(q + 1) * P], KTOK[:, i, m * P:(m + 1) * P])
                    ins.then_inc(ktm_ps, 1)
            j = 0
            for f in range(2):
                pe.wait_ge(conv_done, f + 1)
                for g in range(2):
                    for half in range(2):
                        if j < 4:
                            pe.wait_ge(ktm_sb, j + 1)
                        else:
                            pe.wait_ge(lgate_sb, j - 3)
                        pe.matmul(ps[4 + j % 4][:, :], BD[:, (2 * g + f) * P:(2 * g + f + 1) * P],
                                  LT[f][0][:, half * 512:(half + 1) * 512], start=True, stop=True).then_inc(lgate_ps, 1)
                        j += 1
            pe.wait_ge(rows_done, 5)
            for half in range(2):
                for q in range(4):
                    i = 4 * half + q
                    ins = turn(ps[half][:, q * P:(q + 1) * P], ROWS4[:, i * P:(i + 1) * P])
                ins.then_inc(cols_ps, 1)
            for h in range(MLH):
                ins = pe.matmul(ps[2][:, h * NT:(h + 1) * NT], SEL[:, h * P:(h + 1) * P], DEC[:, :], start=True, stop=True)
            ins.then_inc(cols_ps, 1)
            pe.wait_ge(cols_sb, 3)
            pe.wait_ge(lgate_sb, 8)
            pe.wait_ge(yr_sq, 2)
            for half in range(2):
                for f in range(2):
                    ins = pe.matmul(ps[half][:, :], ONES[:, :], LT[f][3][:, half * 512:(half + 1) * 512],
                                    start=(f == 0), stop=(f == 1))
                ins.then_inc(yr_ps, 1)
            pe.wait_ge(yr_rstd, 2)

            def chunk_front(c):
                if c >= 1:
                    pe.wait_ge(d_ready, c)
                    pe.wait_ge(pw_ready, c)
                for h in range(MLH):
                    ins = pe.matmul(ps[0][:, h * P:(h + 1) * P], SEL[:, h * P:(h + 1) * P],
                                    ROW_A[:, c * P:(c + 1) * P], start=True, stop=True)
                ins.then_inc(db_ps, 1)
                for par in range(2):
                    for m in range(2):
                        r = slice(64 * par, 64 * par + 64)
                        ins = pe.matmul(ps[1 + par][:, m * P:(m + 1) * P], KTM[r, m, c * P:(c + 1) * P],
                                        MQT[r, m, c * P:(c + 1) * P], start=True, stop=True)
                ins.then_inc(st_ps, 1)

            def chunk_state(c):
                pe.wait_ge(state_ready, c + 1)
                if c >= 1:
                    pe.wait_ge(inter_sb, c)
                for par in range(2):
                    for m in range(2):
                        r = slice(64 * par, 64 * par + 64)
                        ins = pe.matmul(ps[4 + par][:, m * VA:(m + 1) * VA], MQT[r, m, c * P:(c + 1) * P],
                                        CST[r, m * VA:(m + 1) * VA], start=True, stop=True)
                ins.then_inc(inter_ps, 1)
                pe.wait_ge(ks_ready, c + 1)
                for m in range(2):
                    ins = pe.matmul(ps[6][:, m * 2 * VA:(m + 1) * 2 * VA], KSB[c % 2][:, m * P:(m + 1) * P],
                                    VAUG[:, c, 2 * m:2 * m + 2, :], start=True, stop=True)
                ins.then_inc(upd_ps, 1)

            def chunk_intra(c):
                pe.wait_ge(pw_ready, c + 1)
                if c >= 1:
                    pe.wait_ge(num_ready, c)
                for h in range(MLH):
                    ins = pe.matmul(ps[3][:, h * VA:(h + 1) * VA], PWB[c % 2][:, h * P:(h + 1) * P], VAUG[:, c, h, :],
                                    start=True, stop=True)
                ins.then_inc(intra_ps, 1)

            def kv_proj(j):
                pe.wait_ge(kv_sb, j) if j >= 1 else pe.wait_ge(ktm_sb, 4)
                if j < 16:
                    h, half = j // 2, j % 2
                    ins = pe.matmul(ps[7][0:NOPE, :], W_UKV[:, h, 0:NOPE], CKVT[:, half * 512:(half + 1) * 512], start=True, stop=True)
                else:
                    i = j - 16
                    ins = pe.matmul(ps[7][:, :], CKVT[:, i * P:(i + 1) * P], W_UKV[:, :, NOPE:], start=True, stop=True)
                ins.then_inc(kv_ps, 1)

            pe.wait_ge(wu_in, 16)
            chunk_front(0)
            for c in range(NT):
                chunk_state(c)
                kv_proj(3 * c)
                if c + 1 < NT:
                    chunk_front(c + 1)
                kv_proj(3 * c + 1)
                chunk_intra(c)
                kv_proj(3 * c + 2)
            pe.wait_ge(num_ready, NT)
            pe.wait_ge(inter_sb, NT)
            pe.wait_ge(state_ready, NT + 1)
            pe.wait_ge(kv_sb, 24)
            pe.wait_ge(wuq_in, 16)

            def q_proj(i):
                if i >= 1:
                    pe.wait_ge(q_sb, i)
                for b in range(2):
                    for k in range(2):
                        ins = pe.matmul(ps[4 + b][:, 0:384], CQT[:, k, i * P:(i + 1) * P],
                                        W_UQ[:, k, b * 384:(b + 1) * 384], start=(k == 0), stop=(k == 1))
                ins.then_inc(q_ps, 1)

            def q_turn(i):
                pe.wait_ge(q_rope, i + 1)
                for b in range(2):
                    if i >= 1:
                        pe.wait_ge(qt_act if b == 0 else qt_dve, i)
                    for q in range(4):
                        ins = turn(ps[6 + b][0:QK, q * P:(q + 1) * P], QTOK[i % 2][:, 4 * b + q, :])
                    ins.then_inc(qt_ps, 1)

            q_proj(0)
            for i in range(NT):
                if i + 1 < NT:
                    q_proj(i + 1)
                q_turn(i)

            pe.wait_ge(ymt_ready, 1)
            for m in range(2):
                for half in range(2):
                    for q in range(4):
                        ins = turn(ps[2 * m + half][:, q * P:(q + 1) * P], OTOK[:, 4 * half + q, m * P:(m + 1) * P])
                    ins.then_inc(ym_ps, 1)
            pe.wait_ge(ym_sb, 4)

            def scores(n):
                i, h = ATT[n]
                if n >= 2:
                    pe.wait_ge(p_ready, n - 1)
                L = (i + 1) * P
                for b in range((L + 511) // 512):
                    w = min(512, L - 512 * b)
                    ins = pe.matmul(ps[2 * (n % 2) + b][:, 0:w], QT[0:QK, i, h, :],
                                    KT[0:QK, h, 512 * b:512 * b + w], start=True, stop=True)
                ins.then_inc(s_ps, 1)

            def probs_turn(n):
                i, h = ATT[n]
                pe.wait_ge(p_ready, n + 1)
                for g in range(G0[n + 1] - G0[n]):
                    gg = G0[n] + g
                    if gg >= 2:
                        pe.wait_ge(pt_act if gg % 2 == 0 else pt_dve, gg // 2)
                    for q in range(min(4, i + 1 - 4 * g)):
                        ins = turn(ps[4 + gg % 2][:, q * P:(q + 1) * P], PB[n % 2][:, (4 * g + q) * P:(4 * g + q + 1) * P])
                    ins.then_inc(pt_ps, 1)

            def values(n):
                i, h = ATT[n]
                if n >= 1:
                    pe.wait_ge(pv_sb, n)
                for kb in range(i + 1):
                    gg = G0[n] + kb // 4
                    if kb % 4 == 0:
                        pe.wait_ge(pt_act if gg % 2 == 0 else pt_dve, gg // 2 + 1)
                    q = kb % 4
                    ins = pe.matmul(ps[6][:, 0:VD], PTB[gg % 4][:, q * P:(q + 1) * P], V[:, kb, h, :],
                                    start=(kb == 0), stop=(kb == i))
                ins.then_inc(pv_ps, 1)

            pe.wait_ge(kv_sb, 24)
            pe.wait_ge(kr_sb, 1)
            pe.wait_ge(qt_act, NT)
            pe.wait_ge(qt_dve, NT)
            def ya_turn(t):
                pe.wait_ge(ya_ready, t + 1)
                pe.wait_ge(x2_ready, t)
                for q in range(4):
                    ins = turn(ps[7][:, q * P:(q + 1) * P], YA[:, ORDER[t], q * P:(q + 1) * P])
                ins.then_inc(yat_ps, 1)

            def out_proj(t, b, ks):
                i = ORDER[t]
                if ks[0] == 0:
                    if b == 0:
                        pe.wait_ge(yat_sb, t + 1)
                    else:
                        pe.wait_ge(x2_half, t + 1)
                lhs = [YM[:, 0, i * P:(i + 1) * P], YM[:, 1, i * P:(i + 1) * P], RXP[:, 0, 3 + i * P:3 + (i + 1) * P],
                       RXP[:, 1, 3 + i * P:3 + (i + 1) * P]] + [YAT[t % 2][:, q * P:(q + 1) * P] for q in range(4)]
                for k in ks:
                    ins = pe.matmul(ps[7][:, :], lhs[k], W_OUT[:, k, b * 512:(b + 1) * 512],
                                    start=(k == 0), stop=(k == KD - 1))
                if ks[-1] == KD - 1:
                    ins.then_inc(o_ps, 1)

            def between(n):
                for t, off in due(n):
                    if off == DUE["turn"]:
                        ya_turn(t)
                    for b in range(2):
                        if off in DUE[f"half{b}"]:
                            out_proj(t, b, ((0, 1, 2), (3, 4, 5), (6, 7))[DUE[f"half{b}"].index(off)])

            pe.wait_ge(wout_in, 16)
            scores(0)
            for n in range(LAST):
                if n + 1 < N:
                    scores(n + 1)
                between(n)
                if n < N:
                    probs_turn(n)
                if 1 <= n <= N:
                    values(n - 1)

            def x2n_turn(j):
                pe.wait_ge(x2n_ready, j + 1)
                for h in range(2):
                    if j >= 2:
                        pe.wait_ge(x2nt_act if h == 0 else x2nt_dve, j - 1)
                    for q in range(4):
                        k = 4 * h + q
                        ins = turn(ps[2 * (j % 2) + h][:, q * P:(q + 1) * P], X2N[j % NX][:, k * P:(k + 1) * P])
                    ins.then_inc(x2nt_ps, 1)

            def router(j):
                pe.wait_ge(x2nt_act, j + 1)
                pe.wait_ge(x2nt_dve, j + 1)
                if j >= 2:
                    pe.wait_ge(r_sb, j - 1)
                for k in range(KD):
                    ins = pe.matmul(ps[4 + j % 2][:, 0:36], X2NT[j % 2][:, k, :], WR[:, k * 36:(k + 1) * 36],
                                    start=(k == 0), stop=(k == KD - 1))
                ins.then_inc(r_ps, 1)

            x2n_turn(0)
            for j in range(NT):
                if j + 1 < NT:
                    x2n_turn(j + 1)
                router(j)

            pe.wait_ge(mask_ready, 1)
            mask = RA[:, 0:NT * NE].rearrange("p (i e) -> p i e", i=NT)
            for i in range(NT):
                pe.matmul(ps[0][:, i * NE:(i + 1) * NE], TRI[:, :], mask[:, i, :], start=True, stop=(i == 0))
                for i2 in range(i):
                    pe.matmul(ps[0][:, i * NE:(i + 1) * NE], ONES[:, :], mask[:, i2, :], start=False, stop=(i2 == i - 1))
            for i in range(NT):
                ins = pe.matmul(ps[1][:, 0:NE], ONES[:, :], mask[:, i, :], start=(i == 0), stop=(i == NT - 1))
            ins.then_inc(pos_ps, 1)
            pe.wait_ge(ids_in, 16)
            turn(ps[2][:, 0:NBLK], IDR[:, :], NBLK).then_inc(ids_ps, 1)
            pe.wait_ge(idx_ready, 1)

            def rows_turn(u, done):
                pe.wait_ge(xgt_act, done)
                pe.wait_ge(xgt_dve, done)
                for h in range(2):
                    for q in range(4):
                        k = 4 * h + q
                        ins = turn(ps[h][:, q * P:(q + 1) * P], XG[u][:, k * P:(k + 1) * P])
                    ins.then_inc(xgt_ps, 1)

            def gate_up(u, w, done):
                pe.wait_ge(xgt_act, done + 1)
                pe.wait_ge(xgt_dve, done + 1)
                for g in range(2):
                    for m in range(2):
                        for k in range(KD):
                            ins = pe.matmul(ps[2 + 2 * u + g][:, m * P:(m + 1) * P],
                                            WGU[w][:, g, k, m * P:(m + 1) * P], XGT[u][:, k, :],
                                            start=(k == 0), stop=(k == KD - 1))
                    ins.then_inc(gu_ps, 1)

            def down(u, w, done):
                pe.wait_ge(h_ready, done + 1)
                pe.wait_ge(y_act, done)
                pe.wait_ge(y_dve, done)
                for b in range(2):
                    for k in range(2):
                        ins = pe.matmul(ps[6 + b][:, :], HT[u][:, k, :], WDN[w][:, k, b * 512:(b + 1) * 512],
                                        start=(k == 0), stop=(k == 1))
                ins.then_inc(y_ps, 1)

            pe.wait_ge(xg_in[0], 16)
            rows_turn(0, 1)
            with pe.Fori(0, NMAIN // NW) as it:
                for j in range(NW):
                    u = j % 2
                    pe.wait_ge(w_in_[j], it * 48 + 48)
                    gate_up(u, j, it * NW + (j + 1))
                    pe.wait_ge(xg_in[1 - u], it * (NW // 2 * 16) + 16 * ((j + 1) // 2 + 1))
                    rows_turn(1 - u, it * NW + (j + 2))
                    down(u, j, it * NW + (j + 1))
            nover = pe.value_load(OVE[0:1, NOVER:NOVER + 1], min_val=0, max_val=NOVER)
            with pe.Fori(0, NOVER) as b:
                with pe.If(b < nover):
                    pe.wait_ge(xg_in[0], (NMAIN // 2 + 2) * 16 + b * 16)
                    pe.wait_ge(w_in_[0], (NMAIN // NW) * 48 + 48 + b * 48)
                    rows_turn(0, NMAIN + 2 + b)
                    gate_up(0, 0, NMAIN + 2 + b)
                    down(0, 0, NMAIN + 1 + b)
                with pe.Else():
                    pe.nop()

        @block.scalar
        def _(act):
            link = chained(act, act_chain)

            def exp_and_ln():
                act.preload_act_table_set("natural_log_exp_and_others")

            exp_and_ln()

            def col_load(dst, src, n):
                act.dma_start(dst, src).then_inc(const_in, 16)

            row = lambda a: a.rearrange("l n -> (l n)").partition_broadcast(P)
            colw = lambda a: a[0].rearrange("(f p) -> p f", p=P)
            with nc.allow_non_contiguous_dma(reason="small columns"):
                act.dma_start(GQ[:, 0:QL], row(t["q_norm_g"])).then_inc(const_in, 16)
                act.dma_start(GQ[:, QL:], row(t["kv_norm_g"])).then_inc(const_in, 16)
                act.dma_start(COS[:, :].rearrange("p (i n) -> p i n", i=NT), t["rope_cos"].rearrange("(i p) n -> p i n", p=P)).then_inc(const_in, 16)
                act.dma_start(SIN[:, :].rearrange("p (i n) -> p i n", i=NT), t["rope_sin"].rearrange("(i p) n -> p i n", p=P)).then_inc(const_in, 16)
                act.dma_start(BGI[:, :], t["ml_i_bias"].rearrange("l h -> h l")).then_inc(const_in, 16)
                act.dma_start(BGF[:, :], t["ml_f_bias"].rearrange("l h -> h l")).then_inc(const_in, 16)
                for f in range(2):
                    act.dma_start(CW[:, f * CONV:(f + 1) * CONV], t["conv_w"][0, :, f * P:(f + 1) * P].rearrange("j p -> p j")).then_inc(const_in, 16)
                act.dma_start(CB[:, :], colw(t["conv_b"])).then_inc(const_in, 16)
                act.dma_start(BR[:, :], colw(t["lru_b_r"])).then_inc(const_in, 16)
                act.dma_start(BI[:, :], colw(t["lru_b_i"])).then_inc(const_in, 16)
                act.dma_start(LAM[:, :], colw(t["lru_lambda"])).then_inc(const_in, 16)
                act.dma_start(GLRU[:, :], colw(t["lru_norm_g"])).then_inc(const_in, 16)
                act.dma_start(GML[:, :], row(t["ml_norm_g"])).then_inc(const_in, 16)
                act.dma_start(GMLA[:, :], row(t["mla_norm_g"])).then_inc(const_in, 16)
                act.wait_ge(masks_set, 7)
                for g, w in enumerate(("lru_w_r", "lru_w_i")):
                    for f in range(2):
                        for q in range(2):
                            r = slice(64 * q, 64 * q + 64)
                            c0 = (2 * g + f) * P + 64 * q
                            act.dma_start(BD[r, c0:c0 + 64], t[w][0, 2 * f + q]).then_inc(const_in, 16)
                wr = WR[:, :].rearrange("p (k n) -> p k n", k=KD)
                act.dma_start(wr[:, :, 0:NG], t["w_group"][0].rearrange("(k p) n -> p k n", p=P)).then_inc(const_in, 16)
                act.dma_start(wr[:, :, NG:], t["w_expert"][0].rearrange("(k p) n -> p k n", p=P)).then_inc(const_in, 16)
                act.dma_start(BRT[:, 0:NG], row(t["b_group"])).then_inc(const_in, 16)
                act.dma_start(BRT[:, NG:], row(t["b_expert"])).then_inc(const_in, 16)

            def norm1_stats(i):
                act.wait_ge(x_in[i % 3], 16 * (i // 3 + 1))
                link(act.activation(JUNK[:, :], XB[i % 3], ACT.Square, accum_out=ST1[:, i:i + 1]))
                link(act.activation(ST1[:, NT + i:NT + i + 1], ST1[:, i:i + 1], ACT.Ln, bias=EPSC[:, :], scale=1.0 / D))
                act.activation(ST1[:, NT + i:NT + i + 1], ST1[:, NT + i:NT + i + 1], ACT.Exp, scale=-0.5).then_inc(x_rstd, 1)

            def norm1_evac(i):
                act.wait_ge(hnt_ps, 2 * i + 1)
                act.activation(HNT[:, 0:4, i * P:(i + 1) * P], ps[0][:, :].rearrange("p (k n) -> p k n", k=4),
                               ACT.Copy).then_inc(hnt_act, 1)

            def proj_evac(n):
                kind, a, b = PROJ[n]
                bank = ps[4 + n % 4]
                act.wait_ge(proj_ps, n + 1)
                if kind == "F":
                    s = slice(a * 512, (a + 1) * 512)
                    dst = [MQT[:, 0, s], MQT[:, 1, s], RXP[:, 0, 3 + a * 512:3 + (a + 1) * 512],
                           RXP[:, 1, 3 + a * 512:3 + (a + 1) * 512], RG[:, 0, s], RG[:, 1, s]][b]
                    act.activation(dst, bank[:, :], ACT.Copy).then_inc(proj_act, 1)
                elif b == 0:
                    act.activation(KTOK[:, a, :], bank[:, 0:MLW], ACT.Copy, scale=MLD ** -0.5)
                    act.activation(VAUG[:, a, :, 0:MLD], bank[:, MLW:512].rearrange("p (h n) -> p h n", h=MLH), ACT.Copy).then_inc(proj_act, 1)
                elif b == 1:
                    act.activation(GATES[:, a * 8:a * 8 + 8], bank[:, MLW:MLW + 8], ACT.Copy)
                    act.activation(OTOK[:, a, :], bank[:, 0:MLW], ACT.Exp, scale=-1.0).then_inc(proj_act, 1)
                else:
                    if a >= 2:
                        act.wait_ge(latt_ps, a - 1)
                    act.activation(CQR[a % 2], bank[:, 0:N_LAT], ACT.Copy).then_inc(proj_act, 1)
                    act.wait_ge(proj_act, n + 1)
                    c = CQR[a % 2]
                    act.activation(JUNK[:, 0:QL], c[:, 0:QL], ACT.Square, accum_out=ST2[:, 2 * a:2 * a + 1])
                    link(act.activation(JUNK[:, QL:QL + KVL], c[:, QL:QL + KVL], ACT.Square, accum_out=ST2[:, 2 * a + 1:2 * a + 2]))
                    o = 2 * NT + 2 * a
                    act.activation(ST2[:, o:o + 1], ST2[:, 2 * a:2 * a + 1], ACT.Ln, bias=EPSC[:, :], scale=1.0 / QL)
                    link(act.activation(ST2[:, o + 1:o + 2], ST2[:, 2 * a + 1:2 * a + 2], ACT.Ln, bias=EPSC[:, :], scale=1.0 / KVL))
                    act.activation(ST2[:, o:o + 2], ST2[:, o:o + 2], ACT.Exp, scale=-0.5).then_inc(lat_rstd, 1)

            def latent_evac(i):
                act.wait_ge(latt_ps, i + 1)
                s = slice(i * P, (i + 1) * P)
                act.activation(CQT[:, :, s], ps[2][:, 0:2 * P].rearrange("p (m n) -> p m n", m=2), ACT.Copy)
                act.activation(CKVT[:, s], ps[2][:, 2 * P:3 * P], ACT.Copy)
                act.activation(KPT[0:QK, s], ps[2][0:QK, 3 * P:4 * P], ACT.Copy).then_inc(latt_sb, 1)

            norm1_stats(0)
            norm1_stats(1)
            n = 0
            for kind, a, b in STEPS:
                if kind == "turn":
                    norm1_evac(a)
                    if a + 2 < NT:
                        norm1_stats(a + 2)
                elif kind == "latent":
                    latent_evac(a)
                else:
                    proj_evac(n)
                    n += 1

            act.wait_ge(const_in, 16 * NC_)
            for kind, dst, bias in ((0, ROW_I, BGI), (1, ROW_F, BGF)):
                for half in range(2):
                    act.wait_ge(gate_ps, 2 * kind + half + 1)
                    act.activation(dst[:, half * 512:(half + 1) * 512], ps[2 * kind + half][0:MLH, :], ACT.Identity,
                                   bias=bias[:, :]).then_inc(gate_rows, 1)
            act.wait_ge(gate_rows, 4)
            link(act.activation(ROW_T, ROW_F, ACT.Abs))
            link(act.activation(ROW_T, ROW_T, ACT.Exp, scale=-1.0))
            act.activation(ROW_T, ROW_T, ACT.Ln, bias=ONEC[0:MLH, :]).then_inc(lf_t, 1)
            for j in range(4):
                act.wait_ge(ktm_ps, j + 1)
                m, half = j // 2, j % 2
                act.activation(KTM[:, m, half * 512:(half + 1) * 512], ps[4 + j][:, :], ACT.Copy).then_inc(ktm_sb, 1)
            act.wait_ge(lam_s, 1)
            act.activation(SPT[:, 2:4], SPT[:, 0:2], ACT.Exp, scale=-1.0).then_inc(lam_s, 1)
            act.wait_ge(rows_pre, 1)
            act.activation(ROWS4[32:32 + MLH, :], ROW_T, ACT.Exp).then_inc(rows_done, 1)
            act.activation(ROWS4[64:64 + MLH, :], ROW_T2, ACT.Exp).then_inc(rows_done, 1)
            act.activation(ROWS4[96:96 + MLH, :], ROW_M, ACT.Exp, scale=-1.0).then_inc(rows_done, 1)
            act.activation(DEC[:, :], MPV[:, :], ACT.Exp).then_inc(rows_done, 1)
            act.wait_ge(lam_done, 1)
            for f in range(2):
                XC, R, IV, T, D1 = LT[f]
                act.wait_ge(gelu_arg, f + 1)
                act.activation(D1, T, ACT.Sigmoid, scale=GELU_S).then_inc(gelu_sig, 1)
                for g in range(2):
                    for half in range(2):
                        j = 4 * f + 2 * g + half
                        act.wait_ge(lgate_ps, j + 1)
                        act.activation((R, IV)[g][:, half * 512:(half + 1) * 512], ps[4 + j % 4][:, :], ACT.Sigmoid,
                                       bias=(BR, BI)[g][:, f:f + 1]).then_inc(lgate_sb, 1)
                act.wait_ge(lgate_sb, 4 * f + 4)
                act.wait_ge(gelu_done, f + 1)
                act.activation(T, R, ACT.Tanh, scale=SPT[:, 8 + f:9 + f]).then_inc(lru_a, 1)
                act.wait_ge(lru_a, 2 * f + 1)
                act.activation(R, R, ACT.Exp, scale=SPT[:, 10 + f:11 + f]).then_inc(lru_a, 1)
            for f in range(2):
                act.wait_ge(lru_ratio, f + 1)
                act.activation(LT[f][3], LT[f][3], ACT.Sqrt).then_inc(lru_root, 1)
            exp_and_ln()
            R = LT[0][1]
            for half in range(2):
                s = slice(half * 512, (half + 1) * 512)
                act.wait_ge(yr_ps, half + 1)
                link(act.activation(R[:, s], ps[half][:, :], ACT.Ln, bias=EPSC[:, :], scale=1.0 / LRU))
                act.activation(R[:, s], R[:, s], ACT.Exp, scale=-0.5).then_inc(yr_rstd, 1)
            act.wait_ge(cols_sb, 3)
            act.wait_ge(yr_done, 1)
            col = COL[:, :].rearrange("p (i k h) -> p i k h", i=NT, k=4)

            def weights(c):
                act.wait_ge(d_ready, c + 1)
                if c >= 2:
                    act.wait_ge(pw_ready, c - 1)
                for h in range(MLH):
                    ins = act.activation(WSB[c % 2][:, h * P:(h + 1) * P], DSB[c % 2][:, h * P:(h + 1) * P], ACT.Exp,
                                         bias=col[:, c, 0, h:h + 1])
                ins.then_inc(w_ready, 1)

            def kv_evac(j):
                act.wait_ge(kv_ps, j + 1)
                if j < 16:
                    h, half = j // 2, j % 2
                    act.activation(KT[0:NOPE, h, half * 512:(half + 1) * 512], ps[7][0:NOPE, :], ACT.Copy).then_inc(kv_sb, 1)
                else:
                    act.activation(V[:, j - 16].rearrange("p h n -> p (h n)"), ps[7][:, :], ACT.Copy).then_inc(kv_sb, 1)

            weights(0)
            for c in range(NT):
                act.wait_ge(inter_ps, c + 1)
                if c >= 2:
                    act.wait_ge(num_ready, c - 1)
                for h in range(MLH):
                    ins = act.activation(INT[c % 2][:, h * VA:(h + 1) * VA], ps[4 + h % 2][:, (h // 2) * VA:(h // 2 + 1) * VA],
                                         ACT.Copy, scale=col[:, c, 1, h:h + 1])
                ins.then_inc(inter_sb, 1)
                kv_evac(3 * c)
                if c + 1 < NT:
                    weights(c + 1)
                kv_evac(3 * c + 1)
                kv_evac(3 * c + 2)

            act.wait_ge(h_done, NT)
            act.wait_ge(pw_ready, NT)
            act.wait_ge(intra_ps, NT)
            act.activation(SQ, OTOK.rearrange("p i n -> p (i n)"), ACT.Square).then_inc(mh_sq, 1)

            def q_evac(i):
                act.wait_ge(q_ps, i + 1)
                if i >= 2:
                    act.wait_ge(qt_ps, 2 * (i - 1))
                for b in range(2):
                    ins = act.activation(QTOK[i % 2][:, 4 * b:4 * b + 4, :], ps[4 + b][:, 0:384].rearrange("p (h n) -> p h n", h=4), ACT.Copy, scale=SCALE)
                ins.then_inc(q_sb, 1)

            def qt_evac(i):
                act.wait_ge(qt_ps, 2 * i + 1)
                act.activation(QT[0:QK, i, 0:4, :], ps[6][0:QK, :].rearrange("p (h n) -> p h n", h=4), ACT.Copy).then_inc(qt_act, 1)

            act.wait_ge(yr_done, 1)
            q_evac(0)
            act.wait_ge(mh_ss, 1)
            n = NT * MLH
            link(act.activation(MSS[:, n:2 * n], MSS[:, 0:n], ACT.Ln, bias=EPSC[:, :], scale=1.0 / MLD))
            act.activation(MSS[:, 2 * n:3 * n], MSS[:, n:2 * n], ACT.Exp, scale=-0.5).then_inc(mh_rstd, 1)
            for i in range(1, NT):
                q_evac(i)
                qt_evac(i - 1)
            qt_evac(NT - 1)
            act.wait_ge(zero_out, 16 * NOVER)
            for j in range(4):
                m, half = j // 2, j % 2
                act.wait_ge(ym_ps, j + 1)
                act.activation(YM[:, m, half * 512:(half + 1) * 512], ps[j][:, :], ACT.Copy).then_inc(ym_sb, 1)

            def probs(n):
                i, h = ATT[n]
                L = (i + 1) * P
                act.wait_ge(s_max, n + 1)
                if n >= 2:
                    act.wait_ge(pt_ps, G0[n - 1])
                for b in range((L + 511) // 512):
                    w = min(512, L - 512 * b)
                    ins = act.activation(PB[n % 2][:, 512 * b:512 * b + w], ps[2 * (n % 2) + b][:, 0:w], ACT.Exp,
                                         bias=NMX[:, n:n + 1],
                                         accum_out=(RSM if b == 0 else RIN)[:, n:n + 1])
                ins.then_inc(p_ready, 1)

            def probs_evac(n):
                i, h = ATT[n]
                for gg in range(G0[n], G0[n + 1]):
                    if gg % 2 == 0:
                        act.wait_ge(pt_ps, gg + 1)
                        if gg >= 4:
                            act.wait_ge(pv_ps, GROUPS[gg - 4][0] + 1)
                        w = P * min(4, i + 1 - 4 * GROUPS[gg][1])
                        act.activation(PTB[gg % 4][:, 0:w], ps[4][:, 0:w], ACT.Copy).then_inc(pt_act, 1)

            def between(n):
                for t, off in due(n):
                    i = ORDER[t]
                    if off == DUE["sumsq"]:
                        act.wait_ge(pv_sb, H * (t + 1))
                        link(act.activation(JUNK[:, 0:H * VD], YA[:, i, :], ACT.Square, accum_out=ST1[:, i:i + 1]))
                        link(act.activation(ST1[:, NT + i:NT + i + 1], ST1[:, i:i + 1], ACT.Ln, bias=EPSC[:, :], scale=1.0 / (H * VD)))
                        act.activation(ST2[:, i:i + 1], ST1[:, NT + i:NT + i + 1], ACT.Exp, scale=-0.5).then_inc(ya_rstd, 1)
                    if off == DUE["turn"]:
                        act.wait_ge(yat_ps, t + 1)
                        act.activation(YAT[t % 2], ps[7][:, :], ACT.Copy).then_inc(yat_sb, 1)
                    if off == DUE["sumsq2"]:
                        act.wait_ge(x2_ready, t + 1)
                        link(act.activation(JUNK[:, :], X2[:, i, :], ACT.Square, accum_out=ST1[:, i:i + 1]))
                        link(act.activation(ST1[:, NT + i:NT + i + 1], ST1[:, i:i + 1], ACT.Ln, bias=EPSC[:, :], scale=1.0 / D))
                        act.activation(ST2[:, NT + i:NT + i + 1], ST1[:, NT + i:NT + i + 1], ACT.Exp, scale=-0.5).then_inc(x2_rstd, 1)

            probs(0)
            for n in range(LAST):
                if n + 1 < N:
                    probs(n + 1)
                if n < N:
                    probs_evac(n)
                between(n)

            for j in range(NT):
                act.wait_ge(x2nt_ps, 2 * j + 1)
                if j >= 2:
                    act.wait_ge(r_ps, j - 1)
                act.activation(X2NT[j % 2][:, 0:4, :], ps[2 * (j % 2)][:, :].rearrange("p (k n) -> p k n", k=4), ACT.Copy).then_inc(x2nt_act, 1)
            act.wait_ge(rt_a, 1)
            act.activation(RB[:, 8 * NT:12 * NT], RB[:, 4 * NT:8 * NT], ACT.Exp).then_inc(rt_b, 1)
            act.wait_ge(rt_a, 2)
            act.activation(RB[:, 13 * NT:14 * NT], RB[:, 12 * NT:13 * NT], ACT.Exp).then_inc(rt_b, 1)
            act.wait_ge(idx_ready, 1)

            def rows_evac(u, done):
                act.wait_ge(xgt_ps, done)
                act.activation(XGT[u][:, 0:4, :], ps[0][:, :].rearrange("p (k n) -> p k n", k=4), ACT.Copy).then_inc(xgt_act, 1)

            def silu(u, gates, prior):
                act.wait_ge(gu_ps, gates)
                act.wait_ge(h_ready, prior)
                act.activation(SG, ps[2 + 2 * u][:, 0:2 * P], ACT.Silu).then_inc(sg_ready, 1)

            def y_evac(done):
                act.wait_ge(y_ps, done)
                act.activation(YB[0], ps[6][:, :], ACT.Copy).then_inc(y_act, 1)

            act.sem_inc(xgt_act, 1)
            act.sem_inc(y_act, 1)
            rows_evac(0, 1)
            with act.Fori(0, NMAIN // NW) as it:
                for j in range(NW):
                    u = j % 2
                    silu(u, it * (2 * NW) + (2 * j + 1), it * NW + (j + 1))
                    rows_evac(1 - u, it * (2 * NW) + (2 * j + 3))
                    act.wait_ge(y_out[0], it * (16 * NW) + 16 * (j + 1))
                    y_evac(it * NW + (j + 1))
            nover = act.value_load(OVE[0:1, NOVER:NOVER + 1], min_val=0, max_val=NOVER)
            with act.Fori(0, NOVER) as b:
                with act.If(b < nover):
                    rows_evac(0, b * 2 + (2 * NMAIN + 3))
                    silu(0, b * 2 + (2 * NMAIN + 1), b + (NMAIN + 1))
                    act.wait_ge(y_out[0], b * 16 + 16 * (NMAIN + 1))
                    y_evac(b + (NMAIN + 1))
                with act.Else():
                    act.nop()
            exp_and_ln()
            for i in range(NT):
                act.wait_ge(f_sum, i + 1)
                link(act.activation(JUNK[:, :], X2[:, i, :], ACT.Square, accum_out=ST1[:, i:i + 1]))
                link(act.activation(ST1[:, NT + i:NT + i + 1], ST1[:, i:i + 1], ACT.Ln, bias=EPSC[:, :], scale=1.0 / D))
                act.activation(ST2[:, i:i + 1], ST1[:, NT + i:NT + i + 1], ACT.Exp, scale=-0.5).then_inc(f_rstd, 1)

        @block.vector
        def _(dve):
            link = chained(dve, dve_chain)
            dve.memset(EPSC[:, :], EPS).then_inc(masks_set, 1)
            dve.memset(ONEC[:, :], 1.0).then_inc(masks_set, 1)
            dve.memset(VAUG[:, :, :, MLD:], 1.0)
            dve.memset(RXP[:, :, 0:3], 0.0)
            dve.memset(CST[:, :], 0.0).then_inc(state_ready, 1)

            def norm1_apply(i):
                dve.wait_ge(x_rstd, i + 1)
                dve.wait_ge(x_in[i % 3], 16 * (i // 3 + 1))
                dve.scalar_tensor_tensor(XB[i % 3], XB[i % 3], ST1[:, NT + i:NT + i + 1], GB[:, :], ALU.mult, ALU.mult).then_inc(hn_ready, 1)

            def norm1_evac(i):
                dve.wait_ge(hnt_ps, 2 * i + 2)
                dve.tensor_copy(HNT[:, 4:8, i * P:(i + 1) * P], ps[1][:, :].rearrange("p (k n) -> p k n", k=4)).then_inc(hnt_dve, 1)

            def output_gate(i):
                dve.wait_ge(proj_act, job("T", i, 1) + 1)
                o = OTOK[:, i, :]
                link(dve.tensor_scalar(o, o, 1.0, None, ALU.add))
                dve.reciprocal(o, o)

            def conv(f):
                dve.wait_ge(proj_act, job("F", 1, 2 + f) + 1)
                dve.wait_ge(hnt_ps, 2 * NT)
                XC = LT[f][0]
                link(dve.tensor_scalar(XC, RXP[:, f, 3:3 + S], CW[:, f * CONV + 3:f * CONV + 4], CB[:, f:f + 1], ALU.mult, ALU.add))
                for j in range(CONV - 1):
                    ins = dve.scalar_tensor_tensor(XC, RXP[:, f, j:j + S], CW[:, f * CONV + j:f * CONV + j + 1], XC, ALU.mult, ALU.add)
                    if j < CONV - 2:
                        link(ins)
                    else:
                        ins.then_inc(conv_done, 1)

            def tile_evac(i):
                dve.wait_ge(lat_rstd, i + 1)
                c = CQR[i % 2]
                o = 2 * NT + 2 * i
                dve.scalar_tensor_tensor(c[:, 0:QL], c[:, 0:QL], ST2[:, o:o + 1], GQ[:, 0:QL], ALU.mult, ALU.mult)
                dve.scalar_tensor_tensor(c[:, QL:QL + KVL], c[:, QL:QL + KVL], ST2[:, o + 1:o + 2], GQ[:, QL:], ALU.mult, ALU.mult).then_inc(lat_ready, 1)

            dve.wait_ge(g1_in, 16)
            norm1_apply(0)
            norm1_apply(1)
            for kind, a, b in STEPS:
                if kind == "turn":
                    norm1_evac(a)
                    if a + 2 < NT:
                        norm1_apply(a + 2)
                elif kind == "T" and b == 1:
                    output_gate(a)
                elif kind == "T" and b == 2:
                    if a == 0:
                        dve.wait_ge(const_in, 16 * NC_)
                    tile_evac(a)

            link(dve.tensor_scalar(SPT[:, 4:6], LAM[:, :], -1.0, None, ALU.mult))
            dve.tensor_tensor(SPT[:, 0:2], LAM[:, :], SPT[:, 4:6], ALU.max).then_inc(lam_s, 1)
            dve.wait_ge(lam_s, 2)
            z, w, w2, acc = SPT[:, 2:4], SPT[:, 6:8], SPT[:, 12:14], SPT[:, 14:16]
            link(dve.tensor_scalar(w, z, 2.0, None, ALU.add))
            link(dve.reciprocal(w, w))
            link(dve.tensor_tensor(w, z, w, ALU.mult))
            link(dve.tensor_tensor(w2, w, w, ALU.mult))
            link(dve.tensor_scalar(acc, w2, 1.0 / 17, 1.0 / 15, ALU.mult, ALU.add))
            for odd in (13, 11, 9, 7, 5, 3, 1):
                link(dve.tensor_tensor(acc, acc, w2, ALU.mult))
                link(dve.tensor_scalar(acc, acc, 1.0 / odd, None, ALU.add))
            link(dve.tensor_tensor(acc, acc, w, ALU.mult))
            link(dve.tensor_scalar(acc, acc, 2.0, None, ALU.mult))
            link(dve.scalar_tensor_tensor(acc, SPT[:, 4:6], 0.0, acc, ALU.max, ALU.add))
            link(dve.tensor_scalar(SPT[:, 8:10], acc, LRU_C, None, ALU.mult))
            dve.tensor_scalar(SPT[:, 10:12], SPT[:, 8:10], -1.0, None, ALU.mult).then_inc(lam_done, 1)

            conv(0)
            conv(1)
            dve.wait_ge(gate_rows, 4)
            dve.wait_ge(lf_t, 1)
            dve.wait_ge(rs_set, 3)
            link(dve.scalar_tensor_tensor(ROW_LF, ROW_F, 0.0, ROW_T, ALU.min, ALU.subtract))
            dve.tensor_tensor_scan(ROW_B, ROW_RS, ROW_LF, 0.0, ALU.mult, ALU.add)
            link(dve.tensor_tensor_scan(ROW_M, ROW_LF, ROW_I, 0.0, ALU.add, ALU.max))
            link(dve.tensor_tensor(ROW_A, ROW_B, ROW_M, ALU.subtract))
            dve.tensor_tensor(ROWS4[0:MLH, :], ROW_I, ROW_B, ALU.subtract).then_inc(rows_done, 1)
            chunks = lambda r: r.rearrange("p (c n) -> p c n", c=NT)
            dve.memset(MPV[:, 0:1], 0.0)
            link(dve.tensor_copy(MPV[:, 1:NT].unsqueeze(2), chunks(ROW_M)[:, 0:NT - 1, P - 1:P]))
            dve.wait_ge(rows_done, 1)
            dve.tensor_tensor(chunks(ROW_T), chunks(ROW_A), MPV[:, :].unsqueeze(2).broadcast_to([MLH, NT, P]), ALU.add)
            link(dve.tensor_tensor(chunks(ROW_T2), chunks(ROWS4[0:MLH, :]), chunks(ROW_A)[:, :, P - 1:P].broadcast_to([MLH, NT, P]), ALU.add))
            dve.tensor_tensor(MPV[:, :].unsqueeze(2), MPV[:, :].unsqueeze(2), chunks(ROW_A)[:, :, P - 1:P], ALU.add).then_inc(rows_pre, 1)

            col = COL[:, :].rearrange("p (i k h) -> p i k h", i=NT, k=4)
            for half in range(2):
                dve.wait_ge(cols_ps, half + 1)
                for q in range(4):
                    ins = dve.tensor_copy(col[:, 4 * half + q], ps[half][:, q * P:(q + 1) * P].rearrange("p (k n) -> p k n", k=4)[:, :, 0:MLH])
                ins.then_inc(cols_sb, 1)
            dve.wait_ge(cols_ps, 3)
            dve.tensor_copy(DECB[:, :], ps[2][:, 0:MLH * NT]).then_inc(cols_sb, 1)
            dve.wait_ge(cols_sb, 3)

            def lru(f):
                XC, R, IV, T, D1 = LT[f]
                dve.wait_ge(lru_a, 2 * f + 2)
                link(dve.tensor_scalar(D1, T, 1.0, None, ALU.add))
                link(dve.reciprocal(D1, D1))
                dve.scalar_tensor_tensor(T, T, 2.0, D1, ALU.mult, ALU.mult).then_inc(lru_ratio, 1)
                link(dve.tensor_tensor(IV, IV, XC, ALU.mult))
                dve.wait_ge(lru_root, f + 1)
                link(dve.tensor_tensor(IV, IV, T, ALU.mult))
                link(dve.tensor_tensor_scan(XC, R, IV, 0.0, ALU.mult, ALU.add))
                link(dve.tensor_tensor(RXP[:, f, 3:3 + S], XC, RG[:, f, :], ALU.mult))
                dve.tensor_tensor(T, RXP[:, f, 3:3 + S], RXP[:, f, 3:3 + S], ALU.mult).then_inc(yr_sq, 1)

            lru(0)
            lru(1)

            dve.wait_ge(yr_rstd, 2)
            for f in range(2):
                ins = dve.scalar_tensor_tensor(RXP[:, f, 3:3 + S], RXP[:, f, 3:3 + S], GLRU[:, f:f + 1], LT[0][1], ALU.mult, ALU.mult)
            ins.then_inc(yr_done, 1)

            heads = lambda a, n: a.rearrange("p (h n) -> p h n", n=n)

            def decay_args(c):
                dve.wait_ge(db_ps, c + 1)
                if c >= 2:
                    dve.wait_ge(w_ready, c - 1)
                dve.tensor_tensor(heads(DSB[c % 2], P), heads(ps[0][:, :], P), TMASK[:, :].unsqueeze(1).broadcast_to([P, MLH, P]), ALU.add).then_inc(d_ready, 1)

            def weigh(c):
                dve.wait_ge(st_ps, c + 1)
                dve.wait_ge(w_ready, c + 1)
                if c >= 2:
                    dve.wait_ge(intra_ps, c - 1)
                for par in range(2):
                    ins = dve.tensor_tensor(heads(PWB[c % 2], P)[:, par::2, :], heads(ps[1 + par][:, 0:2 * P], P), heads(WSB[c % 2], P)[:, par::2, :], ALU.mult)
                ins.then_inc(pw_ready, 1)

            dve.wait_ge(yr_done, 1)
            decay_args(0)
            weigh(0)
            for c in range(NT):
                dve.wait_ge(upd_ps, c + 1)
                dve.wait_ge(inter_ps, c + 1)
                for h in range(MLH):
                    par, m = h % 2, h // 2
                    r = slice(64 * par, 64 * par + 64)
                    cs = CST[r, m * VA:(m + 1) * VA]
                    ins = dve.scalar_tensor_tensor(cs, cs, DECB[r, h * NT + c:h * NT + c + 1],
                                                   ps[6][r, (2 * m + par) * VA:(2 * m + par + 1) * VA], ALU.mult, ALU.add)
                ins.then_inc(state_ready, 1)
                if c + 1 < NT:
                    decay_args(c + 1)
                dve.wait_ge(intra_ps, c + 1)
                dve.wait_ge(inter_sb, c + 1)
                dve.tensor_tensor(NUM[c % 2], ps[3][:, 0:MLH * VA], INT[c % 2], ALU.add).then_inc(num_ready, 1)
                dve.wait_ge(num_ready, c + 1)
                num = heads(NUM[c % 2], VA)
                h4 = heads(OTOK[:, c, :], MLD)
                dve.tensor_tensor(h4, h4, num[:, :, 0:MLD], ALU.mult)
                link(dve.scalar_tensor_tensor(DEN[:, :].unsqueeze(2), num[:, :, MLD:VA], -1.0, num[:, :, MLD:VA], ALU.mult, ALU.max))
                link(dve.tensor_tensor(DEN[:, :], DEN[:, :], col[:, c, 3, :], ALU.max))
                link(dve.reciprocal(DEN[:, :], DEN[:, :]))
                dve.tensor_tensor(h4, h4, DEN[:, :].unsqueeze(2).broadcast_to([P, MLH, MLD]), ALU.mult).then_inc(h_done, 1)
                if c + 1 < NT:
                    weigh(c + 1)

            n = NT * MLH
            groups = OTOK.rearrange("p i (h n) -> p (i h) n", n=MLD)
            dve.wait_ge(mh_sq, 1)
            dve.tensor_reduce(MSS[:, 0:n], SQ.rearrange("p (q n) -> p q n", n=MLD), AX.X, ALU.add).then_inc(mh_ss, 1)
            for i in range(NT):
                if i == 0:
                    dve.wait_ge(mh_rstd, 1)
                    link(dve.tensor_tensor(groups, groups, MSS[:, 2 * n:3 * n].unsqueeze(2).broadcast_to([P, n, MLD]), ALU.mult))
                if i == 1:
                    dve.tensor_tensor(OTOK, OTOK, GML[:, :].unsqueeze(1).broadcast_to([P, NT, MLW]), ALU.mult).then_inc(ymt_ready, 1)
                dve.wait_ge(qt_ps, 2 * i + 2)
                dve.tensor_copy(QT[0:QK, i, 4:8, :], ps[7][0:QK, :].rearrange("p (h n) -> p h n", h=4)).then_inc(qt_dve, 1)

            def row_max(n):
                i, h = ATT[n]
                L = (i + 1) * P
                dve.wait_ge(s_ps, n + 1)
                b, o = (i * P) // 512, (i * P) % 512
                diag = ps[2 * (n % 2) + b][:, o:o + P]
                link(dve.tensor_tensor(diag, diag, CMASK[:, :], ALU.add))
                nb = (L + 511) // 512
                for b in range(nb):
                    w = min(512, L - 512 * b)
                    dst = (NMX if b == 0 else RIN)[:, n:n + 1]
                    ins = dve.tensor_reduce(dst, ps[2 * (n % 2) + b][:, 0:w], AX.X, ALU.max, negate=True)
                if nb == 2:
                    link(ins)
                    ins = dve.tensor_tensor(NMX[:, n:n + 1], NMX[:, n:n + 1], RIN[:, n:n + 1], ALU.min)
                ins.then_inc(s_max, 1)

            def probs_evac(n):
                i, h = ATT[n]
                for gg in range(G0[n], G0[n + 1]):
                    if gg % 2 == 1:
                        dve.wait_ge(pt_ps, gg + 1)
                        if gg >= 4:
                            dve.wait_ge(pv_ps, GROUPS[gg - 4][0] + 1)
                        w = P * min(4, i + 1 - 4 * GROUPS[gg][1])
                        dve.tensor_copy(PTB[gg % 4][:, 0:w], ps[5][:, 0:w]).then_inc(pt_dve, 1)

            def normalise(n):
                i, h = ATT[n]
                dve.wait_ge(p_ready, n + 1)
                if i >= 4:
                    link(dve.tensor_tensor(RSM[:, n:n + 1], RSM[:, n:n + 1], RIN[:, n:n + 1], ALU.add))
                link(dve.reciprocal(RIN[:, n:n + 1], RSM[:, n:n + 1]))
                dve.wait_ge(pv_ps, n + 1)
                dve.tensor_scalar(YA[:, i, h * VD:(h + 1) * VD], ps[6][:, 0:VD], RIN[:, n:n + 1], None, ALU.mult).then_inc(pv_sb, 1)

            def residual(t, b):
                i = ORDER[t]
                dve.wait_ge(o_ps, 2 * t + b + 1)
                dve.wait_ge(xr_in[t % 2], 16 * (t // 2 + 1))
                s = slice(b * 512, (b + 1) * 512)
                dve.tensor_tensor(X2[:, i, s], ps[7][:, :], XR[t % 2][:, s], ALU.add).then_inc(x2_half if b == 0 else x2_ready, 1)

            def between(n):
                for t, off in due(n):
                    if off == DUE["scale"]:
                        dve.wait_ge(ya_rstd, t + 1)
                        dve.scalar_tensor_tensor(YA[:, ORDER[t], :], YA[:, ORDER[t], :], ST2[:, ORDER[t]:ORDER[t] + 1], GMLA[:, :], ALU.mult, ALU.mult).then_inc(ya_ready, 1)
                    for b in range(2):
                        if off == DUE[f"add{b}"]:
                            residual(t, b)

            row_max(0)
            for n in range(LAST):
                if n + 1 < N:
                    row_max(n + 1)
                if n < N:
                    probs_evac(n)
                if 1 <= n <= N:
                    normalise(n - 1)
                between(n)

            def norm2(j):
                i = ORDER[j]
                dve.wait_ge(x2_rstd, j + 1)
                if j >= NX:
                    dve.wait_ge(x2n_out[j % NX], 16 * (j // NX))
                    dve.wait_ge(x2nt_ps, 2 * (j - NX + 1))
                dve.scalar_tensor_tensor(X2N[j % NX], X2[:, i, :], ST2[:, NT + i:NT + i + 1], G2B, ALU.mult, ALU.mult).then_inc(x2n_ready, 1)

            def turn_evac(j):
                dve.wait_ge(x2nt_ps, 2 * j + 2)
                if j >= 2:
                    dve.wait_ge(r_ps, j - 1)
                dve.tensor_copy(X2NT[j % 2][:, 4:8, :], ps[2 * (j % 2) + 1][:, :].rearrange("p (k n) -> p k n", k=4)).then_inc(x2nt_dve, 1)

            def router_evac(j):
                i = ORDER[j]
                dve.wait_ge(r_ps, j + 1)
                dve.tensor_tensor(LG[:, i * 36:(i + 1) * 36], ps[4 + j % 2][:, 0:36], BRT[:, :], ALU.add).then_inc(r_sb, 1)

            dve.wait_ge(g2_in, 16)
            norm2(0)
            for j in range(NT):
                if j + 1 < NT:
                    norm2(j + 1)
                turn_evac(j)
                if j >= 1:
                    router_evac(j - 1)
            router_evac(NT - 1)
            dve.wait_ge(r_sb, NT)

            dve.wait_ge(iota_set, 1)
            lg = LG[:, :].rearrange("p (i n) -> p i n", i=NT)
            gl = lg[:, :, 0:NG]
            el = lg[:, :, NG:].rearrange("p i (g j) -> p i g j", g=NG)

            def rb(a, n):
                return RB[:, a * NT:(a + n) * NT].rearrange("p (i n) -> p i n", i=NT)

            gmax, gd, gex = rb(0, 1), rb(4, 4), rb(8, 4)
            big = [RA[:, q * NT * NE:(q + 1) * NT * NE] for q in range(6)]
            rev4 = IOT[:, 0:NG]
            rev8 = IOT[:, 4:4 + EPG]

            def first_max(dst, vals, n, rev, m, key):
                link(dve.tensor_tensor(key, vals, m.broadcast_to([P, NT, n]), ALU.is_equal))
                link(dve.tensor_tensor(key, key, rev.unsqueeze(1).broadcast_to([P, NT, n]), ALU.mult))
                link(dve.tensor_reduce(rb(15, 1), key, AX.X, ALU.max))
                link(dve.tensor_tensor(dst, key, rb(15, 1).broadcast_to([P, NT, n]), ALU.is_equal))

            link(dve.tensor_reduce(gmax, gl, AX.X, ALU.max))
            link(dve.tensor_tensor(gd, gl, gmax.broadcast_to([P, NT, NG]), ALU.subtract))
            dve.nop().then_inc(rt_a, 1)
            ohg = rb(16, 4)
            first_max(ohg, gl, NG, rev4, gmax, rb(20, 4))
            prod = big[5].rearrange("p (i g j) -> p i g j", i=NT, g=NG)
            sel = big[4][:, 0:NT * EPG].rearrange("p (i j) -> p i j", i=NT)
            for g in range(NG):
                ins = dve.tensor_tensor(prod[:, :, g, :], el[:, :, g, :], ohg[:, :, g:g + 1].broadcast_to([P, NT, EPG]), ALU.mult)
            link(ins)
            link(dve.tensor_tensor(sel, prod[:, :, 0, :], prod[:, :, 1, :], ALU.add))
            link(dve.tensor_tensor(sel, sel, prod[:, :, 2, :], ALU.add))
            link(dve.tensor_tensor(sel, sel, prod[:, :, 3, :], ALU.add))
            e8 = [big[4][:, (1 + q) * NT * EPG:(2 + q) * NT * EPG].rearrange("p (i j) -> p i j", i=NT) for q in range(3)]
            m1, m2 = rb(1, 1), rb(2, 1)
            link(dve.tensor_reduce(m1, sel, AX.X, ALU.max))
            first_max(e8[0], sel, EPG, rev8, m1, e8[2])
            link(dve.scalar_tensor_tensor(sel, e8[0], -BIG, sel, ALU.mult, ALU.add))
            link(dve.tensor_reduce(m2, sel, AX.X, ALU.max))
            first_max(e8[1], sel, EPG, rev8, m2, e8[2])
            link(dve.tensor_tensor(rb(12, 1), m2, m1, ALU.subtract))
            dve.nop().then_inc(rt_a, 1)
            oh = [big[1], big[2]]
            for q in range(2):
                ohq = oh[q].rearrange("p (i g j) -> p i g j", i=NT, g=NG)
                for g in range(NG):
                    ins = dve.tensor_tensor(ohq[:, :, g, :], e8[q], ohg[:, :, g:g + 1].broadcast_to([P, NT, EPG]), ALU.mult)
            link(ins)
            dve.tensor_tensor(big[0], oh[0], oh[1], ALU.add).then_inc(mask_ready, 1)
            dve.wait_ge(rt_b, 2)
            link(dve.tensor_reduce(rb(3, 1), gex, AX.X, ALU.add))
            link(dve.tensor_scalar(rb(14, 1), rb(13, 1), 1.0, None, ALU.add))
            link(dve.tensor_tensor(rb(14, 1), rb(14, 1), rb(3, 1), ALU.mult))
            w0, w1 = WTS[:, 0:NT], WTS[:, NT:2 * NT]
            link(dve.reciprocal(w0, RB[:, 14 * NT:15 * NT]))
            link(dve.tensor_tensor(w1, w0, RB[:, 13 * NT:14 * NT], ALU.mult))
            dve.wait_ge(pos_ps, 1)
            cnt = lambda q: CNT[:, q * NE:(q + 1) * NE]
            link(dve.tensor_copy(cnt(0), ps[1][:, 0:NE]))
            link(dve.tensor_scalar(cnt(1), cnt(0), float(CAP), None, ALU.is_gt))
            for j in range(2, S // CAP):
                link(dve.scalar_tensor_tensor(cnt(1), cnt(0), float(CAP * j), cnt(1), ALU.is_gt, ALU.add))
            link(dve.memset(cnt(4), 1.0))
            link(dve.tensor_tensor_scan(cnt(2), cnt(4), cnt(1), 0.0, ALU.mult, ALU.add))
            link(dve.tensor_tensor(cnt(3), cnt(2), cnt(1), ALU.subtract))
            link(dve.scalar_tensor_tensor(cnt(3), cnt(3), float(NMAIN - 1), IOT[:, NE:2 * NE], ALU.add, ALU.subtract))
            link(dve.tensor_scalar(cnt(3), cnt(3), float(CAP), None, ALU.mult))
            link(dve.tensor_scalar(cnt(5), IOT[:, NE:2 * NE], float(CAP), None, ALU.mult))
            link(dve.tensor_copy(big[3], ps[0][:, 0:NT * NE]))
            b3 = big[3].rearrange("p (i e) -> p i e", i=NT)
            b4 = big[4].rearrange("p (i e) -> p i e", i=NT)
            link(dve.tensor_scalar(big[4], big[3], float(CAP), None, ALU.is_ge))
            link(dve.tensor_tensor(b4, b4, cnt(3).unsqueeze(1).broadcast_to([P, NT, NE]), ALU.mult))
            link(dve.tensor_tensor(big[3], big[3], big[4], ALU.add))
            link(dve.tensor_tensor(b3, b3, cnt(5).unsqueeze(1).broadcast_to([P, NT, NE]), ALU.add))
            for q in range(2):
                link(dve.tensor_tensor(big[5], oh[q], big[3], ALU.mult))
                link(dve.tensor_reduce(SLOTF[:, q * NT:(q + 1) * NT], big[5].rearrange("p (i e) -> p i e", i=NT), AX.X, ALU.add))
            dve.tensor_copy(SLOT[:, :], SLOTF[:, :]).then_inc(slot_ready, 1)
            for b in range(NOVER):
                link(dve.tensor_scalar(cnt(6)[0:1, :], cnt(2)[0:1, :], float(b), None, ALU.is_le))
                link(dve.tensor_reduce(cnt(7)[0:1, b:b + 1], cnt(6)[0:1, :], AX.X, ALU.add))
            link(dve.tensor_scalar(cnt(7)[0:1, 0:NOVER], cnt(7)[0:1, 0:NOVER], float(NE - 1), None, ALU.min))
            dve.tensor_copy(OVE[0:1, 0:NOVER], cnt(7)[0:1, 0:NOVER])
            link(dve.tensor_copy(OVE[0:1, NOVER:NOVER + 1], cnt(2)[0:1, NE - 1:NE]))
            dve.wait_ge(ids_ps, 1)
            dve.tensor_copy(IDX[:, :], ps[2][:, 0:NBLK]).then_inc(idx_ready, 1)

            def rows_evac(u, done):
                dve.wait_ge(xgt_ps, done)
                dve.tensor_copy(XGT[u][:, 4:8, :], ps[1][:, :].rearrange("p (k n) -> p k n", k=4)).then_inc(xgt_dve, 1)

            def swiglu(u, ups, done):
                dve.wait_ge(gu_ps, ups)
                dve.wait_ge(sg_ready, done)
                dve.tensor_tensor(HT[u].rearrange("p k n -> p (k n)"), SG, ps[3 + 2 * u][:, 0:2 * P], ALU.mult).then_inc(h_ready, 1)

            def y_evac(done):
                dve.wait_ge(y_ps, done)
                dve.tensor_copy(YB[1], ps[7][:, :]).then_inc(y_dve, 1)

            dve.sem_inc(xgt_dve, 1)
            dve.sem_inc(y_dve, 1)
            dve.sem_inc(h_ready, 1)
            rows_evac(0, 2)
            with dve.Fori(0, NMAIN // NW) as it:
                for j in range(NW):
                    u = j % 2
                    swiglu(u, it * (2 * NW) + (2 * j + 2), it * NW + (j + 1))
                    rows_evac(1 - u, it * (2 * NW) + (2 * j + 4))
                    dve.wait_ge(y_out[1], it * (16 * NW) + 16 * (j + 1))
                    y_evac(it * NW + (j + 1))
            nover = dve.value_load(OVE[0:1, NOVER:NOVER + 1], min_val=0, max_val=NOVER)
            with dve.Fori(0, NOVER) as b:
                with dve.If(b < nover):
                    rows_evac(0, b * 2 + (2 * NMAIN + 4))
                    swiglu(0, b * 2 + (2 * NMAIN + 2), b + (NMAIN + 1))
                    dve.wait_ge(y_out[1], b * 16 + 16 * (NMAIN + 1))
                    y_evac(b + (NMAIN + 1))
                with dve.Else():
                    dve.nop()

            def combine(i):
                dve.wait_ge(yg_in[i % NY], 32 * (i // NY + 1))
                link(dve.scalar_tensor_tensor(X2[:, i, :], YG[i % NY][0], WTS[:, i:i + 1], X2[:, i, :], ALU.mult, ALU.add))
                dve.scalar_tensor_tensor(X2[:, i, :], YG[i % NY][1], WTS[:, NT + i:NT + i + 1], X2[:, i, :], ALU.mult, ALU.add).then_inc(f_sum, 1)

            def final_norm(i):
                dve.wait_ge(f_rstd, i + 1)
                if i >= 2:
                    dve.wait_ge(out_done[i % 2], 16 * (i // 2))
                dve.scalar_tensor_tensor(OUT[i % 2], X2[:, i, :], ST2[:, i:i + 1], GFB, ALU.mult, ALU.mult).then_inc(f_ready, 1)

            combine(0)
            dve.wait_ge(gf_in, 16)
            for i in range(NT):
                if i + 1 < NT:
                    combine(i + 1)
                final_norm(i)

        @block.gpsimd
        def _(pool):
            link = chained(pool, pool_chain)
            sel = SEL[:, :].rearrange("p (h n) -> p h n", h=MLH)
            pool.memset(BD[:, :], 0.0)
            pool.memset(ONES[:, :], 1.0)
            pool.memset(KRP[0], 0.0)
            pool.memset(KRP[1], 0.0)
            pool.memset(IDENT[:, :], 0.0)
            pool.memset(CMASK[:, :], 0.0)
            pool.memset(TMASK[:, :], 0.0)
            pool.memset(SEL[:, :], 0.0)
            link(pool.memset(TRI[:, :], 0.0))
            pool.affine_select(out=IDENT[:, :], in_=IDENT[:, :], compare_op=ALU.not_equal, fill=1.0, base=0,
                               pattern=[[-1, P]], channel_multiplier=1).then_inc(masks_set, 1)
            pool.affine_select(out=CMASK[:, :], in_=CMASK[:, :], compare_op=ALU.is_ge, fill=-BIG, base=0,
                               pattern=[[-1, P]], channel_multiplier=1).then_inc(masks_set, 1)
            pool.affine_select(out=TMASK[:, :], in_=TMASK[:, :], compare_op=ALU.is_ge, fill=-BIG, base=0,
                               pattern=[[1, P]], channel_multiplier=-1).then_inc(masks_set, 1)
            pool.affine_select(out=TRI[:, :], in_=TRI[:, :], compare_op=ALU.is_ge, fill=1.0, base=0,
                               pattern=[[-1, P]], channel_multiplier=1).then_inc(masks_set, 1)
            pool.affine_select(out=sel, in_=sel, compare_op=ALU.not_equal, fill=1.0, base=0,
                               pattern=[[-1, MLH], [0, P]], channel_multiplier=1).then_inc(masks_set, 1)
            link(pool.memset(SPT[:, :], 0.0))
            link(pool.iota(IOT[:, 0:4], pattern=[[-1, 4]], base=NG, channel_multiplier=0, allow_small_or_imprecise_dtypes=True))
            link(pool.iota(IOT[:, 4:12], pattern=[[-1, 8]], base=EPG, channel_multiplier=0, allow_small_or_imprecise_dtypes=True))
            link(pool.iota(IOT[:, NE:2 * NE], pattern=[[1, NE]], base=0, channel_multiplier=0, allow_small_or_imprecise_dtypes=True))
            link(pool.iota(TOK[:, :], pattern=[[P, NT]], base=0, channel_multiplier=1, allow_small_or_imprecise_dtypes=True))
            link(pool.memset(IDR[:, :], float(S)))
            pool.nop().then_inc(iota_set, 1)
            pool.dma_start(ids_d.rearrange("(b n) o -> b (n o)", b=NBLK), IDR[:, :]).then_inc(ids_init, 16)
            pool.memset(ZERO, 0.0).then_inc(zero_set, 1)

            pool.wait_ge(const_in, 16 * NC_)
            for i in range(NT):
                pool.wait_ge(proj_act, job("T", i, 2) + 1)
                if i >= 2:
                    pool.wait_ge(latt_ps, i - 1)
                t1, t2 = CQR[i % 2][:, QL + KVL:QL + KVL + 16], CQR[i % 2][:, QL + KVL + 16:]
                cs, sn = COS[:, i * 16:(i + 1) * 16], SIN[:, i * 16:(i + 1) * 16]
                a, b, c, d = (RTMP[:, q * 16:(q + 1) * 16] for q in range(4))
                pool.tensor_tensor(a, t1, cs, ALU.mult)
                pool.tensor_tensor(b, t2, sn, ALU.mult)
                pool.tensor_tensor(c, t1, sn, ALU.mult)
                link(pool.tensor_tensor(d, t2, cs, ALU.mult))
                pool.tensor_tensor(KRP[i % 2][:, NOPE:NOPE + 16], a, b, ALU.subtract)
                pool.tensor_tensor(KRP[i % 2][:, NOPE + 16:QK], c, d, ALU.add).then_inc(krp_ready, 1)
                pool.wait_ge(krp_ready, i + 1)
            pool.wait_ge(proj_ps, NPROJ)
            pool.memset(ROWS4, 0.0).then_inc(rs_set, 1)
            link(pool.memset(ROW_RS, 1.0))
            pool.memset(ROW_RS.rearrange("p (c n) -> p c n", c=NT)[:, :, 0:1], 0.0).then_inc(rs_set, 2)
            pool.wait_ge(proj_act, NPROJ)
            for f in range(2):
                XC, R, IV, T, D1 = LT[f]
                g = RG[:, f, :]
                link(pool.tensor_tensor(T, g, g, ALU.mult))
                link(pool.tensor_scalar(T, T, GELU_A, 1.0, ALU.mult, ALU.add))
                pool.tensor_tensor(T, T, g, ALU.mult).then_inc(gelu_arg, 1)
            for f in range(2):
                pool.wait_ge(gelu_sig, f + 1)
                pool.tensor_tensor(RG[:, f, :], RG[:, f, :], LT[f][4], ALU.mult).then_inc(gelu_done, 1)
            pool.wait_ge(latt_sb, NT)
            pool.wait_ge(gelu_done, 2)
            pool.tensor_copy(KT[NOPE:QK, :, :], KPT[NOPE:QK, :].unsqueeze(1).broadcast_to([ROPE, H, S])).then_inc(kr_sb, 1)
            pool.wait_ge(kr_sb, 1)
            pool.wait_ge(cols_sb, 3)
            col = COL[:, :].rearrange("p (i k h) -> p i k h", i=NT, k=4)
            for c in range(NT):
                if c >= 2:
                    pool.wait_ge(upd_ps, c - 1)
                if c == 0:
                    pool.wait_ge(yr_done, 1)
                pool.tensor_tensor(KSB[c % 2].rearrange("p (h n) -> p h n", h=MLH),
                                   KTOK[:, c, :].rearrange("p (h n) -> p h n", h=MLH),
                                   col[:, c, 2, :].unsqueeze(2).broadcast_to([P, MLH, MLD]), ALU.mult).then_inc(ks_ready, 1)
            for i in range(NT):
                pool.wait_ge(q_sb, i + 1)
                q = QTOK[i % 2]
                t1, t2 = q[:, :, NOPE:NOPE + 16], q[:, :, NOPE + 16:QK]
                cs = COS[:, i * 16:(i + 1) * 16].unsqueeze(1).broadcast_to([P, H, 16])
                sn = SIN[:, i * 16:(i + 1) * 16].unsqueeze(1).broadcast_to([P, H, 16])
                a, b, c, d = (RTMP[:, w * 128:(w + 1) * 128].rearrange("p (h n) -> p h n", h=H) for w in range(4))
                pool.tensor_tensor(a, t1, cs, ALU.mult)
                pool.tensor_tensor(b, t2, sn, ALU.mult)
                pool.tensor_tensor(c, t1, sn, ALU.mult)
                link(pool.tensor_tensor(d, t2, cs, ALU.mult))
                pool.tensor_tensor(t1, a, b, ALU.subtract)
                pool.tensor_tensor(t2, c, d, ALU.add).then_inc(q_rope, 1)
                pool.wait_ge(q_rope, i + 1)
            pool.wait_ge(ids_init, 16)
            pool.wait_ge(slot_ready, 1)
            for q in range(2):
                for i in range(NT):
                    pool.indirect_dma_start(ids_d, bass.IndirectOffsetOnAxis(ap=SLOT[:, q * NT + i:q * NT + i + 1], axis=0),
                                            TOK[:, i:i + 1], None).then_inc(ids_out, 16)
            pool.wait_ge(ids_out, 16 * 2 * NT)
            pool.dma_start(IDR[:, :], ids_d.rearrange("(b n) o -> b (n o)", b=NBLK)).then_inc(ids_in, 16)
            pool.wait_ge(yr_done, 1)
            pool.wait_ge(x2_ready, NT)
            pool.memset(XG[0], 0.0).then_inc(xg_set, 1)
            pool.memset(XG[1], 0.0).then_inc(xg_set, 1)
            pool.wait_ge(xg_set, 2)
            pool.wait_ge(idx_ready, 1)
            for j in range(NX):
                pool.wait_ge(x2n_out[j], 16 * (NT // NX))

            def stand():
                pool.sem_inc(pool_waits, 1)

            def gather(u, col, done):
                pool.tensor_copy(IDXC[u][:, :], col).then_inc(list_ready, 1)
                pool.wait_ge(list_ready, done)
                stand()
                col = IDXC[u][:, :]
                pool.indirect_dma_start(XG[u], None, x2n_d, bass.IndirectOffsetOnAxis(ap=col, axis=0),
                                        bounds_check=S - 1, oob_is_err=False).then_inc(xg_in[u], 16)

            gather(0, IDX[:, 0:1], 1)
            gather(1, IDX[:, 1:2], 2)
            with pool.Fori(0, NMAIN // NW) as it:
                for j in range(NW):
                    u = j % 2
                    pool.wait_ge(xgt_ps, it * (2 * NW) + (2 * j + 2))
                    stand()
                    gather(u, IDX[:, bass.ds(it * NW + (j + 2), 1)], it * NW + (j + 3))
            nover = pool.value_load(OVE[0:1, NOVER:NOVER + 1], min_val=0, max_val=NOVER)
            with pool.Fori(0, NOVER) as b:
                with pool.If(b < nover):
                    pool.wait_ge(xgt_ps, b * 2 + (2 * NMAIN + 2))
                    stand()
                    gather(0, IDX[:, bass.ds(b + NMAIN, 1)], b + (NMAIN + 3))
                with pool.Else():
                    pool.nop()
            total = pool.snap(nover * 16 + 16 * (NMAIN + 1))
            pool.wait_ge(y_out[0], total)
            pool.wait_ge(y_out[1], total)
            stand()
            for i in range(NT):
                if i >= NY:
                    pool.wait_ge(f_sum, i - NY + 1)
                for q in range(2):
                    pool.indirect_dma_start(YG[i % NY][q], None, y_d, bass.IndirectOffsetOnAxis(ap=SLOT[:, q * NT + i:q * NT + i + 1], axis=0)).then_inc(yg_in[i % NY], 16)


NAMES = ["x", "norm1_g", "w_in", "ml_i_bias", "ml_f_bias", "ml_norm_g", "conv_w", "conv_b", "lru_w_r", "lru_b_r",
         "lru_w_i", "lru_b_i", "lru_lambda", "lru_norm_g", "q_norm_g", "w_uq", "kv_norm_g", "w_ukv", "mla_norm_g",
         "w_out", "norm2_g", "w_group", "b_group", "w_expert", "b_expert", "w_gate", "w_up", "w_down", "final_norm_g"]


def kernel(**inputs):
    import concourse.bacc as bacc
    from concourse.bass_utils import run_bass_kernel_spmd

    nc = bacc.Bacc("TRN2", target_bir_lowering=False, num_devices=1)
    inv = (1.0 / (np.float32(10000.0) ** (np.arange(0, ROPE, 2, dtype=np.float32) / np.float32(ROPE)))).astype(np.float32)
    ang = np.arange(S, dtype=np.float32)[:, None] * inv[None, :]
    arrays = {"rope_cos": np.cos(ang), "rope_sin": np.sin(ang)}
    arrays.update({name: np.ascontiguousarray(inputs[name]) for name in NAMES})
    t = {name: nc.dram_tensor(f"in_{name}", a.shape, mybir.dt.from_np(a.dtype), kind="ExternalInput").ap()
         for name, a in arrays.items()}
    t["out"] = nc.dram_tensor("out_0", (1, S, D), F32, kind="ExternalOutput").ap()
    build(nc, t)
    r = run_bass_kernel_spmd(nc, [{f"in_{name}": a for name, a in arrays.items()}], core_ids=[0])
    return r.results[0]["out_0"]
```

```python
from contextlib import ExitStack

import numpy as np
import concourse.bass as bass
from concourse import mybir

F32 = mybir.dt.float32
BF16 = mybir.dt.bfloat16
I32 = mybir.dt.int32
ALU = mybir.AluOpType
ACT = mybir.ActivationFunctionType
AX = mybir.AxisListType

P = 128
D = 1024
S = 1024
NT = S // P
KD = D // P
MLH, MLD = 4, 64
MLW = MLH * MLD
VA = MLD + 1
LRU = 256
CONV = 4
H, NOPE, ROPE, VD = 8, 64, 32, 64
QK = NOPE + ROPE
QL, KVL = 256, 128
NG, EPG = 4, 8
NE = NG * EPG
DE = 256
EPS = 1e-6
BIG = 1.0e30
SCALE = float(QK) ** -0.5
LRU_C = 8.0

C_MQ, C_MK, C_MO = 0, 256, 768
C_RX, C_RG, C_CQ = 1032, 1288, 1544
N_IN = 1960
N_LAT = QL + KVL + ROPE

CAP = P
NMAIN = NE
NOVER = 2 * S // P - 1
NBLK = NMAIN + NOVER
NW = 4

GELU_S = 1.5957691216057308
GELU_A = 0.044715


def build(nc, t):
    ctx = ExitStack()
    with ctx:
        def sb(name, cols, dt=F32, parts=P):
            return ctx.enter_context(nc.sbuf_tensor(name, [parts, cols], dt))

        def sem(name):
            return ctx.enter_context(nc.semaphore(name))

        mem = sb("mem", 45696)

        def at(a, n, parts=P, p0=0):
            return mem[p0:p0 + parts, a:a + n]

        W_IN = at(0, KD * N_IN).rearrange("p (k n) -> p k n", k=KD)
        HNT = at(15680, 8192).rearrange("p (s k n) -> p s k n", s=2, k=KD)
        R2 = 24576
        KTOK = at(R2, 2048).rearrange("p (i n) -> p i n", i=NT)
        VAUG = at(R2 + 2048, 2080).rearrange("p (i h n) -> p i h n", i=NT, h=MLH)
        OTOK = at(R2 + 4128, 2048).rearrange("p (i n) -> p i n", i=NT)
        MQT = at(R2 + 6176, 2048).rearrange("p (m n) -> p m n", m=2)
        R3 = R2 + 8224
        CQT = at(R3, 2048).rearrange("p (m n) -> p m n", m=2)
        CKVT = at(R3 + 2048, 1024)
        KPT = at(R3 + 3072, 1024)
        R4 = R3 + 4096
        RXP = at(R4, 2 * (S + 3)).rearrange("p (m n) -> p m n", m=2)
        RG = at(R4 + 2054, 2048).rearrange("p (m n) -> p m n", m=2)
        R5 = R4 + 4102
        XB = [at(R5 + 1024 * j, 1024) for j in range(3)]
        CQR = [at(R5 + 3072 + N_LAT * j, N_LAT) for j in range(2)]
        KRP = [at(R5 + 3072 + 2 * N_LAT + QK * j, QK) for j in range(2)]
        ZERO = at(R5 + 4186, 512)
        LT = [[at(R5 + 1024 * f, 1024)] + [at(8192 + 5120 * f + 1024 * j, 1024) for j in range(5)] for f in range(2)]
        ROW_F = ROW_LF = ROW_T = at(15680, 1024, MLH)
        ROW_I = ROW_T2 = at(16704, 1024, MLH)
        ROW_L = ROW_RS = at(17728, 1024, MLH)
        ROWS4 = at(18752, 1024)
        ROW_M = at(R5 + 2048, 1024, MLH)
        ROW_B = at(R5 + 3072, 1024, MLH)
        KTM = at(20480, 2048).rearrange("p (m n) -> p m n", m=2)
        DSB, WSB, PWB = ([at(o + 512 * j, MLH * P) for j in range(2)] for o in (9216, 11264, 12288))
        KSB = [at(13312 + 256 * j, MLW) for j in range(2)]
        INT, NUM = ([at(13824 + 520 * q + 260 * j, MLH * VA) for j in range(2)] for q in range(2))
        SQ = at(8192, 2048)
        KT = at(0, 8192).rearrange("p (h n) -> p h n", h=H)
        QT = at(8192, 8192).rearrange("p (i h n) -> p i h n", i=NT, h=H)
        V = at(16384, 4096).rearrange("p (i h n) -> p i h n", i=NT, h=H)
        YA = at(20480, 4096).rearrange("p (i n) -> p i n", i=NT)
        W_UQ = at(R5, 1536).rearrange("p (k n) -> p k n", k=2)
        W_UKV = at(22528, 1024).rearrange("p (h n) -> p h n", h=H)
        YM = at(R5 + 2560, 2048).rearrange("p (m n) -> p m n", m=2)
        QTOK = [at(R4 + 2054 + 768 * j, 768).rearrange("p (h n) -> p h n", h=H) for j in range(2)]
        PB = [at(R3 + 1024 * j, 1024) for j in range(2)]
        PTB = [at(R3 + 2048 + 512 * j, 512) for j in range(4)]
        W_OUT = at(R2, 8192).rearrange("p (k n) -> p k n", k=KD)
        X2 = at(8192, 8192).rearrange("p (i n) -> p i n", i=NT)
        XR = [at(R4 + 2054 + 1024 * j, 1024) for j in range(2)]
        YAT = [at(R5 + 512 * j, 512) for j in range(2)]
        G2B = at(R5 + 1024, 1024)
        XNOFF = (19456, 23552, 18432, 22528, 17408, 21504, 19456, 23552)
        X2N = [at(o, 1024) for o in XNOFF]
        X2NT = [at(R3 + 1024 * j, 1024).rearrange("p (k n) -> p k n", k=KD) for j in range(2)]
        WOFF = (0, 16384, R2, R3)
        WGU = [at(o, 4096).rearrange("p (g k n) -> p g k n", g=2, k=KD) for o in WOFF]
        WDN = [at(o + 4096, 2048).rearrange("p (k n) -> p k n", k=2) for o in WOFF]
        E5 = R3 + 6144
        XG = [at(E5 + 1024 * j, 1024) for j in range(2)]
        XGT = [at(E5 + 2048 + 1024 * j, 1024).rearrange("p (k n) -> p k n", k=KD) for j in range(2)]
        SG = at(6144, 256)
        HT = [at(6400 + 256 * j, 256).rearrange("p (k n) -> p k n", k=2) for j in range(2)]
        YB = [at(6912 + 512 * j, 512) for j in range(2)]
        RA = at(E5 + 4096, 6 * NT * NE)
        NS = 2 * NT
        BGE = at(E5 + 4096 + 6 * NT * NE, NS * NBLK).rearrange("p (n b) -> p n b", n=NS)
        BEQ = at(E5 + 3072, NS * NBLK).rearrange("p (n b) -> p n b", n=NS)
        OHP = at(6144, NS * P).rearrange("p (n q) -> p n q", n=NS)
        NY = 4
        YG = [[at((0, 2048, 16384, 18432)[j] + 1024 * q, 1024) for q in range(2)] for j in range(NY)]
        OUT = [at(R2 + 1024 * j, 1024) for j in range(2)]

        IDENT = sb("ident", P)
        ONES = sb("ones", P)
        CMASK = sb("cmask", P)
        TMASK = sb("tmask", P)
        TRI = sb("tri", P)
        SEL = sb("sel", MLH * P, parts=MLH)
        GB = sb("gb", D)
        ROW_A = GB[0:MLH, :]
        COS = sb("cos", NT * 16)
        SIN = sb("sin", NT * 16)
        GQ = sb("gq", QL + KVL)
        GML = sb("gml", MLW)
        GMLA = sb("gmla", H * VD)
        GLRU = sb("glru", 2)
        CW = sb("cw", 2 * CONV)
        CB = sb("cb", 2)
        BR = sb("br", 2)
        BI = sb("bi", 2)
        LAM = sb("lam", 2)
        BGI = sb("bgi", 1, parts=MLH)
        BGF = sb("bgf", 1, parts=MLH)
        BD = sb("bd", 4 * P)
        WR = sb("wr", KD * 36)
        BRT = sb("brt", 36)
        EPSC = sb("epsc", 1)
        ONEC = sb("onec", 1)
        JUNK = sb("junk", D, BF16)
        ST1 = sb("st1", 2 * NT)
        ST2 = sb("st2", 4 * NT)
        GATES = sb("gates", NT * 8)
        RTMP = sb("rtmp", 4 * H * 16)
        SCM = RTMP[:, 0:NT * NE]
        SPT = sb("spt", 16)
        COL = sb("col", NT * 16)
        DEC = sb("dec", 8, parts=MLH)
        MPV = sb("mpv", 8, parts=MLH)
        DECB = sb("decb", MLH * NT)
        CST = sb("cst", 2 * VA)
        DEN = sb("den", MLH)
        MSS = sb("mss", 3 * NT * MLH)
        NMX = sb("nmx", 64)
        RSM = sb("rsm", 64)
        RIN = sb("rin", 64)
        LG = sb("lg", NT * 36)
        RB = sb("rb", 24 * NT)
        CNT = sb("cnt", 8 * NE)
        IOT = sb("iot", 4 * NE)
        SLOTF = sb("slotf", 2 * NT)
        SLOT = sb("slot", 2 * NT, I32)
        TOK = sb("tok", NT)
        WTS = sb("wts", 2 * NT)
        IOB = sb("iob", NBLK)
        IOP = sb("iop", P)
        TOKS = sb("toks", NT)
        PLACE = sb("place", 2 * NT)
        IDX = sb("idx", NBLK, I32)
        IDXC = [sb(f"idxc{j}", 1, I32) for j in range(2)]
        OVE = sb("ove", 32, I32, parts=1)

        ps = [ctx.enter_context(nc.psum_tensor(f"ps{b}", [P, 512], F32)) for b in range(8)]

        x2n_d = nc.dram_tensor("x2n_rows", [S, D], F32, kind="Internal").ap()
        y_d = nc.dram_tensor("expert_rows", [NBLK * CAP, D], F32, kind="Internal").ap()

        x_d = t["x"].rearrange("b (i p) d -> (b i) p d", p=P)
        out_d = t["out"].rearrange("b (i p) d -> (b i) p d", p=P)

        act_chain, dve_chain, pool_chain = sem("act_chain"), sem("dve_chain"), sem("pool_chain")
        const_in, masks_set = sem("const_in"), sem("masks_set")
        x_in = [sem(f"x_in{j}") for j in range(3)]
        win_in = [sem(f"win_in{k}") for k in range(4)]
        g1_in = sem("g1_in")
        x_rstd, hn_ready = sem("x_rstd"), sem("hn_ready")
        hnt_ps, hnt_act, hnt_dve = sem("hnt_ps"), sem("hnt_act"), sem("hnt_dve")
        proj_ps, proj_act = sem("proj_ps"), sem("proj_act")
        lat_rstd, lat_ready, krp_ready = sem("lat_rstd"), sem("lat_ready"), sem("krp_ready")
        latt_ps, latt_sb = sem("latt_ps"), sem("latt_sb")
        gate_ps, gate_rows, lf_t, rows_pre, rows_done = (sem(n) for n in
                                                         ("gate_ps", "gate_rows", "lf_t", "rows_pre", "rows_done"))
        rs_set = sem("rs_set")
        cols_ps, cols_sb = sem("cols_ps"), sem("cols_sb")
        ktm_ps, ktm_sb = sem("ktm_ps"), sem("ktm_sb")
        lam_s, lam_done = sem("lam_s"), sem("lam_done")
        conv_done, lgate_ps, lgate_sb = sem("conv_done"), sem("lgate_ps"), sem("lgate_sb")
        gelu_arg_pool = sem("gelu_arg_pool")
        gelu_arg, gelu_sig, gelu_done = sem("gelu_arg"), sem("gelu_sig"), sem("gelu_done")
        lru_t, lru_ix, lru_y = sem("lru_t"), sem("lru_ix"), sem("lru_y")
        lru_a, lru_ratio, lru_root = sem("lru_a"), sem("lru_ratio"), sem("lru_root")
        yr_sq, yr_ps, yr_rstd, yr_done = sem("yr_sq"), sem("yr_ps"), sem("yr_rstd"), sem("yr_done")
        db_ps, d_ready, w_ready = sem("db_ps"), sem("d_ready"), sem("w_ready")
        st_ps, pw_ready, ks_ready = sem("st_ps"), sem("pw_ready"), sem("ks_ready")
        inter_ps, inter_sb, upd_ps, state_ready = sem("inter_ps"), sem("inter_sb"), sem("upd_ps"), sem("state_ready")
        intra_ps, num_ready, mh_sq, mh_ss, mh_rstd, ymt_ready, h_done = (sem(n) for n in (
            "intra_ps", "num_ready", "mh_sq", "mh_ss", "mh_rstd", "ymt_ready", "h_done"))
        ym_ps, ym_sb = sem("ym_ps"), sem("ym_sb")
        wu_in, wuq_in, kv_ps, kv_sb, kr_sb = sem("wu_in"), sem("wuq_in"), sem("kv_ps"), sem("kv_sb"), sem("kr_sb")
        q_ps, q_sb, q_rope, qt_ps, qt_act, qt_dve = (sem(n) for n in ("q_ps", "q_sb", "q_rope", "qt_ps", "qt_act", "qt_dve"))
        s_ps, s_max, p_ready = sem("s_ps"), sem("s_max"), sem("p_ready")
        pt_ps, pt_act, pt_dve, pv_ps, pv_sb = sem("pt_ps"), sem("pt_act"), sem("pt_dve"), sem("pv_ps"), sem("pv_sb")
        wout_in, g2_in = sem("wout_in"), sem("g2_in")
        xr_in = [sem(f"xr_in{j}") for j in range(2)]
        ya_rstd, ya_ready, yat_ps, yat_sb = (sem(n) for n in ("ya_rstd", "ya_ready", "yat_ps", "yat_sb"))
        o_ps, x2_half, x2_ready, x2_rstd, x2n_ready = sem("o_ps"), sem("x2_half"), sem("x2_ready"), sem("x2_rstd"), sem("x2n_ready")
        x2n_out = sem("x2n_out")
        x2nt_ps, x2nt_act, x2nt_dve, r_ps, r_sb = (sem(n) for n in ("x2nt_ps", "x2nt_act", "x2nt_dve", "r_ps", "r_sb"))
        rt_a, rt_b, mask_ready, pos_ps, slot_ready = (sem(n) for n in ("rt_a", "rt_b", "mask_ready", "pos_ps", "slot_ready"))
        iota_set, places_ready, ids_ps, idx_ready, ove_ready = (sem(n) for n in (
            "iota_set", "places_ready", "ids_ps", "idx_ready", "ove_ready"))
        w_in_ = [sem(f"wexp_in{j}") for j in range(NW)]
        pool_waits, zero_set, zero_out = sem("pool_waits"), sem("zero_set"), sem("zero_out")
        list_ready, scm_set = sem("list_ready"), sem("scm_set")
        xg_set = sem("xg_set")
        xg_in = [sem(f"xg_in{j}") for j in range(2)]
        xgt_ps, xgt_act, xgt_dve = sem("xgt_ps"), sem("xgt_act"), sem("xgt_dve")
        gu_ps, sg_ready, h_ready = sem("gu_ps"), sem("sg_ready"), sem("h_ready")
        y_ps, y_act, y_dve = sem("y_ps"), sem("y_act"), sem("y_dve")
        y_out = [sem(f"y_out{j}") for j in range(2)]
        yg_in = [sem(f"yg_in{j}") for j in range(NY)]
        gf_in = sem("gf_in")
        f_sum, f_rstd, f_ready = sem("f_sum"), sem("f_rstd"), sem("f_ready")
        out_done = [sem(f"out_done{j}") for j in range(2)]

        STEPS, PROJ = [], []

        def step(kind, a, b=0):
            STEPS.append((kind, a, b))
            if kind in "TF":
                PROJ.append((kind, a, b))

        for i in range(4):
            step("turn", i)
            step("T", i, 0)
        for i in range(4):
            step("T", i, 1)
            step("T", i, 2)
            if i >= 1:
                step("latent", i - 1)
        step("turn", 4)
        for m in range(6):
            step("F", 0, m)
            if m == 0:
                step("latent", 3)
        for i in range(4, NT):
            if i + 1 < NT:
                step("turn", i + 1)
            for b in range(3):
                step("T", i, b)
            if i >= 5:
                step("latent", i - 1)
        step("F", 1, 2)
        step("latent", NT - 1)
        step("F", 1, 3)
        step("gates", 0)
        step("F", 1, 4)
        step("F", 1, 5)
        step("F", 1, 0)
        step("row_exps", 0)
        step("F", 1, 1)
        NPROJ = len(PROJ)
        W_PIECES = (((C_MK, 512),), ((C_MO, MLW + 8),), ((C_CQ, N_LAT),), ((C_MQ, 256), (C_RX, 512)))
        T_COLS = ((C_MK, 512), (C_MO, MLW + 8), (C_CQ, N_LAT))
        F_COLS = (C_MQ, C_MQ + P, C_RX, C_RX + P, C_RG, C_RG + P)

        def job(kind, a, b):
            return PROJ.index((kind, a, b))

        NC_ = 27

        def chained(eng, chain):
            count = [0]

            def link(ins):
                count[0] += 1
                ins.then_inc(chain, 1)
                eng.wait_ge(chain, count[0])
            return link

        ORDER = list(reversed(range(NT)))
        ATT = [(i, h) for i in ORDER for h in range(H)]
        GROUPS = [(n, g) for n, (i, h) in enumerate(ATT) for g in range((i + 4) // 4)]
        G0 = [sum(1 for (m, _) in GROUPS if m < n) for n in range(len(ATT) + 1)]
        N = len(ATT)
        KV_EARLY, KV_CHUNK = 8, 2
        DUE = {"sumsq": 1, "scale": 2, "turn": 3, "half0": (4, 5, 6), "add0": 6, "half1": (7, 8, 9), "add1": 9, "sumsq2": 10, "norm2": 11}
        DUE_LAST = {"sumsq": 1, "scale": 2, "turn": 3, "half0": (4,), "add0": 4, "half1": (5,), "add1": 5, "sumsq2": 6, "norm2": 7}
        LAST = N + NT + 1

        def out_bank(t, b):
            return 6 if t == NT - 1 and b == 1 else 7

        def plan(t):
            return DUE if t < NT - 1 else DUE_LAST


        def due(n):
            return [(t, n - H * (t + 1)) for t in range(NT) if 0 < n - H * (t + 1) <= 11]

        block = ctx.enter_context(nc.Block())

        @block.sync
        def _(sp):
            def load_x(i):
                if i >= 3:
                    sp.wait_ge(hnt_ps, 2 * (i - 2))
                sp.dma_start(XB[i % 3], x_d[i]).then_inc(x_in[i % 3], 16)

            def load_w(g):
                for c0, w in W_PIECES[g]:
                    sp.dma_start(W_IN[:, :, c0:c0 + w], t["w_in"][0].rearrange("(k p) n -> p k n", p=P)[:, :, c0:c0 + w]).then_inc(win_in[g], 16)

            def load_constants():
                row = lambda a: a.rearrange("l n -> (l n)").partition_broadcast(P)
                colw = lambda a: a[0].rearrange("(f p) -> p f", p=P)
                with nc.allow_non_contiguous_dma(reason="small columns"):
                    sp.dma_start(GQ[:, 0:QL], row(t["q_norm_g"])).then_inc(const_in, 16)
                    sp.dma_start(GQ[:, QL:], row(t["kv_norm_g"])).then_inc(const_in, 16)
                    sp.dma_start(COS[:, :].rearrange("p (i n) -> p i n", i=NT), t["rope_cos"].rearrange("(i p) n -> p i n", p=P)).then_inc(const_in, 16)
                    sp.dma_start(SIN[:, :].rearrange("p (i n) -> p i n", i=NT), t["rope_sin"].rearrange("(i p) n -> p i n", p=P)).then_inc(const_in, 16)
                    sp.dma_start(BGI[:, :], t["ml_i_bias"].rearrange("l h -> h l")).then_inc(const_in, 16)
                    sp.dma_start(BGF[:, :], t["ml_f_bias"].rearrange("l h -> h l")).then_inc(const_in, 16)
                    for f in range(2):
                        sp.dma_start(CW[:, f * CONV:(f + 1) * CONV], t["conv_w"][0, :, f * P:(f + 1) * P].rearrange("j p -> p j")).then_inc(const_in, 16)
                    sp.dma_start(CB[:, :], colw(t["conv_b"])).then_inc(const_in, 16)
                    sp.dma_start(BR[:, :], colw(t["lru_b_r"])).then_inc(const_in, 16)
                    sp.dma_start(BI[:, :], colw(t["lru_b_i"])).then_inc(const_in, 16)
                    sp.dma_start(LAM[:, :], colw(t["lru_lambda"])).then_inc(const_in, 16)
                    sp.dma_start(GLRU[:, :], colw(t["lru_norm_g"])).then_inc(const_in, 16)
                    sp.dma_start(GML[:, :], row(t["ml_norm_g"])).then_inc(const_in, 16)
                    sp.dma_start(GMLA[:, :], row(t["mla_norm_g"])).then_inc(const_in, 16)
                    sp.wait_ge(masks_set, 7)
                    for g, w in enumerate(("lru_w_r", "lru_w_i")):
                        for f in range(2):
                            for q in range(2):
                                r = slice(64 * q, 64 * q + 64)
                                c0 = (2 * g + f) * P + 64 * q
                                sp.dma_start(BD[r, c0:c0 + 64], t[w][0, 2 * f + q]).then_inc(const_in, 16)
                    wr = WR[:, :].rearrange("p (k n) -> p k n", k=KD)
                    sp.dma_start(wr[:, :, 0:NG], t["w_group"][0].rearrange("(k p) n -> p k n", p=P)).then_inc(const_in, 16)
                    sp.dma_start(wr[:, :, NG:], t["w_expert"][0].rearrange("(k p) n -> p k n", p=P)).then_inc(const_in, 16)
                    sp.dma_start(BRT[:, 0:NG], row(t["b_group"])).then_inc(const_in, 16)
                    sp.dma_start(BRT[:, NG:], row(t["b_expert"])).then_inc(const_in, 16)

            load_x(0)
            sp.dma_start(GB[:, :], t["norm1_g"].rearrange("l d -> (l d)").partition_broadcast(P)).then_inc(g1_in, 16)
            load_w(0)
            load_x(1)
            load_x(2)
            load_w(1)
            load_x(3)
            load_w(2)
            load_w(3)
            load_constants()
            for i in range(4, NT):
                load_x(i)
            sp.wait_ge(zero_set, 1)
            for b in range(NMAIN, NBLK):
                sp.dma_start(y_d[b * CAP:(b + 1) * CAP, :].rearrange("p (q n) -> p q n", q=2),
                             ZERO.unsqueeze(1).broadcast_to([P, 2, 512])).then_inc(zero_out, 16)
            sp.wait_ge(proj_ps, NPROJ)
            sp.dma_start(W_UKV, t["w_ukv"][0].rearrange("p (h n) -> p h n", h=H)).then_inc(wu_in, 16)
            sp.wait_ge(latt_sb, NT)
            sp.dma_start(KT[NOPE:QK, :, :], KPT[NOPE:QK, :].unsqueeze(1).broadcast_to([ROPE, H, S])).then_inc(kr_sb, 16)
            sp.wait_ge(yr_sq, 2)
            sp.dma_start(W_UQ, t["w_uq"][0].rearrange("(k p) n -> p k n", p=P)).then_inc(wuq_in, 16)
            sp.wait_ge(upd_ps, NT)
            sp.dma_start(GB[:, :], t["final_norm_g"].partition_broadcast(P)).then_inc(gf_in, 16)
            sp.wait_ge(ym_ps, 4)
            sp.dma_start(W_OUT, t["w_out"][0].rearrange("(k p) n -> p k n", p=P)).then_inc(wout_in, 16)
            sp.wait_ge(kv_ps, 24)
            sp.wait_ge(qt_ps, 2 * NT)
            sp.dma_start(G2B, t["norm2_g"].rearrange("l d -> (l d)").partition_broadcast(P)).then_inc(g2_in, 16)
            def load_expert(j, e):
                sp.dma_start(WGU[j][:, 0], t["w_gate"][0, e].rearrange("(k p) n -> p k n", p=P)).then_inc(w_in_[j], 16)
                sp.dma_start(WGU[j][:, 1], t["w_up"][0, e].rearrange("(k p) n -> p k n", p=P)).then_inc(w_in_[j], 16)
                sp.dma_start(WDN[j], t["w_down"][0, e].rearrange("(k p) n -> p k n", p=P)).then_inc(w_in_[j], 16)

            def load_xr(j):
                if j >= 2:
                    sp.wait_ge(x2_ready, j - 1)
                sp.dma_start(XR[j % 2], x_d[ORDER[j]]).then_inc(xr_in[j % 2], 16)

            load_xr(0)
            load_xr(1)
            for j, i in enumerate(ORDER):
                if j + 2 < NT:
                    load_xr(j + 2)
                sp.wait_ge(x2n_ready, j + 1)
                sp.dma_start(x2n_d[i * P:(i + 1) * P, :], X2N[j]).then_inc(x2n_out, 16)
                if j == NT - 2:
                    sp.wait_ge(pv_ps, N)
                    load_expert(0, 0)
                    sp.wait_ge(o_ps, 2 * NT)
                    load_expert(2, 2)

            sp.wait_ge(r_ps, NT)
            sp.wait_ge(x2n_out, 16 * NT)
            load_expert(1, 1)
            load_expert(3, 3)

            def store(row, done):
                rows = y_d.rearrange("(b p) d -> b p d", p=CAP)[row]
                sp.wait_ge(y_act, done)
                sp.dma_start(rows[:, 0:512], YB[0]).then_inc(y_out[0], 16)
                sp.wait_ge(y_dve, done)
                sp.dma_start(rows[:, 512:1024], YB[1]).then_inc(y_out[1], 16)

            sp.sem_inc(y_out[0], 16)
            sp.sem_inc(y_out[1], 16)
            with sp.Fori(0, NMAIN // NW - 1) as it:
                for j in range(NW):
                    store(it * NW + j, it * NW + (j + 2))
                    sp.wait_ge(y_ps, it * NW + (j + 1))
                    load_expert(j, it * NW + (NW + j))
            for n in range(NMAIN - NW, NMAIN):
                store(n, n + 2)
            sp.wait_ge(ove_ready, 1)
            nover = sp.value_load(OVE[0:1, NOVER:NOVER + 1], min_val=0, max_val=NOVER)
            with sp.Fori(0, NOVER) as b:
                eid = sp.value_load(OVE[0:1, bass.ds(b, 1)], min_val=0, max_val=NE - 1)
                with sp.If(b < nover):
                    sp.wait_ge(y_ps, NMAIN + b)
                    load_expert(0, eid)
                    store(b + NMAIN, b + (NMAIN + 2))
                with sp.Else():
                    sp.nop()
            for i in range(NT):
                sp.wait_ge(f_ready, i + 1)
                sp.dma_start(out_d[i], OUT[i % 2]).then_inc(out_done[i % 2], 16)
            sp.wait_ge(out_done[0], 16 * (NT // 2))
            sp.wait_ge(out_done[1], 16 * (NT // 2))

        @block.tensor
        def _(pe):
            def turn(out, in_, n=P):
                return pe.transpose(out, in_, IDENT[0:n, 0:n])

            pe.wait_ge(masks_set, 7)

            def norm1_turn(i):
                pe.wait_ge(hn_ready, i + 1)
                for h in range(2):
                    if i >= 1:
                        pe.wait_ge(hnt_act if h == 0 else hnt_dve, i)
                    for q in range(4):
                        k = 4 * h + q
                        ins = turn(ps[h][:, q * P:(q + 1) * P], XB[i % 3][:, k * P:(k + 1) * P])
                    ins.then_inc(hnt_ps, 1)

            def proj(n):
                kind, a, b = PROJ[n]
                bank = ps[4 + n % 4]
                if n >= 4:
                    pe.wait_ge(proj_act, n - 3)
                need = a + 1 if kind == "T" else 4 * a + 4
                pe.wait_ge(hnt_act, need)
                pe.wait_ge(hnt_dve, need)
                for k in range(KD):
                    if k == 0:
                        pe.wait_ge(win_in[b if kind == "T" else 3], 16 if kind == "T" else 32)
                    if kind == "T":
                        c0, w = T_COLS[b]
                        ins = pe.matmul(bank[:, 0:w], HNT[:, a // 4, k, a % 4 * P:(a % 4 + 1) * P], W_IN[:, k, c0:c0 + w],
                                        start=(k == 0), stop=(k == KD - 1))
                    else:
                        ins = pe.matmul(bank[:, :], W_IN[:, k, F_COLS[b]:F_COLS[b] + P],
                                        HNT[:, a, k, :], start=(k == 0), stop=(k == KD - 1))
                ins.then_inc(proj_ps, 1)

            def latent_turn(i):
                pe.wait_ge(lat_ready, i + 1)
                pe.wait_ge(krp_ready, i + 1)
                if i >= 1:
                    pe.wait_ge(latt_sb, i)
                c = CQR[i % 2]
                for q in range(3):
                    turn(ps[2][:, q * P:(q + 1) * P], c[:, q * P:(q + 1) * P])
                turn(ps[2][0:QK, 3 * P:4 * P], KRP[i % 2]).then_inc(latt_ps, 1)

            def gates_turn():
                pe.wait_ge(hnt_act, NT)
                pe.wait_ge(hnt_dve, NT)
                pe.wait_ge(latt_sb, NT)
                pe.wait_ge(proj_act, job("T", NT - 1, 1) + 1)
                for kind in range(2):
                    for half in range(2):
                        for q in range(4):
                            i = 4 * half + q
                            ins = turn(ps[2 * kind + half][0:MLH, q * P:(q + 1) * P],
                                       GATES[:, i * 8 + 4 * kind:i * 8 + 4 * kind + 4])
                        ins.then_inc(gate_ps, 1)

            n = 0
            for kind, a, b in STEPS:
                if kind == "turn":
                    norm1_turn(a)
                elif kind == "latent":
                    latent_turn(a)
                elif kind == "gates":
                    gates_turn()
                elif kind in "TF":
                    proj(n)
                    n += 1

            pe.wait_ge(proj_act, NPROJ)
            pe.wait_ge(gate_rows, 4)
            for f in range(2):
                pe.wait_ge(conv_done, f + 1)
                for g in range(2):
                    for half in range(2):
                        pe.matmul(ps[4 * (1 - f) + 2 * g + half][:, :], BD[:, (2 * g + f) * P:(2 * g + f + 1) * P],
                                  LT[f][0][:, half * 512:(half + 1) * 512], start=True, stop=True).then_inc(lgate_ps, 1)
            for m in range(2):
                for half in range(2):
                    pe.wait_ge(lgate_sb, 2 * m + half + 1)
                    for q in range(4):
                        i = 4 * half + q
                        ins = turn(ps[4 + 2 * m + half][:, q * P:(q + 1) * P], KTOK[:, i, m * P:(m + 1) * P])
                    ins.then_inc(ktm_ps, 1)
            pe.wait_ge(rows_done, 5)
            pe.wait_ge(lgate_sb, 8)
            for half in range(2):
                for q in range(4):
                    i = 4 * half + q
                    ins = turn(ps[half][:, q * P:(q + 1) * P], ROWS4[:, i * P:(i + 1) * P])
                ins.then_inc(cols_ps, 1)
            for h in range(MLH):
                ins = pe.matmul(ps[2][:, h * NT:(h + 1) * NT], SEL[:, h * P:(h + 1) * P], DEC[:, :], start=True, stop=True)
            ins.then_inc(cols_ps, 1)

            def kv_proj(j, bank):
                if j < 16:
                    h, half = j // 2, j % 2
                    ins = pe.matmul(ps[bank][0:NOPE, :], W_UKV[:, h, 0:NOPE], CKVT[:, half * 512:(half + 1) * 512], start=True, stop=True)
                else:
                    i = j - 16
                    ins = pe.matmul(ps[bank][:, :], CKVT[:, i * P:(i + 1) * P], W_UKV[:, :, NOPE:], start=True, stop=True)
                ins.then_inc(kv_ps, 1)

            pe.wait_ge(wu_in, 16)
            for j in range(KV_EARLY):
                if j < 4:
                    pe.wait_ge(ktm_sb, j + 1)
                else:
                    pe.wait_ge(kv_sb, j - 3)
                kv_proj(j, 4 + j % 4)
            pe.wait_ge(cols_sb, 3)
            pe.wait_ge(kv_sb, KV_EARLY)

            def lru_sumsq(half):
                pe.wait_ge(yr_sq, 2)
                if half == 1:
                    pe.wait_ge(yr_rstd, 1)
                for f in range(2):
                    ins = pe.matmul(ps[7][:, :], ONES[:, :], LT[f][3][:, half * 512:(half + 1) * 512],
                                    start=(f == 0), stop=(f == 1))
                ins.then_inc(yr_ps, 1)

            def chunk_front(c):
                if c >= 1:
                    pe.wait_ge(d_ready, c)
                    pe.wait_ge(pw_ready, c)
                for h in range(MLH):
                    ins = pe.matmul(ps[0][:, h * P:(h + 1) * P], SEL[:, h * P:(h + 1) * P],
                                    ROW_A[:, c * P:(c + 1) * P], start=True, stop=True)
                ins.then_inc(db_ps, 1)
                for par in range(2):
                    for m in range(2):
                        r = slice(64 * par, 64 * par + 64)
                        ins = pe.matmul(ps[1 + par][:, m * P:(m + 1) * P], KTM[r, m, c * P:(c + 1) * P],
                                        MQT[r, m, c * P:(c + 1) * P], start=True, stop=True)
                ins.then_inc(st_ps, 1)

            def chunk_state(c):
                pe.wait_ge(state_ready, c + 1)
                if c >= 1:
                    pe.wait_ge(inter_sb, c)
                for par in range(2):
                    for m in range(2):
                        r = slice(64 * par, 64 * par + 64)
                        ins = pe.matmul(ps[4 + par][:, m * VA:(m + 1) * VA], MQT[r, m, c * P:(c + 1) * P],
                                        CST[r, m * VA:(m + 1) * VA], start=True, stop=True)
                ins.then_inc(inter_ps, 1)
                pe.wait_ge(ks_ready, c + 1)
                for m in range(2):
                    ins = pe.matmul(ps[6][:, m * 2 * VA:(m + 1) * 2 * VA], KSB[c % 2][:, m * P:(m + 1) * P],
                                    VAUG[:, c, 2 * m:2 * m + 2, :], start=True, stop=True)
                ins.then_inc(upd_ps, 1)

            def chunk_intra(c):
                pe.wait_ge(pw_ready, c + 1)
                if c >= 1:
                    pe.wait_ge(num_ready, c)
                for h in range(MLH):
                    ins = pe.matmul(ps[3][:, h * VA:(h + 1) * VA], PWB[c % 2][:, h * P:(h + 1) * P], VAUG[:, c, h, :],
                                    start=True, stop=True)
                ins.then_inc(intra_ps, 1)

            def kv_between(j):
                pe.wait_ge(kv_sb, j)
                kv_proj(j, 7)

            chunk_front(0)
            for c in range(NT):
                chunk_state(c)
                if c == 0:
                    lru_sumsq(0)
                    chunk_front(1)
                    lru_sumsq(1)
                    pe.wait_ge(yr_rstd, 2)
                    kv_between(KV_EARLY)
                else:
                    kv_between(KV_EARLY + KV_CHUNK * c)
                    if c + 1 < NT:
                        chunk_front(c + 1)
                chunk_intra(c)
                kv_between(KV_EARLY + KV_CHUNK * c + 1)
            pe.wait_ge(num_ready, NT)
            pe.wait_ge(inter_sb, NT)
            pe.wait_ge(state_ready, NT + 1)
            pe.wait_ge(kv_sb, 24)
            pe.wait_ge(wuq_in, 16)

            def q_proj(i):
                if i >= 1:
                    pe.wait_ge(q_sb, i)
                for b in range(2):
                    for k in range(2):
                        ins = pe.matmul(ps[4 + b][:, 0:384], CQT[:, k, i * P:(i + 1) * P],
                                        W_UQ[:, k, b * 384:(b + 1) * 384], start=(k == 0), stop=(k == 1))
                ins.then_inc(q_ps, 1)

            def q_turn(i):
                pe.wait_ge(q_rope, i + 1)
                for b in range(2):
                    if i >= 1:
                        pe.wait_ge(qt_act if b == 0 else qt_dve, i)
                    for q in range(4):
                        ins = turn(ps[6 + b][0:QK, q * P:(q + 1) * P], QTOK[i % 2][:, 4 * b + q, :])
                    ins.then_inc(qt_ps, 1)

            q_proj(0)
            for i in range(NT):
                if i + 1 < NT:
                    q_proj(i + 1)
                q_turn(i)

            pe.wait_ge(ymt_ready, 1)
            for m in range(2):
                for half in range(2):
                    for q in range(4):
                        ins = turn(ps[2 * m + half][:, q * P:(q + 1) * P], OTOK[:, 4 * half + q, m * P:(m + 1) * P])
                    ins.then_inc(ym_ps, 1)
            pe.wait_ge(ym_sb, 4)

            def scores(n):
                i, h = ATT[n]
                if n >= 2:
                    pe.wait_ge(p_ready, n - 1)
                L = (i + 1) * P
                for b in range((L + 511) // 512):
                    w = min(512, L - 512 * b)
                    ins = pe.matmul(ps[2 * (n % 2) + b][:, 0:w], QT[0:QK, i, h, :],
                                    KT[0:QK, h, 512 * b:512 * b + w], start=True, stop=True)
                ins.then_inc(s_ps, 1)

            def probs_turn(n):
                i, h = ATT[n]
                pe.wait_ge(p_ready, n + 1)
                for g in range(G0[n + 1] - G0[n]):
                    gg = G0[n] + g
                    if gg >= 2:
                        pe.wait_ge(pt_act if gg % 2 == 0 else pt_dve, gg // 2)
                    for q in range(min(4, i + 1 - 4 * g)):
                        ins = turn(ps[4 + gg % 2][:, q * P:(q + 1) * P], PB[n % 2][:, (4 * g + q) * P:(4 * g + q + 1) * P])
                    ins.then_inc(pt_ps, 1)

            def values(n):
                i, h = ATT[n]
                if n >= 1:
                    pe.wait_ge(pv_sb, n)
                for kb in range(i + 1):
                    gg = G0[n] + kb // 4
                    if kb % 4 == 0:
                        pe.wait_ge(pt_act if gg % 2 == 0 else pt_dve, gg // 2 + 1)
                    q = kb % 4
                    ins = pe.matmul(ps[6][:, 0:VD], PTB[gg % 4][:, q * P:(q + 1) * P], V[:, kb, h, :],
                                    start=(kb == 0), stop=(kb == i))
                ins.then_inc(pv_ps, 1)

            pe.wait_ge(kv_sb, 24)
            pe.wait_ge(kr_sb, 16)
            pe.wait_ge(qt_act, NT)
            pe.wait_ge(qt_dve, NT)
            def ya_turn(t):
                pe.wait_ge(ya_ready, t + 1)
                pe.wait_ge(x2_ready, t)
                for q in range(4):
                    ins = turn(ps[7][:, q * P:(q + 1) * P], YA[:, ORDER[t], q * P:(q + 1) * P])
                ins.then_inc(yat_ps, 1)

            def out_proj(t, b, ks):
                i = ORDER[t]
                if ks[0] == 0:
                    if b == 0:
                        pe.wait_ge(wout_in, 16)
                        pe.wait_ge(yat_sb, t + 1)
                    elif t < NT - 1:
                        pe.wait_ge(x2_half, t + 1)
                    else:
                        pe.wait_ge(pv_sb, N)
                lhs = [YM[:, 0, i * P:(i + 1) * P], YM[:, 1, i * P:(i + 1) * P], RXP[:, 0, 3 + i * P:3 + (i + 1) * P],
                       RXP[:, 1, 3 + i * P:3 + (i + 1) * P]] + [YAT[t % 2][:, q * P:(q + 1) * P] for q in range(4)]
                for k in ks:
                    ins = pe.matmul(ps[out_bank(t, b)][:, :], lhs[k], W_OUT[:, k, b * 512:(b + 1) * 512],
                                    start=(k == 0), stop=(k == KD - 1))
                if ks[-1] == KD - 1:
                    ins.then_inc(o_ps, 1)

            def between(n):
                for t, off in due(n):
                    if off == plan(t)["turn"]:
                        ya_turn(t)
                    for b in range(2):
                        if off in plan(t)[f"half{b}"]:
                            parts = ((0, 1, 2), (3, 4, 5), (6, 7)) if t < NT - 1 else (tuple(range(KD)),)
                            out_proj(t, b, parts[plan(t)[f"half{b}"].index(off)])

            def x2n_turn(j):
                pe.wait_ge(x2n_ready, j + 1)
                for h in range(2):
                    if j >= 2:
                        pe.wait_ge(x2nt_act if h == 0 else x2nt_dve, j - 1)
                    for q in range(4):
                        k = 4 * h + q
                        ins = turn(ps[2 * (j % 2) + h][:, q * P:(q + 1) * P], X2N[j][:, k * P:(k + 1) * P])
                    ins.then_inc(x2nt_ps, 1)

            def router(j):
                pe.wait_ge(x2nt_act, j + 1)
                pe.wait_ge(x2nt_dve, j + 1)
                if j >= 2:
                    pe.wait_ge(r_sb, j - 1)
                for k in range(KD):
                    ins = pe.matmul(ps[4 + j % 2][:, 0:36], X2NT[j % 2][:, k, :], WR[:, k * 36:(k + 1) * 36],
                                    start=(k == 0), stop=(k == KD - 1))
                ins.then_inc(r_ps, 1)

            scores(0)
            for n in range(LAST):
                if n + 1 < N:
                    scores(n + 1)
                between(n)
                if n < N:
                    probs_turn(n)
                if 1 <= n <= N:
                    values(n - 1)
                if N + 1 <= n <= N + NT - 1:
                    x2n_turn(n - N - 1)
                if N + 2 <= n <= N + NT:
                    router(n - N - 2)
            x2n_turn(NT - 1)
            router(NT - 1)

            pe.wait_ge(mask_ready, 1)
            pe.matmul(ps[0][:, 0:NT * NE], TRI[:, :], RA[:, 0:NT * NE], start=True, stop=True)
            pe.matmul(ps[1][:, 0:NT * NE], ONES[:, :], RA[:, 0:NT * NE].rearrange("p (i e) -> p e i", i=NT), start=True, stop=True).then_inc(pos_ps, 1)
            for n in range(NS):
                pe.wait_ge(places_ready, n + 1)
                ins = pe.matmul(ps[2][:, 0:NBLK], OHP[:, n, :], BEQ[:, n, :], start=(n == 0), stop=(n == NS - 1))
            ins.then_inc(ids_ps, 1)
            pe.wait_ge(idx_ready, 1)

            def rows_turn(u, done):
                pe.wait_ge(xgt_act, done)
                pe.wait_ge(xgt_dve, done)
                for h in range(2):
                    for q in range(4):
                        k = 4 * h + q
                        ins = turn(ps[h][:, q * P:(q + 1) * P], XG[u][:, k * P:(k + 1) * P])
                    ins.then_inc(xgt_ps, 1)

            def gate_up(u, w, done):
                pe.wait_ge(xgt_act, done + 1)
                pe.wait_ge(xgt_dve, done + 1)
                for g in range(2):
                    for m in range(2):
                        for k in range(KD):
                            ins = pe.matmul(ps[2 + 2 * u + g][:, m * P:(m + 1) * P],
                                            WGU[w][:, g, k, m * P:(m + 1) * P], XGT[u][:, k, :],
                                            start=(k == 0), stop=(k == KD - 1))
                    ins.then_inc(gu_ps, 1)

            def down(u, w, done):
                pe.wait_ge(h_ready, done + 1)
                pe.wait_ge(y_act, done)
                pe.wait_ge(y_dve, done)
                for b in range(2):
                    for k in range(2):
                        ins = pe.matmul(ps[6 + b][:, :], HT[u][:, k, :], WDN[w][:, k, b * 512:(b + 1) * 512],
                                        start=(k == 0), stop=(k == 1))
                ins.then_inc(y_ps, 1)

            pe.wait_ge(xg_in[0], 16)
            rows_turn(0, 1)
            with pe.Fori(0, NMAIN // NW) as it:
                for j in range(NW):
                    u = j % 2
                    pe.wait_ge(w_in_[j], it * 48 + 48)
                    gate_up(u, j, it * NW + (j + 1))
                    pe.wait_ge(xg_in[1 - u], it * (NW // 2 * 16) + 16 * ((j + 1) // 2 + 1))
                    rows_turn(1 - u, it * NW + (j + 2))
                    down(u, j, it * NW + (j + 1))
            pe.wait_ge(ove_ready, 1)
            nover = pe.value_load(OVE[0:1, NOVER:NOVER + 1], min_val=0, max_val=NOVER)
            with pe.Fori(0, NOVER) as b:
                with pe.If(b < nover):
                    pe.wait_ge(xg_in[0], (NMAIN // 2 + 2) * 16 + b * 16)
                    pe.wait_ge(w_in_[0], (NMAIN // NW) * 48 + 48 + b * 48)
                    rows_turn(0, NMAIN + 2 + b)
                    gate_up(0, 0, NMAIN + 2 + b)
                    down(0, 0, NMAIN + 1 + b)
                with pe.Else():
                    pe.nop()

        @block.scalar
        def _(act):
            link = chained(act, act_chain)

            def exp_and_ln():
                act.preload_act_table_set("natural_log_exp_and_others")

            exp_and_ln()

            def norm1_stats(i):
                act.wait_ge(x_in[i % 3], 16 * (i // 3 + 1))
                link(act.activation(JUNK[:, :], XB[i % 3], ACT.Square, accum_out=ST1[:, i:i + 1]))
                link(act.activation(ST1[:, NT + i:NT + i + 1], ST1[:, i:i + 1], ACT.Ln, bias=EPSC[:, :], scale=1.0 / D))
                act.activation(ST1[:, NT + i:NT + i + 1], ST1[:, NT + i:NT + i + 1], ACT.Exp, scale=-0.5).then_inc(x_rstd, 1)

            def norm1_evac(i):
                act.wait_ge(hnt_ps, 2 * i + 1)
                act.activation(HNT[:, i // 4, 0:4, i % 4 * P:(i % 4 + 1) * P], ps[0][:, :].rearrange("p (k n) -> p k n", k=4),
                               ACT.Copy).then_inc(hnt_act, 1)

            def proj_evac(n):
                kind, a, b = PROJ[n]
                bank = ps[4 + n % 4]
                act.wait_ge(proj_ps, n + 1)
                if kind == "F":
                    s = slice(a * 512, (a + 1) * 512)
                    dst = [MQT[:, 0, s], MQT[:, 1, s], RXP[:, 0, 3 + a * 512:3 + (a + 1) * 512],
                           RXP[:, 1, 3 + a * 512:3 + (a + 1) * 512], RG[:, 0, s], RG[:, 1, s]][b]
                    act.activation(dst, bank[:, :], ACT.Copy).then_inc(proj_act, 1)
                elif b == 0:
                    act.activation(KTOK[:, a, :], bank[:, 0:MLW], ACT.Copy, scale=MLD ** -0.5)
                    act.activation(VAUG[:, a, :, 0:MLD], bank[:, MLW:512].rearrange("p (h n) -> p h n", h=MLH), ACT.Copy).then_inc(proj_act, 1)
                elif b == 1:
                    act.activation(GATES[:, a * 8:a * 8 + 8], bank[:, MLW:MLW + 8], ACT.Copy)
                    act.activation(OTOK[:, a, :], bank[:, 0:MLW], ACT.Exp, scale=-1.0).then_inc(proj_act, 1)
                else:
                    if a >= 2:
                        act.wait_ge(latt_ps, a - 1)
                    act.activation(CQR[a % 2], bank[:, 0:N_LAT], ACT.Copy).then_inc(proj_act, 1)
                    act.wait_ge(proj_act, n + 1)
                    c = CQR[a % 2]
                    act.activation(JUNK[:, 0:QL], c[:, 0:QL], ACT.Square, accum_out=ST2[:, 2 * a:2 * a + 1])
                    link(act.activation(JUNK[:, QL:QL + KVL], c[:, QL:QL + KVL], ACT.Square, accum_out=ST2[:, 2 * a + 1:2 * a + 2]))
                    o = 2 * NT + 2 * a
                    act.activation(ST2[:, o:o + 1], ST2[:, 2 * a:2 * a + 1], ACT.Ln, bias=EPSC[:, :], scale=1.0 / QL)
                    link(act.activation(ST2[:, o + 1:o + 2], ST2[:, 2 * a + 1:2 * a + 2], ACT.Ln, bias=EPSC[:, :], scale=1.0 / KVL))
                    act.activation(ST2[:, o:o + 2], ST2[:, o:o + 2], ACT.Exp, scale=-0.5).then_inc(lat_rstd, 1)

            def latent_evac(i):
                act.wait_ge(latt_ps, i + 1)
                s = slice(i * P, (i + 1) * P)
                act.activation(CQT[:, :, s], ps[2][:, 0:2 * P].rearrange("p (m n) -> p m n", m=2), ACT.Copy)
                act.activation(CKVT[:, s], ps[2][:, 2 * P:3 * P], ACT.Copy)
                act.activation(KPT[0:QK, s], ps[2][0:QK, 3 * P:4 * P], ACT.Copy).then_inc(latt_sb, 1)

            def gate_rows_evac():
                act.wait_ge(const_in, 16 * NC_)
                for kind, dst, bias in ((0, ROW_I, BGI), (1, ROW_F, BGF)):
                    for half in range(2):
                        act.wait_ge(gate_ps, 2 * kind + half + 1)
                        act.activation(dst[:, half * 512:(half + 1) * 512], ps[2 * kind + half][0:MLH, :], ACT.Identity,
                                       bias=bias[:, :]).then_inc(gate_rows, 1)
                act.wait_ge(gate_rows, 4)
                link(act.activation(ROW_L, ROW_F, ACT.Abs))
                link(act.activation(ROW_L, ROW_L, ACT.Exp, scale=-1.0))
                act.activation(ROW_L, ROW_L, ACT.Ln, bias=ONEC[0:MLH, :]).then_inc(lf_t, 1)
                act.wait_ge(lam_s, 1)
                act.activation(SPT[:, 2:4], SPT[:, 0:2], ACT.Exp, scale=-1.0).then_inc(lam_s, 1)

            def row_exps():
                act.wait_ge(rows_pre, 1)
                act.activation(ROWS4[32:32 + MLH, :], ROW_T, ACT.Exp).then_inc(rows_done, 1)
                act.activation(ROWS4[64:64 + MLH, :], ROW_T2, ACT.Exp).then_inc(rows_done, 1)
                act.activation(ROWS4[96:96 + MLH, :], ROW_M, ACT.Exp, scale=-1.0).then_inc(rows_done, 1)
                act.activation(DEC[:, :], MPV[:, :], ACT.Exp).then_inc(rows_done, 1)

            act.wait_ge(masks_set, 7)
            norm1_stats(0)
            n = 0
            for kind, a, b in STEPS:
                if kind == "turn":
                    norm1_evac(a)
                    if a + 1 < NT:
                        norm1_stats(a + 1)
                elif kind == "latent":
                    latent_evac(a)
                elif kind == "gates":
                    gate_rows_evac()
                elif kind == "row_exps":
                    row_exps()
                else:
                    proj_evac(n)
                    n += 1

            act.wait_ge(lam_done, 1)
            for f in range(2):
                XC, R, IV, T, D1, E1 = LT[f]
                for g in range(2):
                    for half in range(2):
                        j = 4 * f + 2 * g + half
                        act.wait_ge(lgate_ps, j + 1)
                        act.activation((R, IV)[g][:, half * 512:(half + 1) * 512], ps[4 * (1 - f) + j % 4][:, :], ACT.Sigmoid,
                                       bias=(BR, BI)[g][:, f:f + 1]).then_inc(lgate_sb, 1)
                act.wait_ge(lgate_sb, 4 * f + 4)
                act.activation(T, R, ACT.Tanh, scale=SPT[:, 8 + f:9 + f]).then_inc(lru_t, 1)
            for f in range(2):
                act.wait_ge((gelu_arg_pool, gelu_arg)[f], 1)
                act.activation(LT[f][4], LT[f][4], ACT.Sigmoid, scale=GELU_S).then_inc(gelu_sig, 1)
            act.wait_ge(lru_t, 2)
            for f in range(2):
                act.activation(LT[f][1], LT[f][1], ACT.Exp, scale=SPT[:, 10 + f:11 + f]).then_inc(lru_a, 1)
            for f in range(2):
                act.wait_ge(lru_ratio, f + 1)
                act.activation(LT[f][3], LT[f][3], ACT.Sqrt).then_inc(lru_root, 1)
            exp_and_ln()
            for f in range(2):
                act.wait_ge(lru_y, f + 1)
                act.activation(LT[f][3], RXP[:, f, 3:3 + S], ACT.Square).then_inc(yr_sq, 1)
            R = LT[0][1]

            def lru_rstd(half):
                s = slice(half * 512, (half + 1) * 512)
                act.wait_ge(yr_ps, half + 1)
                link(act.activation(R[:, s], ps[7][:, :], ACT.Ln, bias=EPSC[:, :], scale=1.0 / LRU))
                act.activation(R[:, s], R[:, s], ACT.Exp, scale=-0.5).then_inc(yr_rstd, 1)

            act.wait_ge(cols_sb, 3)
            act.wait_ge(lru_y, 2)
            col = COL[:, :].rearrange("p (i k h) -> p i k h", i=NT, k=4)

            def weights(c):
                act.wait_ge(d_ready, c + 1)
                if c >= 2:
                    act.wait_ge(pw_ready, c - 1)
                for h in range(MLH):
                    ins = act.activation(WSB[c % 2][:, h * P:(h + 1) * P], DSB[c % 2][:, h * P:(h + 1) * P], ACT.Exp,
                                         bias=col[:, c, 0, h:h + 1])
                ins.then_inc(w_ready, 1)

            def kv_evac(j):
                act.wait_ge(kv_ps, j + 1)
                if j < 16:
                    h, half = j // 2, j % 2
                    act.activation(KT[0:NOPE, h, half * 512:(half + 1) * 512], ps[7][0:NOPE, :], ACT.Copy).then_inc(kv_sb, 1)
                else:
                    act.activation(V[:, j - 16].rearrange("p h n -> p (h n)"), ps[7][:, :], ACT.Copy).then_inc(kv_sb, 1)

            weights(0)
            for c in range(NT):
                act.wait_ge(inter_ps, c + 1)
                if c >= 2:
                    act.wait_ge(num_ready, c - 1)
                for h in range(MLH):
                    ins = act.activation(INT[c % 2][:, h * VA:(h + 1) * VA], ps[4 + h % 2][:, (h // 2) * VA:(h // 2 + 1) * VA],
                                         ACT.Copy, scale=col[:, c, 1, h:h + 1])
                ins.then_inc(inter_sb, 1)
                if c == 0:
                    lru_rstd(0)
                    weights(1)
                    lru_rstd(1)
                    kv_evac(KV_EARLY)
                else:
                    kv_evac(KV_EARLY + KV_CHUNK * c)
                    if c + 1 < NT:
                        weights(c + 1)
                kv_evac(KV_EARLY + KV_CHUNK * c + 1)

            act.wait_ge(h_done, NT)
            act.wait_ge(yr_done, 1)
            act.wait_ge(pw_ready, NT)
            act.wait_ge(intra_ps, NT)
            act.activation(SQ, OTOK.rearrange("p i n -> p (i n)"), ACT.Square).then_inc(mh_sq, 1)

            def q_evac(i):
                act.wait_ge(q_ps, i + 1)
                if i >= 2:
                    act.wait_ge(qt_ps, 2 * (i - 1))
                for b in range(2):
                    ins = act.activation(QTOK[i % 2][:, 4 * b:4 * b + 4, :], ps[4 + b][:, 0:384].rearrange("p (h n) -> p h n", h=4), ACT.Copy, scale=SCALE)
                ins.then_inc(q_sb, 1)

            def qt_evac(i):
                act.wait_ge(qt_ps, 2 * i + 1)
                act.activation(QT[0:QK, i, 0:4, :], ps[6][0:QK, :].rearrange("p (h n) -> p h n", h=4), ACT.Copy).then_inc(qt_act, 1)

            act.wait_ge(yr_done, 1)
            q_evac(0)
            act.wait_ge(mh_ss, 1)
            n = NT * MLH
            link(act.activation(MSS[:, n:2 * n], MSS[:, 0:n], ACT.Ln, bias=EPSC[:, :], scale=1.0 / MLD))
            act.activation(MSS[:, 2 * n:3 * n], MSS[:, n:2 * n], ACT.Exp, scale=-0.5).then_inc(mh_rstd, 1)
            for i in range(1, NT):
                q_evac(i)
                qt_evac(i - 1)
            qt_evac(NT - 1)
            act.wait_ge(zero_out, 16 * NOVER)
            for j in range(4):
                m, half = j // 2, j % 2
                act.wait_ge(ym_ps, j + 1)
                act.activation(YM[:, m, half * 512:(half + 1) * 512], ps[j][:, :], ACT.Copy).then_inc(ym_sb, 1)

            def probs(n):
                i, h = ATT[n]
                L = (i + 1) * P
                act.wait_ge(s_max, n + 1)
                if n >= 2:
                    act.wait_ge(pt_ps, G0[n - 1])
                for b in range((L + 511) // 512):
                    w = min(512, L - 512 * b)
                    ins = act.activation(PB[n % 2][:, 512 * b:512 * b + w], ps[2 * (n % 2) + b][:, 0:w], ACT.Exp,
                                         bias=NMX[:, n:n + 1],
                                         accum_out=(RSM if b == 0 else RIN)[:, n:n + 1])
                ins.then_inc(p_ready, 1)

            def probs_evac(n):
                i, h = ATT[n]
                for gg in range(G0[n], G0[n + 1]):
                    if gg % 2 == 0:
                        act.wait_ge(pt_ps, gg + 1)
                        if gg >= 4:
                            act.wait_ge(pv_ps, GROUPS[gg - 4][0] + 1)
                        w = P * min(4, i + 1 - 4 * GROUPS[gg][1])
                        act.activation(PTB[gg % 4][:, 0:w], ps[4][:, 0:w], ACT.Copy).then_inc(pt_act, 1)

            def between(n):
                for t, off in due(n):
                    i = ORDER[t]
                    if off == plan(t)["sumsq"]:
                        act.wait_ge(pv_sb, H * (t + 1))
                        link(act.activation(JUNK[:, 0:H * VD], YA[:, i, :], ACT.Square, accum_out=ST1[:, i:i + 1]))
                        link(act.activation(ST1[:, NT + i:NT + i + 1], ST1[:, i:i + 1], ACT.Ln, bias=EPSC[:, :], scale=1.0 / (H * VD)))
                        act.activation(ST2[:, i:i + 1], ST1[:, NT + i:NT + i + 1], ACT.Exp, scale=-0.5).then_inc(ya_rstd, 1)
                    if off == plan(t)["turn"]:
                        act.wait_ge(yat_ps, t + 1)
                        act.activation(YAT[t % 2], ps[7][:, :], ACT.Copy).then_inc(yat_sb, 1)
                    if off == plan(t)["sumsq2"]:
                        act.wait_ge(x2_ready, t + 1)
                        link(act.activation(JUNK[:, :], X2[:, i, :], ACT.Square, accum_out=ST1[:, i:i + 1]))
                        link(act.activation(ST1[:, NT + i:NT + i + 1], ST1[:, i:i + 1], ACT.Ln, bias=EPSC[:, :], scale=1.0 / D))
                        act.activation(ST2[:, NT + i:NT + i + 1], ST1[:, NT + i:NT + i + 1], ACT.Exp, scale=-0.5).then_inc(x2_rstd, 1)

            def turn_evac(j):
                act.wait_ge(x2nt_ps, 2 * j + 1)
                if j >= 2:
                    act.wait_ge(r_ps, j - 1)
                act.activation(X2NT[j % 2][:, 0:4, :], ps[2 * (j % 2)][:, :].rearrange("p (k n) -> p k n", k=4), ACT.Copy).then_inc(x2nt_act, 1)

            probs(0)
            for n in range(LAST):
                if n + 1 < N:
                    probs(n + 1)
                if n < N:
                    probs_evac(n)
                between(n)
                if N + 1 <= n <= N + NT - 1:
                    turn_evac(n - N - 1)
            turn_evac(NT - 1)
            act.wait_ge(rt_a, 1)
            act.activation(RB[:, 8 * NT:12 * NT], RB[:, 4 * NT:8 * NT], ACT.Exp).then_inc(rt_b, 1)
            act.wait_ge(rt_a, 2)
            act.activation(RB[:, 13 * NT:14 * NT], RB[:, 12 * NT:13 * NT], ACT.Exp).then_inc(rt_b, 1)
            act.wait_ge(idx_ready, 1)

            def rows_evac(u, done):
                act.wait_ge(xgt_ps, done)
                act.activation(XGT[u][:, 0:4, :], ps[0][:, :].rearrange("p (k n) -> p k n", k=4), ACT.Copy).then_inc(xgt_act, 1)

            def silu(u, gates, prior):
                act.wait_ge(gu_ps, gates)
                act.wait_ge(h_ready, prior)
                act.activation(SG, ps[2 + 2 * u][:, 0:2 * P], ACT.Silu).then_inc(sg_ready, 1)

            def y_evac(done):
                act.wait_ge(y_ps, done)
                act.activation(YB[0], ps[6][:, :], ACT.Copy).then_inc(y_act, 1)

            act.sem_inc(xgt_act, 1)
            act.sem_inc(y_act, 1)
            rows_evac(0, 1)
            with act.Fori(0, NMAIN // NW) as it:
                for j in range(NW):
                    u = j % 2
                    silu(u, it * (2 * NW) + (2 * j + 1), it * NW + (j + 1))
                    rows_evac(1 - u, it * (2 * NW) + (2 * j + 3))
                    act.wait_ge(y_out[0], it * (16 * NW) + 16 * (j + 1))
                    y_evac(it * NW + (j + 1))
            act.wait_ge(ove_ready, 1)
            nover = act.value_load(OVE[0:1, NOVER:NOVER + 1], min_val=0, max_val=NOVER)
            with act.Fori(0, NOVER) as b:
                with act.If(b < nover):
                    rows_evac(0, b * 2 + (2 * NMAIN + 3))
                    silu(0, b * 2 + (2 * NMAIN + 1), b + (NMAIN + 1))
                    act.wait_ge(y_out[0], b * 16 + 16 * (NMAIN + 1))
                    y_evac(b + (NMAIN + 1))
                with act.Else():
                    act.nop()
            exp_and_ln()
            for i in range(NT):
                act.wait_ge(f_sum, i + 1)
                link(act.activation(JUNK[:, :], X2[:, i, :], ACT.Square, accum_out=ST1[:, i:i + 1]))
                link(act.activation(ST1[:, NT + i:NT + i + 1], ST1[:, i:i + 1], ACT.Ln, bias=EPSC[:, :], scale=1.0 / D))
                act.activation(ST2[:, i:i + 1], ST1[:, NT + i:NT + i + 1], ACT.Exp, scale=-0.5).then_inc(f_rstd, 1)

        @block.vector
        def _(dve):
            link = chained(dve, dve_chain)
            dve.memset(EPSC[:, :], EPS).then_inc(masks_set, 1)
            dve.memset(ONEC[:, :], 1.0).then_inc(masks_set, 1)
            dve.memset(VAUG[:, :, :, MLD:], 1.0)
            dve.memset(RXP[:, :, 0:3], 0.0)
            dve.memset(CST[:, :], 0.0).then_inc(state_ready, 1)

            def norm1_apply(i):
                dve.wait_ge(x_rstd, i + 1)
                dve.wait_ge(x_in[i % 3], 16 * (i // 3 + 1))
                dve.scalar_tensor_tensor(XB[i % 3], XB[i % 3], ST1[:, NT + i:NT + i + 1], GB[:, :], ALU.mult, ALU.mult).then_inc(hn_ready, 1)

            def norm1_evac(i):
                dve.wait_ge(hnt_ps, 2 * i + 2)
                dve.tensor_copy(HNT[:, i // 4, 4:8, i % 4 * P:(i % 4 + 1) * P], ps[1][:, :].rearrange("p (k n) -> p k n", k=4)).then_inc(hnt_dve, 1)

            def output_gate(i):
                dve.wait_ge(proj_act, job("T", i, 1) + 1)
                o = OTOK[:, i, :]
                link(dve.tensor_scalar(o, o, 1.0, None, ALU.add))
                dve.reciprocal(o, o)

            def conv(f):
                dve.wait_ge(proj_act, job("F", 1, 2 + f) + 1)
                dve.wait_ge(hnt_ps, 2 * NT)
                XC = LT[f][0]
                link(dve.tensor_scalar(XC, RXP[:, f, 3:3 + S], CW[:, f * CONV + 3:f * CONV + 4], CB[:, f:f + 1], ALU.mult, ALU.add))
                for j in range(CONV - 1):
                    ins = dve.scalar_tensor_tensor(XC, RXP[:, f, j:j + S], CW[:, f * CONV + j:f * CONV + j + 1], XC, ALU.mult, ALU.add)
                    if j < CONV - 2:
                        link(ins)
                    else:
                        ins.then_inc(conv_done, 1)

            def tile_evac(i):
                dve.wait_ge(lat_rstd, i + 1)
                c = CQR[i % 2]
                o = 2 * NT + 2 * i
                dve.scalar_tensor_tensor(c[:, 0:QL], c[:, 0:QL], ST2[:, o:o + 1], GQ[:, 0:QL], ALU.mult, ALU.mult)
                dve.scalar_tensor_tensor(c[:, QL:QL + KVL], c[:, QL:QL + KVL], ST2[:, o + 1:o + 2], GQ[:, QL:], ALU.mult, ALU.mult).then_inc(lat_ready, 1)

            dve.wait_ge(g1_in, 16)
            norm1_apply(0)
            for kind, a, b in STEPS:
                if kind == "turn":
                    norm1_evac(a)
                    if a + 1 < NT:
                        norm1_apply(a + 1)
                elif kind == "T" and b == 1:
                    output_gate(a)
                elif kind == "T" and b == 2:
                    if a == 0:
                        dve.wait_ge(const_in, 16 * NC_)
                    tile_evac(a)

            conv(0)
            link(dve.tensor_scalar(SPT[:, 4:6], LAM[:, :], -1.0, None, ALU.mult))
            dve.tensor_tensor(SPT[:, 0:2], LAM[:, :], SPT[:, 4:6], ALU.max).then_inc(lam_s, 1)
            dve.wait_ge(gate_rows, 4)
            dve.wait_ge(lf_t, 1)
            dve.wait_ge(lam_s, 2)
            z, w, w2, acc = SPT[:, 2:4], SPT[:, 6:8], SPT[:, 12:14], SPT[:, 14:16]
            link(dve.tensor_scalar(w, z, 2.0, None, ALU.add))
            link(dve.reciprocal(w, w))
            link(dve.tensor_tensor(w, z, w, ALU.mult))
            link(dve.tensor_tensor(w2, w, w, ALU.mult))
            link(dve.tensor_scalar(acc, w2, 1.0 / 17, 1.0 / 15, ALU.mult, ALU.add))
            for odd in (13, 11, 9, 7, 5, 3, 1):
                link(dve.tensor_tensor(acc, acc, w2, ALU.mult))
                link(dve.tensor_scalar(acc, acc, 1.0 / odd, None, ALU.add))
            link(dve.tensor_tensor(acc, acc, w, ALU.mult))
            link(dve.tensor_scalar(acc, acc, 2.0, None, ALU.mult))
            link(dve.scalar_tensor_tensor(acc, SPT[:, 4:6], 0.0, acc, ALU.max, ALU.add))
            link(dve.tensor_scalar(SPT[:, 8:10], acc, LRU_C, None, ALU.mult))
            dve.tensor_scalar(SPT[:, 10:12], SPT[:, 8:10], -1.0, None, ALU.mult).then_inc(lam_done, 1)
            link(dve.scalar_tensor_tensor(ROW_LF, ROW_F, 0.0, ROW_L, ALU.min, ALU.subtract))
            link(dve.memset(ROW_RS, 1.0))
            link(dve.memset(ROW_RS.rearrange("p (c n) -> p c n", c=NT)[:, :, 0:1], 0.0))
            dve.wait_ge(latt_ps, NT)
            dve.tensor_tensor_scan(ROW_B, ROW_RS, ROW_LF, 0.0, ALU.mult, ALU.add)
            link(dve.tensor_tensor_scan(ROW_M, ROW_LF, ROW_I, 0.0, ALU.add, ALU.max))
            link(dve.tensor_tensor(ROW_A, ROW_B, ROW_M, ALU.subtract))
            dve.wait_ge(rs_set, 1)
            dve.tensor_tensor(ROWS4[0:MLH, :], ROW_I, ROW_B, ALU.subtract).then_inc(rows_done, 1)
            chunks = lambda r: r.rearrange("p (c n) -> p c n", c=NT)
            dve.memset(MPV[:, 0:1], 0.0)
            link(dve.tensor_copy(MPV[:, 1:NT].unsqueeze(2), chunks(ROW_M)[:, 0:NT - 1, P - 1:P]))
            dve.wait_ge(rows_done, 1)
            dve.tensor_tensor(chunks(ROW_T), chunks(ROW_A), MPV[:, :].unsqueeze(2).broadcast_to([MLH, NT, P]), ALU.add)
            link(dve.tensor_tensor(chunks(ROW_T2), chunks(ROWS4[0:MLH, :]), chunks(ROW_A)[:, :, P - 1:P].broadcast_to([MLH, NT, P]), ALU.add))
            dve.tensor_tensor(MPV[:, :].unsqueeze(2), MPV[:, :].unsqueeze(2), chunks(ROW_A)[:, :, P - 1:P], ALU.add).then_inc(rows_pre, 1)
            conv(1)

            for j in range(4):
                dve.wait_ge(ktm_ps, j + 1)
                m, half = j // 2, j % 2
                dve.tensor_copy(KTM[:, m, half * 512:(half + 1) * 512], ps[4 + j][:, :]).then_inc(ktm_sb, 1)
            col = COL[:, :].rearrange("p (i k h) -> p i k h", i=NT, k=4)
            for half in range(2):
                dve.wait_ge(cols_ps, half + 1)
                for q in range(4):
                    ins = dve.tensor_copy(col[:, 4 * half + q], ps[half][:, q * P:(q + 1) * P].rearrange("p (k n) -> p k n", k=4)[:, :, 0:MLH])
                ins.then_inc(cols_sb, 1)
            dve.wait_ge(cols_ps, 3)
            dve.tensor_copy(DECB[:, :], ps[2][:, 0:MLH * NT]).then_inc(cols_sb, 1)
            dve.wait_ge(cols_sb, 3)

            def lru(f):
                XC, R, IV, T, D1, A2 = LT[f]
                dve.wait_ge(lru_a, f + 1)
                link(dve.tensor_tensor(A2, R, R, ALU.mult))
                dve.scalar_tensor_tensor(T, A2, 1.0, T, ALU.add, ALU.mult).then_inc(lru_ratio, 1)

            def gelu_argument(f):
                T, g = LT[f][4], RG[:, f, :]
                link(dve.tensor_tensor(T, g, g, ALU.mult))
                link(dve.tensor_scalar(T, T, GELU_A, 1.0, ALU.mult, ALU.add))
                dve.tensor_tensor(T, T, g, ALU.mult).then_inc(gelu_arg, 1)

            def gated_input(f):
                dve.wait_ge(lgate_sb, 4 * f + 4)
                dve.tensor_tensor(LT[f][2], LT[f][2], LT[f][0], ALU.mult).then_inc(lru_ix, 1)

            def lru_scan(f):
                XC, R, IV, T, D1, E1 = LT[f]
                dve.wait_ge(lru_root, f + 1)
                dve.wait_ge(lru_ix, f + 1)
                link(dve.tensor_tensor(IV, IV, T, ALU.mult))
                link(dve.tensor_tensor_scan(XC, R, IV, 0.0, ALU.mult, ALU.add))
                dve.wait_ge(gelu_done, f + 1)
                dve.tensor_tensor(RXP[:, f, 3:3 + S], XC, RG[:, f, :], ALU.mult).then_inc(lru_y, 1)

            dve.wait_ge(proj_act, NPROJ)
            gelu_argument(1)
            gated_input(0)
            gated_input(1)
            for j in range(KV_EARLY):
                dve.wait_ge(kv_ps, j + 1)
                h, half = j // 2, j % 2
                dve.tensor_copy(KT[0:NOPE, h, half * 512:(half + 1) * 512], ps[4 + j % 4][0:NOPE, :]).then_inc(kv_sb, 1)
            lru(0)
            lru(1)
            lru_scan(0)
            lru_scan(1)

            heads = lambda a, n: a.rearrange("p (h n) -> p h n", n=n)

            def decay_args(c):
                dve.wait_ge(db_ps, c + 1)
                if c >= 2:
                    dve.wait_ge(w_ready, c - 1)
                dve.tensor_tensor(heads(DSB[c % 2], P), heads(ps[0][:, :], P), TMASK[:, :].unsqueeze(1).broadcast_to([P, MLH, P]), ALU.add).then_inc(d_ready, 1)

            def weigh(c):
                dve.wait_ge(st_ps, c + 1)
                dve.wait_ge(w_ready, c + 1)
                if c >= 2:
                    dve.wait_ge(intra_ps, c - 1)
                for par in range(2):
                    ins = dve.tensor_tensor(heads(PWB[c % 2], P)[:, par::2, :], heads(ps[1 + par][:, 0:2 * P], P), heads(WSB[c % 2], P)[:, par::2, :], ALU.mult)
                ins.then_inc(pw_ready, 1)

            decay_args(0)
            weigh(0)
            for c in range(NT):
                dve.wait_ge(upd_ps, c + 1)
                dve.wait_ge(inter_ps, c + 1)
                for h in range(MLH):
                    par, m = h % 2, h // 2
                    r = slice(64 * par, 64 * par + 64)
                    cs = CST[r, m * VA:(m + 1) * VA]
                    ins = dve.scalar_tensor_tensor(cs, cs, DECB[r, h * NT + c:h * NT + c + 1],
                                                   ps[6][r, (2 * m + par) * VA:(2 * m + par + 1) * VA], ALU.mult, ALU.add)
                ins.then_inc(state_ready, 1)
                if c + 1 < NT:
                    decay_args(c + 1)
                dve.wait_ge(intra_ps, c + 1)
                dve.wait_ge(inter_sb, c + 1)
                dve.tensor_tensor(NUM[c % 2], ps[3][:, 0:MLH * VA], INT[c % 2], ALU.add).then_inc(num_ready, 1)
                dve.wait_ge(num_ready, c + 1)
                num = heads(NUM[c % 2], VA)
                h4 = heads(OTOK[:, c, :], MLD)
                dve.tensor_tensor(h4, h4, num[:, :, 0:MLD], ALU.mult)
                link(dve.scalar_tensor_tensor(DEN[:, :].unsqueeze(2), num[:, :, MLD:VA], -1.0, num[:, :, MLD:VA], ALU.mult, ALU.max))
                link(dve.tensor_tensor(DEN[:, :], DEN[:, :], col[:, c, 3, :], ALU.max))
                link(dve.reciprocal(DEN[:, :], DEN[:, :]))
                dve.tensor_tensor(h4, h4, DEN[:, :].unsqueeze(2).broadcast_to([P, MLH, MLD]), ALU.mult).then_inc(h_done, 1)
                if c + 1 < NT:
                    weigh(c + 1)
                if c == 0:
                    dve.wait_ge(yr_rstd, 2)
                    for f in range(2):
                        ins = dve.scalar_tensor_tensor(RXP[:, f, 3:3 + S], RXP[:, f, 3:3 + S], GLRU[:, f:f + 1], LT[0][1], ALU.mult, ALU.mult)
                    ins.then_inc(yr_done, 1)

            n = NT * MLH
            groups = OTOK.rearrange("p i (h n) -> p (i h) n", n=MLD)
            dve.wait_ge(mh_sq, 1)
            dve.tensor_reduce(MSS[:, 0:n], SQ.rearrange("p (q n) -> p q n", n=MLD), AX.X, ALU.add).then_inc(mh_ss, 1)
            for i in range(NT):
                if i == 0:
                    dve.wait_ge(mh_rstd, 1)
                    link(dve.tensor_tensor(groups, groups, MSS[:, 2 * n:3 * n].unsqueeze(2).broadcast_to([P, n, MLD]), ALU.mult))
                if i == 1:
                    dve.tensor_tensor(OTOK, OTOK, GML[:, :].unsqueeze(1).broadcast_to([P, NT, MLW]), ALU.mult).then_inc(ymt_ready, 1)
                dve.wait_ge(qt_ps, 2 * i + 2)
                dve.tensor_copy(QT[0:QK, i, 4:8, :], ps[7][0:QK, :].rearrange("p (h n) -> p h n", h=4)).then_inc(qt_dve, 1)

            def row_max(n):
                i, h = ATT[n]
                L = (i + 1) * P
                dve.wait_ge(s_ps, n + 1)
                b, o = (i * P) // 512, (i * P) % 512
                diag = ps[2 * (n % 2) + b][:, o:o + P]
                link(dve.tensor_tensor(diag, diag, CMASK[:, :], ALU.add))
                nb = (L + 511) // 512
                for b in range(nb):
                    w = min(512, L - 512 * b)
                    dst = (NMX if b == 0 else RIN)[:, n:n + 1]
                    ins = dve.tensor_reduce(dst, ps[2 * (n % 2) + b][:, 0:w], AX.X, ALU.max, negate=True)
                if nb == 2:
                    link(ins)
                    ins = dve.tensor_tensor(NMX[:, n:n + 1], NMX[:, n:n + 1], RIN[:, n:n + 1], ALU.min)
                ins.then_inc(s_max, 1)

            def probs_evac(n):
                i, h = ATT[n]
                for gg in range(G0[n], G0[n + 1]):
                    if gg % 2 == 1:
                        dve.wait_ge(pt_ps, gg + 1)
                        if gg >= 4:
                            dve.wait_ge(pv_ps, GROUPS[gg - 4][0] + 1)
                        w = P * min(4, i + 1 - 4 * GROUPS[gg][1])
                        dve.tensor_copy(PTB[gg % 4][:, 0:w], ps[5][:, 0:w]).then_inc(pt_dve, 1)

            def normalise(n):
                i, h = ATT[n]
                dve.wait_ge(p_ready, n + 1)
                if i >= 4:
                    link(dve.tensor_tensor(RSM[:, n:n + 1], RSM[:, n:n + 1], RIN[:, n:n + 1], ALU.add))
                link(dve.reciprocal(RIN[:, n:n + 1], RSM[:, n:n + 1]))
                dve.wait_ge(pv_ps, n + 1)
                dve.tensor_scalar(YA[:, i, h * VD:(h + 1) * VD], ps[6][:, 0:VD], RIN[:, n:n + 1], None, ALU.mult).then_inc(pv_sb, 1)

            def residual(t, b):
                i = ORDER[t]
                dve.wait_ge(o_ps, 2 * t + b + 1)
                dve.wait_ge(xr_in[t % 2], 16 * (t // 2 + 1))
                s = slice(b * 512, (b + 1) * 512)
                dve.tensor_tensor(X2[:, i, s], ps[out_bank(t, b)][:, :], XR[t % 2][:, s], ALU.add).then_inc(x2_half if b == 0 else x2_ready, 1)

            def between(n):
                for t, off in due(n):
                    if off == plan(t)["scale"]:
                        dve.wait_ge(ya_rstd, t + 1)
                        dve.scalar_tensor_tensor(YA[:, ORDER[t], :], YA[:, ORDER[t], :], ST2[:, ORDER[t]:ORDER[t] + 1], GMLA[:, :], ALU.mult, ALU.mult).then_inc(ya_ready, 1)
                    for b in range(2):
                        if off == plan(t)[f"add{b}"]:
                            residual(t, b)
                    if off == plan(t)["norm2"]:
                        norm2(t)

            def norm2(j):
                i = ORDER[j]
                dve.wait_ge(x2_rstd, j + 1)
                if j == 0:
                    dve.wait_ge(g2_in, 16)
                if j == NT - 2:
                    dve.wait_ge(x2n_out, 16 * (NT - 2))
                if j >= NT - 2:
                    dve.wait_ge(x2nt_ps, 2 * (j - NT + 3))
                dve.scalar_tensor_tensor(X2N[j], X2[:, i, :], ST2[:, NT + i:NT + i + 1], G2B, ALU.mult, ALU.mult).then_inc(x2n_ready, 1)

            def turn_evac(j):
                dve.wait_ge(x2nt_ps, 2 * j + 2)
                if j >= 2:
                    dve.wait_ge(r_ps, j - 1)
                dve.tensor_copy(X2NT[j % 2][:, 4:8, :], ps[2 * (j % 2) + 1][:, :].rearrange("p (k n) -> p k n", k=4)).then_inc(x2nt_dve, 1)

            def router_evac(j):
                i = ORDER[j]
                dve.wait_ge(r_ps, j + 1)
                dve.tensor_tensor(LG[:, i * 36:(i + 1) * 36], ps[4 + j % 2][:, 0:36], BRT[:, :], ALU.add).then_inc(r_sb, 1)

            row_max(0)
            for n in range(LAST):
                if n + 1 < N:
                    row_max(n + 1)
                if n < N:
                    probs_evac(n)
                if 1 <= n <= N:
                    normalise(n - 1)
                between(n)
                if N + 1 <= n <= N + NT - 1:
                    turn_evac(n - N - 1)
                if N + 2 <= n <= N + NT:
                    router_evac(n - N - 2)
            turn_evac(NT - 1)
            router_evac(NT - 1)
            dve.wait_ge(r_sb, NT)

            dve.wait_ge(iota_set, 1)
            lg = LG[:, :].rearrange("p (i n) -> p i n", i=NT)
            gl = lg[:, :, 0:NG]
            el = lg[:, :, NG:].rearrange("p i (g j) -> p i g j", g=NG)

            def rb(a, n):
                return RB[:, a * NT:(a + n) * NT].rearrange("p (i n) -> p i n", i=NT)

            gmax, gd, gex = rb(0, 1), rb(4, 4), rb(8, 4)
            big = [RA[:, q * NT * NE:(q + 1) * NT * NE] for q in range(6)]
            rev4 = IOT[:, 0:NG]
            rev8 = IOT[:, 4:4 + EPG]

            def first_max(dst, vals, n, rev, m, key):
                link(dve.tensor_tensor(key, vals, m.broadcast_to([P, NT, n]), ALU.is_equal))
                link(dve.tensor_tensor(key, key, rev.unsqueeze(1).broadcast_to([P, NT, n]), ALU.mult))
                link(dve.tensor_reduce(rb(15, 1), key, AX.X, ALU.max))
                link(dve.tensor_tensor(dst, key, rb(15, 1).broadcast_to([P, NT, n]), ALU.is_equal))

            link(dve.tensor_reduce(gmax, gl, AX.X, ALU.max))
            link(dve.tensor_tensor(gd, gl, gmax.broadcast_to([P, NT, NG]), ALU.subtract))
            dve.nop().then_inc(rt_a, 1)
            ohg = rb(16, 4)
            first_max(ohg, gl, NG, rev4, gmax, rb(20, 4))
            prod = big[5].rearrange("p (i g j) -> p i g j", i=NT, g=NG)
            sel = big[4][:, 0:NT * EPG].rearrange("p (i j) -> p i j", i=NT)
            link(dve.tensor_tensor(prod, el, ohg.unsqueeze(3).broadcast_to([P, NT, NG, EPG]), ALU.mult))
            link(dve.tensor_tensor(sel, prod[:, :, 0, :], prod[:, :, 1, :], ALU.add))
            link(dve.tensor_tensor(sel, sel, prod[:, :, 2, :], ALU.add))
            link(dve.tensor_tensor(sel, sel, prod[:, :, 3, :], ALU.add))
            e8 = [big[4][:, (1 + q) * NT * EPG:(2 + q) * NT * EPG].rearrange("p (i j) -> p i j", i=NT) for q in range(3)]
            m1, m2 = rb(1, 1), rb(2, 1)
            link(dve.tensor_reduce(m1, sel, AX.X, ALU.max))
            first_max(e8[0], sel, EPG, rev8, m1, e8[2])
            link(dve.scalar_tensor_tensor(sel, e8[0], -BIG, sel, ALU.mult, ALU.add))
            link(dve.tensor_reduce(m2, sel, AX.X, ALU.max))
            first_max(e8[1], sel, EPG, rev8, m2, e8[2])
            link(dve.tensor_tensor(rb(12, 1), m2, m1, ALU.subtract))
            dve.nop().then_inc(rt_a, 1)
            oh = [big[1], big[2]]
            for q in range(2):
                ohq = oh[q].rearrange("p (i g j) -> p i g j", i=NT, g=NG)
                ins = dve.tensor_tensor(ohq, e8[q].unsqueeze(2).broadcast_to([P, NT, NG, EPG]), ohg.unsqueeze(3).broadcast_to([P, NT, NG, EPG]), ALU.mult)
            link(ins)
            dve.tensor_tensor(big[0], oh[0], oh[1], ALU.add).then_inc(mask_ready, 1)
            dve.wait_ge(rt_b, 2)
            link(dve.tensor_reduce(rb(3, 1), gex, AX.X, ALU.add))
            link(dve.tensor_scalar(rb(14, 1), rb(13, 1), 1.0, None, ALU.add))
            link(dve.tensor_tensor(rb(14, 1), rb(14, 1), rb(3, 1), ALU.mult))
            w0, w1 = WTS[:, 0:NT], WTS[:, NT:2 * NT]
            link(dve.reciprocal(w0, RB[:, 14 * NT:15 * NT]))
            link(dve.tensor_tensor(w1, w0, RB[:, 13 * NT:14 * NT], ALU.mult))
            dve.wait_ge(pos_ps, 1)
            cnt = lambda q: CNT[:, q * NE:(q + 1) * NE]
            b3 = big[3].rearrange("p (i e) -> p i e", i=NT)
            dve.wait_ge(scm_set, 1)
            link(dve.tensor_tensor_scan(big[5], SCM, ps[1][:, 0:NT * NE], 0.0, ALU.mult, ALU.add))
            dve.tensor_copy(cnt(0).unsqueeze(2), big[5].rearrange("p (e i) -> p e i", e=NE)[:, :, NT - 1:NT])
            link(dve.tensor_tensor(big[4], big[5], ps[1][:, 0:NT * NE], ALU.subtract))
            dve.tensor_tensor(b3, ps[0][:, 0:NT * NE].rearrange("p (i e) -> p i e", i=NT), big[4].rearrange("p (e i) -> p i e", e=NE), ALU.add)
            nj = S // CAP - 1
            over = big[5][:, 0:NE * nj].rearrange("p (e j) -> p e j", e=NE)
            dve.memset(cnt(4), 1.0)
            link(dve.tensor_tensor(over, cnt(0).unsqueeze(2).broadcast_to([P, NE, nj]), IOB[:, 1:1 + nj].unsqueeze(1).broadcast_to([P, NE, nj]), ALU.is_gt))
            link(dve.tensor_reduce(cnt(1), over, AX.X, ALU.add))
            link(dve.tensor_tensor_scan(cnt(2), cnt(4), cnt(1), 0.0, ALU.mult, ALU.add))
            link(dve.tensor_tensor(cnt(3), cnt(2), cnt(1), ALU.subtract))
            link(dve.scalar_tensor_tensor(cnt(3), cnt(3), float(NMAIN - 1), IOT[:, NE:2 * NE], ALU.add, ALU.subtract))
            link(dve.tensor_scalar(cnt(3), cnt(3), float(CAP), None, ALU.mult))
            link(dve.tensor_scalar(cnt(5), IOT[:, NE:2 * NE], float(CAP), None, ALU.mult))
            b4 = big[4].rearrange("p (i e) -> p i e", i=NT)
            link(dve.tensor_scalar(big[4], big[3], float(CAP), None, ALU.is_ge))
            link(dve.tensor_tensor(b4, b4, cnt(3).unsqueeze(1).broadcast_to([P, NT, NE]), ALU.mult))
            link(dve.tensor_tensor(big[3], big[3], big[4], ALU.add))
            link(dve.tensor_tensor(b3, b3, cnt(5).unsqueeze(1).broadcast_to([P, NT, NE]), ALU.add))
            for q in range(2):
                link(dve.tensor_tensor(big[5], oh[q], big[3], ALU.mult))
                link(dve.tensor_reduce(SLOTF[:, q * NT:(q + 1) * NT], big[5].rearrange("p (i e) -> p i e", i=NT), AX.X, ALU.add))
            slots = SLOTF[:, :].unsqueeze(2).broadcast_to([P, NS, NBLK])
            link(dve.tensor_tensor(BGE, slots, IOB[:, :].unsqueeze(1).broadcast_to([P, NS, NBLK]), ALU.is_ge))
            dve.tensor_copy(BEQ[:, :, NBLK - 1:], BGE[:, :, NBLK - 1:])
            dve.tensor_tensor(BEQ[:, :, 0:NBLK - 1], BGE[:, :, 0:NBLK - 1], BGE[:, :, 1:], ALU.subtract)
            link(dve.tensor_reduce(PLACE[:, :], BGE, AX.X, ALU.add))
            link(dve.tensor_scalar(PLACE[:, :], PLACE[:, :], -float(CAP), float(CAP), ALU.mult, ALU.add))
            link(dve.tensor_tensor(PLACE[:, :], PLACE[:, :], SLOTF[:, :], ALU.add))
            for n in range(NS):
                dve.tensor_scalar(OHP[:, n, :], IOP[:, :], PLACE[:, n:n + 1], TOKS[:, n % NT:n % NT + 1], ALU.is_equal, ALU.mult).then_inc(places_ready, 1)
            dve.wait_ge(ids_ps, 1)
            dve.tensor_scalar(IDX[:, :], ps[2][:, 0:NBLK], float(S), None, ALU.add).then_inc(idx_ready, 1)

            def rows_evac(u, done):
                dve.wait_ge(xgt_ps, done)
                dve.tensor_copy(XGT[u][:, 4:8, :], ps[1][:, :].rearrange("p (k n) -> p k n", k=4)).then_inc(xgt_dve, 1)

            def swiglu(u, ups, done):
                dve.wait_ge(gu_ps, ups)
                dve.wait_ge(sg_ready, done)
                dve.tensor_tensor(HT[u].rearrange("p k n -> p (k n)"), SG, ps[3 + 2 * u][:, 0:2 * P], ALU.mult).then_inc(h_ready, 1)

            def y_evac(done):
                dve.wait_ge(y_ps, done)
                dve.tensor_copy(YB[1], ps[7][:, :]).then_inc(y_dve, 1)

            dve.sem_inc(xgt_dve, 1)
            dve.sem_inc(y_dve, 1)
            dve.sem_inc(h_ready, 1)
            rows_evac(0, 2)
            for b in range(NOVER):
                link(dve.tensor_scalar(cnt(6)[0:1, :], cnt(2)[0:1, :], float(b), None, ALU.is_le))
                link(dve.tensor_reduce(cnt(7)[0:1, b:b + 1], cnt(6)[0:1, :], AX.X, ALU.add))
            link(dve.tensor_scalar(cnt(7)[0:1, 0:NOVER], cnt(7)[0:1, 0:NOVER], float(NE - 1), None, ALU.min))
            dve.tensor_copy(OVE[0:1, 0:NOVER], cnt(7)[0:1, 0:NOVER])
            dve.tensor_copy(OVE[0:1, NOVER:NOVER + 1], cnt(2)[0:1, NE - 1:NE]).then_inc(ove_ready, 1)
            dve.tensor_copy(SLOT[:, :], SLOTF[:, :]).then_inc(slot_ready, 1)
            dve.wait_ge(slot_ready, 1)
            with dve.Fori(0, NMAIN // NW) as it:
                for j in range(NW):
                    u = j % 2
                    swiglu(u, it * (2 * NW) + (2 * j + 2), it * NW + (j + 1))
                    rows_evac(1 - u, it * (2 * NW) + (2 * j + 4))
                    dve.wait_ge(y_out[1], it * (16 * NW) + 16 * (j + 1))
                    y_evac(it * NW + (j + 1))
            nover = dve.value_load(OVE[0:1, NOVER:NOVER + 1], min_val=0, max_val=NOVER)
            with dve.Fori(0, NOVER) as b:
                with dve.If(b < nover):
                    rows_evac(0, b * 2 + (2 * NMAIN + 4))
                    swiglu(0, b * 2 + (2 * NMAIN + 2), b + (NMAIN + 1))
                    dve.wait_ge(y_out[1], b * 16 + 16 * (NMAIN + 1))
                    y_evac(b + (NMAIN + 1))
                with dve.Else():
                    dve.nop()

            def combine(i):
                dve.wait_ge(yg_in[i % NY], 32 * (i // NY + 1))
                link(dve.scalar_tensor_tensor(X2[:, i, :], YG[i % NY][0], WTS[:, i:i + 1], X2[:, i, :], ALU.mult, ALU.add))
                dve.scalar_tensor_tensor(X2[:, i, :], YG[i % NY][1], WTS[:, NT + i:NT + i + 1], X2[:, i, :], ALU.mult, ALU.add).then_inc(f_sum, 1)

            def final_norm(i):
                dve.wait_ge(f_rstd, i + 1)
                if i >= 2:
                    dve.wait_ge(out_done[i % 2], 16 * (i // 2))
                dve.scalar_tensor_tensor(OUT[i % 2], X2[:, i, :], ST2[:, i:i + 1], GB[:, :], ALU.mult, ALU.mult).then_inc(f_ready, 1)

            combine(0)
            dve.wait_ge(gf_in, 16)
            for i in range(NT):
                if i + 1 < NT:
                    combine(i + 1)
                final_norm(i)

        @block.gpsimd
        def _(pool):
            link = chained(pool, pool_chain)
            sel = SEL[:, :].rearrange("p (h n) -> p h n", h=MLH)
            pool.memset(BD[:, :], 0.0)
            pool.memset(ONES[:, :], 1.0)
            pool.memset(KRP[0], 0.0)
            pool.memset(KRP[1], 0.0)
            pool.memset(IDENT[:, :], 0.0)
            pool.memset(CMASK[:, :], 0.0)
            pool.memset(TMASK[:, :], 0.0)
            pool.memset(SEL[:, :], 0.0)
            link(pool.memset(TRI[:, :], 0.0))
            pool.affine_select(out=IDENT[:, :], in_=IDENT[:, :], compare_op=ALU.not_equal, fill=1.0, base=0,
                               pattern=[[-1, P]], channel_multiplier=1).then_inc(masks_set, 1)
            pool.affine_select(out=CMASK[:, :], in_=CMASK[:, :], compare_op=ALU.is_ge, fill=-BIG, base=0,
                               pattern=[[-1, P]], channel_multiplier=1).then_inc(masks_set, 1)
            pool.affine_select(out=TMASK[:, :], in_=TMASK[:, :], compare_op=ALU.is_ge, fill=-BIG, base=0,
                               pattern=[[1, P]], channel_multiplier=-1).then_inc(masks_set, 1)
            pool.affine_select(out=TRI[:, :], in_=TRI[:, :], compare_op=ALU.is_ge, fill=1.0, base=0,
                               pattern=[[-1, P]], channel_multiplier=1).then_inc(masks_set, 1)
            pool.affine_select(out=sel, in_=sel, compare_op=ALU.not_equal, fill=1.0, base=0,
                               pattern=[[-1, MLH], [0, P]], channel_multiplier=1).then_inc(masks_set, 1)
            link(pool.memset(SPT[:, :], 0.0))
            link(pool.iota(IOT[:, 0:4], pattern=[[-1, 4]], base=NG, channel_multiplier=0, allow_small_or_imprecise_dtypes=True))
            link(pool.iota(IOT[:, 4:12], pattern=[[-1, 8]], base=EPG, channel_multiplier=0, allow_small_or_imprecise_dtypes=True))
            link(pool.iota(IOT[:, NE:2 * NE], pattern=[[1, NE]], base=0, channel_multiplier=0, allow_small_or_imprecise_dtypes=True))
            link(pool.iota(TOK[:, :], pattern=[[P, NT]], base=0, channel_multiplier=1, allow_small_or_imprecise_dtypes=True))
            link(pool.tensor_scalar(TOKS[:, :], TOK[:, :], -float(S), None, ALU.add))
            link(pool.iota(IOB[:, :], pattern=[[CAP, NBLK]], base=0, channel_multiplier=0, allow_small_or_imprecise_dtypes=True))
            link(pool.iota(IOP[:, :], pattern=[[1, P]], base=0, channel_multiplier=0, allow_small_or_imprecise_dtypes=True))
            pool.nop().then_inc(iota_set, 1)
            pool.memset(ZERO, 0.0).then_inc(zero_set, 1)

            pool.wait_ge(const_in, 16 * NC_)
            for i in range(NT):
                pool.wait_ge(proj_act, job("T", i, 2) + 1)
                if i >= 2:
                    pool.wait_ge(latt_ps, i - 1)
                t1, t2 = CQR[i % 2][:, QL + KVL:QL + KVL + 16], CQR[i % 2][:, QL + KVL + 16:]
                cs, sn = COS[:, i * 16:(i + 1) * 16], SIN[:, i * 16:(i + 1) * 16]
                a, b, c, d = (RTMP[:, q * 16:(q + 1) * 16] for q in range(4))
                pool.tensor_tensor(a, t1, cs, ALU.mult)
                pool.tensor_tensor(b, t2, sn, ALU.mult)
                pool.tensor_tensor(c, t1, sn, ALU.mult)
                link(pool.tensor_tensor(d, t2, cs, ALU.mult))
                pool.tensor_tensor(KRP[i % 2][:, NOPE:NOPE + 16], a, b, ALU.subtract)
                pool.tensor_tensor(KRP[i % 2][:, NOPE + 16:QK], c, d, ALU.add).then_inc(krp_ready, 1)
                pool.wait_ge(krp_ready, i + 1)
            pool.wait_ge(proj_ps, job("F", 0, 5) + 1)
            pool.memset(ROWS4, 0.0).then_inc(rs_set, 1)
            pool.wait_ge(proj_act, NPROJ)
            pool.wait_ge(rows_done, 5)
            T, g = LT[0][4], RG[:, 0, :]
            link(pool.tensor_tensor(T, g, g, ALU.mult))
            link(pool.tensor_scalar(T, T, GELU_A, 1.0, ALU.mult, ALU.add))
            pool.tensor_tensor(T, T, g, ALU.mult).then_inc(gelu_arg_pool, 1)
            for f in range(2):
                pool.wait_ge(gelu_sig, f + 1)
                pool.tensor_tensor(RG[:, f, :], RG[:, f, :], LT[f][4], ALU.mult).then_inc(gelu_done, 1)
            pool.wait_ge(cols_sb, 3)
            col = COL[:, :].rearrange("p (i k h) -> p i k h", i=NT, k=4)
            for c in range(NT):
                if c >= 2:
                    pool.wait_ge(upd_ps, c - 1)
                if c == 0:
                    pool.wait_ge(lru_y, 2)
                pool.tensor_tensor(KSB[c % 2].rearrange("p (h n) -> p h n", h=MLH),
                                   KTOK[:, c, :].rearrange("p (h n) -> p h n", h=MLH),
                                   col[:, c, 2, :].unsqueeze(2).broadcast_to([P, MLH, MLD]), ALU.mult).then_inc(ks_ready, 1)
            for i in range(NT):
                pool.wait_ge(q_sb, i + 1)
                q = QTOK[i % 2]
                t1, t2 = q[:, :, NOPE:NOPE + 16], q[:, :, NOPE + 16:QK]
                cs = COS[:, i * 16:(i + 1) * 16].unsqueeze(1).broadcast_to([P, H, 16])
                sn = SIN[:, i * 16:(i + 1) * 16].unsqueeze(1).broadcast_to([P, H, 16])
                a, b, c, d = (RTMP[:, w * 128:(w + 1) * 128].rearrange("p (h n) -> p h n", h=H) for w in range(4))
                pool.tensor_tensor(a, t1, cs, ALU.mult)
                pool.tensor_tensor(b, t2, sn, ALU.mult)
                pool.tensor_tensor(c, t1, sn, ALU.mult)
                link(pool.tensor_tensor(d, t2, cs, ALU.mult))
                pool.tensor_tensor(t1, a, b, ALU.subtract)
                pool.tensor_tensor(t2, c, d, ALU.add).then_inc(q_rope, 1)
                pool.wait_ge(q_rope, i + 1)
            link(pool.memset(SCM, 1.0))
            pool.memset(SCM.rearrange("p (e i) -> p e i", e=NE)[:, :, 0:1], 0.0).then_inc(scm_set, 1)
            pool.wait_ge(yr_done, 1)
            pool.wait_ge(x2_ready, NT)
            pool.memset(XG[0], 0.0).then_inc(xg_set, 1)
            pool.memset(XG[1], 0.0).then_inc(xg_set, 1)
            pool.wait_ge(xg_set, 2)
            pool.wait_ge(idx_ready, 1)
            pool.wait_ge(x2n_out, 16 * NT)

            def stand():
                pool.sem_inc(pool_waits, 1)

            def gather(u, col, done):
                pool.tensor_copy(IDXC[u][:, :], col).then_inc(list_ready, 1)
                pool.wait_ge(list_ready, done)
                stand()
                col = IDXC[u][:, :]
                pool.indirect_dma_start(XG[u], None, x2n_d, bass.IndirectOffsetOnAxis(ap=col, axis=0),
                                        bounds_check=S - 1, oob_is_err=False).then_inc(xg_in[u], 16)

            gather(0, IDX[:, 0:1], 1)
            gather(1, IDX[:, 1:2], 2)
            with pool.Fori(0, NMAIN // NW) as it:
                for j in range(NW):
                    u = j % 2
                    pool.wait_ge(xgt_ps, it * (2 * NW) + (2 * j + 2))
                    stand()
                    gather(u, IDX[:, bass.ds(it * NW + (j + 2), 1)], it * NW + (j + 3))
            pool.wait_ge(ove_ready, 1)
            nover = pool.value_load(OVE[0:1, NOVER:NOVER + 1], min_val=0, max_val=NOVER)
            with pool.Fori(0, NOVER) as b:
                with pool.If(b < nover):
                    pool.wait_ge(xgt_ps, b * 2 + (2 * NMAIN + 2))
                    stand()
                    gather(0, IDX[:, bass.ds(b + NMAIN, 1)], b + (NMAIN + 3))
                with pool.Else():
                    pool.nop()
            total = pool.snap(nover * 16 + 16 * (NMAIN + 1))
            pool.wait_ge(y_out[0], total)
            pool.wait_ge(y_out[1], total)
            stand()
            for i in range(NT):
                if i >= NY:
                    pool.wait_ge(f_sum, i - NY + 1)
                for q in range(2):
                    pool.indirect_dma_start(YG[i % NY][q], None, y_d, bass.IndirectOffsetOnAxis(ap=SLOT[:, q * NT + i:q * NT + i + 1], axis=0)).then_inc(yg_in[i % NY], 16)


NAMES = ["x", "norm1_g", "w_in", "ml_i_bias", "ml_f_bias", "ml_norm_g", "conv_w", "conv_b", "lru_w_r", "lru_b_r",
         "lru_w_i", "lru_b_i", "lru_lambda", "lru_norm_g", "q_norm_g", "w_uq", "kv_norm_g", "w_ukv", "mla_norm_g",
         "w_out", "norm2_g", "w_group", "b_group", "w_expert", "b_expert", "w_gate", "w_up", "w_down", "final_norm_g"]


def kernel(**inputs):
    import concourse.bacc as bacc
    from concourse.bass_utils import run_bass_kernel_spmd

    nc = bacc.Bacc("TRN2", target_bir_lowering=False, num_devices=1)
    inv = (1.0 / (np.float32(10000.0) ** (np.arange(0, ROPE, 2, dtype=np.float32) / np.float32(ROPE)))).astype(np.float32)
    ang = np.arange(S, dtype=np.float32)[:, None] * inv[None, :]
    arrays = {"rope_cos": np.cos(ang), "rope_sin": np.sin(ang)}
    arrays.update({name: np.ascontiguousarray(inputs[name]) for name in NAMES})
    t = {name: nc.dram_tensor(f"in_{name}", a.shape, mybir.dt.from_np(a.dtype), kind="ExternalInput").ap()
         for name, a in arrays.items()}
    t["out"] = nc.dram_tensor("out_0", (1, S, D), F32, kind="ExternalOutput").ap()
    build(nc, t)
    r = run_bass_kernel_spmd(nc, [{f"in_{name}": a for name, a in arrays.items()}], core_ids=[0])
    return r.results[0]["out_0"]
```
